# Optimizing a Trainium2 kernel written in Bass

```python
import jax, jax.numpy as jnp
from jax import lax
import numpy as np
import math

D_MODEL = 1024
BATCH = 1
SEQ = 256
DEPTH = 2

CHUNK = 64
MEM_LEN = 256
Q_BLOCK = 128
N_MIXERS = 2
DA_HEADS = 6
DA_HEAD_DIM = 64
DA_WIDTH = DA_HEADS * 2 * DA_HEAD_DIM
HG_HEADS = 6
HG_KEY_DIM = 128
HG_VAL_DIM = 128
HG_KEY_WIDTH = HG_HEADS * HG_KEY_DIM
HG_VAL_WIDTH = HG_HEADS * HG_VAL_DIM
MEM_HEADS = 4
MEM_HEAD_DIM = 64
MEM_WIDTH = MEM_HEADS * MEM_HEAD_DIM
MIX_WIDTH = DA_WIDTH + MEM_WIDTH
D_FF_DENSE = 2816
N_EXPERTS = 8
TOP_K = 2
D_FF_EXPERT = 3584
EPS = 1e-6
MASK_VALUE = -1e30
N_A = (DEPTH + 1) // 2
N_B = DEPTH // 2


F32 = jnp.float32

def rms_norm(x, g):
    xf = x.astype(F32)
    y = xf * lax.rsqrt(jnp.mean(xf * xf, axis=-1, keepdims=True) + EPS)
    return (y * g.astype(F32)).astype(x.dtype)

def alibi_slopes(n):
    return jnp.asarray(2.0 ** (-8.0 * np.arange(1, n + 1) / n), F32)

def memory_attention(q_mem, mem, mem_norm_g, w_mem_kv):
    B, S, _ = q_mem.shape
    kv = rms_norm(mem, mem_norm_g) @ w_mem_kv
    k, v = jnp.split(kv, 2, axis=-1)
    q = q_mem.reshape(B, S, MEM_HEADS, MEM_HEAD_DIM)
    k = k.reshape(B, -1, MEM_HEADS, MEM_HEAD_DIM)
    v = v.reshape(B, -1, MEM_HEADS, MEM_HEAD_DIM)
    s = jnp.einsum('bshd,bmhd->bhsm', q, k).astype(F32) * (MEM_HEAD_DIM ** -0.5)
    p = jax.nn.softmax(s, axis=-1).astype(v.dtype)
    o = jnp.einsum('bhsm,bmhd->bshd', p, v)
    return o.reshape(B, S, MEM_WIDTH)

def diff_attention(q, k, v, lam, lam_init, subln_g):
    B, S = q.shape[:2]
    nb = S // Q_BLOCK
    scale = DA_HEAD_DIM ** -0.5
    slopes = alibi_slopes(DA_HEADS)
    kpos = jnp.arange(S)
    kchunk = kpos // CHUNK
    qb = q.reshape(B, nb, Q_BLOCK, DA_HEADS, 2, DA_HEAD_DIM).transpose(1, 0, 2, 3, 4, 5)
    starts = jnp.arange(nb) * Q_BLOCK

    def block(args):
        q_blk, start = args
        qpos = start + jnp.arange(Q_BLOCK)
        dist = jnp.abs(qpos[:, None] - kpos[None, :]).astype(F32)
        allowed = kchunk[None, :] <= (qpos // CHUNK)[:, None]
        bias = jnp.where(allowed[None], -slopes[:, None, None] * dist[None], MASK_VALUE)
        s = jnp.einsum('bqhmd,bkhmd->bhmqk', q_blk, k).astype(F32) * scale + bias[None, :, None]
        p = jax.nn.softmax(s, axis=-1)
        a = (p[:, :, 0] - lam * p[:, :, 1]).astype(v.dtype)
        return jnp.einsum('bhqk,bkhe->bqhe', a, v)

    o = lax.map(block, (qb, starts))
    o = o.transpose(1, 0, 2, 3, 4).reshape(B, S, DA_HEADS, 2 * DA_HEAD_DIM)
    o = rms_norm(o, subln_g) * (1.0 - lam_init)
    return o.reshape(B, S, DA_WIDTH)

def diff_attention_mixer(h, mem, w_in, lq1, lk1, lq2, lk2, subln_g, mem_norm_g, w_mem_kv, w_out, lam_init):
    B, S, _ = h.shape
    proj = h @ w_in
    q, k, v, qm = jnp.split(proj, [DA_WIDTH, 2 * DA_WIDTH, 3 * DA_WIDTH], axis=-1)
    q = q.reshape(B, S, DA_HEADS, 2, DA_HEAD_DIM)
    k = k.reshape(B, S, DA_HEADS, 2, DA_HEAD_DIM)
    v = v.reshape(B, S, DA_HEADS, 2 * DA_HEAD_DIM)
    lam = (jnp.exp(jnp.sum(lq1.astype(F32) * lk1.astype(F32)))
           - jnp.exp(jnp.sum(lq2.astype(F32) * lk2.astype(F32))) + lam_init)
    o = diff_attention(q, k, v, lam, lam_init, subln_g).astype(h.dtype)
    om = memory_attention(qm, mem, mem_norm_g, w_mem_kv).astype(h.dtype)
    return jnp.concatenate([o, om], axis=-1) @ w_out

def hgrn2_chunkwise(q, k, v, log_f):
    B, S, H, dk = q.shape
    dv = v.shape[-1]
    nc = S // CHUNK

    def to_chunks(t):
        return t.astype(F32).reshape(B, nc, CHUNK, H, t.shape[-1]).transpose(1, 0, 3, 2, 4)

    xs = (to_chunks(q), to_chunks(k), to_chunks(v), to_chunks(log_f))
    causal = jnp.tril(jnp.ones((CHUNK, CHUNK), bool))[None, None, :, :, None]

    def step(state, inp):
        q_, k_, v_, g_ = inp
        b = jnp.cumsum(g_, axis=2)
        b_last = b[:, :, -1:, :]
        diff = jnp.where(causal, b[:, :, :, None, :] - b[:, :, None, :, :], 0.0)
        decay = jnp.where(causal, jnp.exp(diff), 0.0)
        attn = jnp.einsum('bhtsk,bhsk->bhts', q_[:, :, :, None, :] * decay, k_)
        o = (jnp.einsum('bhts,bhsv->bhtv', attn, v_)
             + jnp.einsum('bhtk,bhkv->bhtv', q_ * jnp.exp(b), state))
        state = (jnp.exp(b_last)[:, :, 0, :, None] * state
                 + jnp.einsum('bhsk,bhsv->bhkv', k_ * jnp.exp(b_last - b), v_))
        return state, o

    state0 = jnp.zeros((B, H, dk, dv), F32)
    _, o = lax.scan(step, state0, xs)
    return o.transpose(1, 0, 3, 2, 4).reshape(B, S, H, dv)

def hgrn2_mixer(h, mem, w_in, lb, out_norm_g, mem_norm_g, w_mem_kv, w_out):
    B, S, _ = h.shape
    proj = h @ w_in
    q, fz, i, g, qm = jnp.split(
        proj, [HG_KEY_WIDTH, 2 * HG_KEY_WIDTH, 2 * HG_KEY_WIDTH + HG_VAL_WIDTH,
               2 * HG_KEY_WIDTH + 2 * HG_VAL_WIDTH], axis=-1)
    fz32 = fz.astype(F32)
    f = lb + (1.0 - lb) * jax.nn.sigmoid(fz32)
    log_f = jnp.log(f)
    k = (1.0 - lb) * jax.nn.sigmoid(-fz32)
    heads = lambda t: t.reshape(B, S, HG_HEADS, -1)
    o = hgrn2_chunkwise(heads(q), heads(k), heads(i), heads(log_f))
    o = rms_norm(o, out_norm_g) * jax.nn.silu(heads(g).astype(F32))
    o = o.reshape(B, S, HG_VAL_WIDTH).astype(h.dtype)
    om = memory_attention(qm, mem, mem_norm_g, w_mem_kv).astype(h.dtype)
    return jnp.concatenate([o, om], axis=-1) @ w_out

def dense_swiglu(h, w_gate_up, w_down):
    gt, up = jnp.split(h @ w_gate_up, 2, axis=-1)
    return (jax.nn.silu(gt) * up) @ w_down

def moe_swiglu(h, w_router, w_gate_up, w_down):
    B, S, D = h.shape
    t = h.reshape(-1, D)
    logits = (t @ w_router).astype(F32)
    top_val, top_idx = lax.top_k(logits, TOP_K)
    top_w = jax.nn.softmax(top_val, axis=-1)
    combine = jnp.sum(jax.nn.one_hot(top_idx, N_EXPERTS, dtype=F32) * top_w[..., None], axis=1)
    out = jnp.zeros_like(t)
    for e in range(N_EXPERTS):
        gt, up = jnp.split(t @ w_gate_up[e], 2, axis=-1)
        y = (jax.nn.silu(gt) * up) @ w_down[e]
        out = out + combine[:, e:e + 1].astype(t.dtype) * y
    return out.reshape(B, S, D)

def first_inputs(seed: int = 0) -> dict:
    key = jax.random.key(seed)
    ks = iter(jax.random.split(key, 40))
    D = D_MODEL
    res = (2.0 * DEPTH) ** -0.5

    def nrm(shape, scale):
        return jax.random.normal(next(ks), shape, F32) * scale

    def gain(shape):
        return 1.0 + 0.02 * jax.random.normal(next(ks), shape, F32)

    return {
        "x": nrm((BATCH, SEQ, D), 1.0),
        "mem": nrm((BATCH, MEM_LEN, D), 1.0),
        "a_norm_mix": gain((N_A, D)),
        "a_w_in": nrm((N_A, D, 3 * DA_WIDTH + MEM_WIDTH), D ** -0.5),
        "a_lam_q1": nrm((N_A, DA_HEAD_DIM), 0.1),
        "a_lam_k1": nrm((N_A, DA_HEAD_DIM), 0.1),
        "a_lam_q2": nrm((N_A, DA_HEAD_DIM), 0.1),
        "a_lam_k2": nrm((N_A, DA_HEAD_DIM), 0.1),
        "a_subln": gain((N_A, 2 * DA_HEAD_DIM)),
        "a_mem_norm": gain((N_A, D)),
        "a_w_mem_kv": nrm((N_A, D, 2 * MEM_WIDTH), D ** -0.5),
        "a_w_out": nrm((N_A, MIX_WIDTH, D), MIX_WIDTH ** -0.5 * res),
        "b_norm_mix": gain((N_B, D)),
        "b_w_in": nrm((N_B, D, 2 * HG_KEY_WIDTH + 2 * HG_VAL_WIDTH + MEM_WIDTH), D ** -0.5),
        "b_lb_logits": nrm((N_B, HG_KEY_WIDTH), 0.5),
        "b_out_norm": gain((N_B, HG_VAL_DIM)),
        "b_mem_norm": gain((N_B, D)),
        "b_w_mem_kv": nrm((N_B, D, 2 * MEM_WIDTH), D ** -0.5),
        "b_w_out": nrm((N_B, HG_VAL_WIDTH + MEM_WIDTH, D), (HG_VAL_WIDTH + MEM_WIDTH) ** -0.5 * res),
        "dense_norm": gain((N_A, D)),
        "dense_w_gate_up": nrm((N_A, D, 2 * D_FF_DENSE), D ** -0.5),
        "dense_w_down": nrm((N_A, D_FF_DENSE, D), D_FF_DENSE ** -0.5 * res),
        "moe_norm": gain((N_B, D)),
        "moe_router": nrm((N_B, D, N_EXPERTS), D ** -0.5),
        "moe_w_gate_up": nrm((N_B, N_EXPERTS, D, 2 * D_FF_EXPERT), D ** -0.5),
        "moe_w_down": nrm((N_B, N_EXPERTS, D_FF_EXPERT, D), D_FF_EXPERT ** -0.5 * res),
        "final_norm": gain((D,)),
    }

def first_block(x, mem,
              a_norm_mix, a_w_in, a_lam_q1, a_lam_k1, a_lam_q2, a_lam_k2, a_subln, a_mem_norm, a_w_mem_kv, a_w_out,
              b_norm_mix, b_w_in, b_lb_logits, b_out_norm, b_mem_norm, b_w_mem_kv, b_w_out,
              dense_norm, dense_w_gate_up, dense_w_down,
              moe_norm, moe_router, moe_w_gate_up, moe_w_down,
              final_norm):
    lb_p = jax.nn.softmax(b_lb_logits.astype(F32), axis=0)
    lb_all = jnp.cumsum(lb_p, axis=0) - lb_p[0:1]
    for i in range(DEPTH):
        if i % N_MIXERS == 0:
            j = i // N_MIXERS
            lam_init = 0.8 - 0.6 * float(np.exp(-0.3 * i))
            h = rms_norm(x, a_norm_mix[j])
            x = x + diff_attention_mixer(h, mem, a_w_in[j], a_lam_q1[j], a_lam_k1[j], a_lam_q2[j], a_lam_k2[j],
                                         a_subln[j], a_mem_norm[j], a_w_mem_kv[j], a_w_out[j], lam_init)
        else:
            j = i // N_MIXERS
            h = rms_norm(x, b_norm_mix[j])
            x = x + hgrn2_mixer(h, mem, b_w_in[j], lb_all[j], b_out_norm[j], b_mem_norm[j],
                                b_w_mem_kv[j], b_w_out[j])
        if i % 2 == 0:
            j = i // 2
            x = x + dense_swiglu(rms_norm(x, dense_norm[j]), dense_w_gate_up[j], dense_w_down[j])
        else:
            j = i // 2
            x = x + moe_swiglu(rms_norm(x, moe_norm[j]), moe_router[j], moe_w_gate_up[j], moe_w_down[j])
    return rms_norm(x, final_norm)


RET_HEADS = 4
RET_DK = 256
RET_DV = 512
RET_CHUNK = 128
MLA_HEADS = 8
MLA_NOPE = 128
MLA_ROPE = 64
MLA_V = 128
MLA_Q_RANK = 256
MLA_KV_RANK = 256
ATTN_Q_BLOCK = 128
MOBA_HEADS = 16
MOBA_DH = D_MODEL // MOBA_HEADS
MOBA_BLOCK = 256
MOBA_TOPK = 3
MOBA_Q_CHUNK = 32

ROPE_THETA = 10000.0
LN_EPS = 1e-5
RMS_EPS = 1e-6
NEG = -1e30
DN_ALPHA = (2.0 * DEPTH) ** 0.25
DN_BETA = (8.0 * DEPTH) ** -0.25
N_EVEN = (DEPTH + 1) // 2
N_ODD = DEPTH // 2

RET_W = RET_HEADS * RET_DV
MLA_W = MLA_HEADS * MLA_V
MOBA_W = MOBA_HEADS * MOBA_DH
EVEN_SPLITS = (RET_HEADS * RET_DK, RET_HEADS * RET_DK, RET_W, RET_W,
               MLA_Q_RANK, MLA_KV_RANK, MLA_ROPE, MLA_W)
EVEN_IN = sum(EVEN_SPLITS)
ODD_SPLITS = (MOBA_W, MOBA_W, MOBA_W, MOBA_W)
ODD_IN = sum(ODD_SPLITS)


def _split(h, sizes):
    offs = np.cumsum(sizes)[:-1].tolist()
    return jnp.split(h, offs, axis=-1)

def _heads(t, n):
    B, S, W = t.shape
    return t.reshape(B, S, n, W // n).transpose(0, 2, 1, 3)

def _merge(t):
    B, H, S, d = t.shape
    return t.transpose(0, 2, 1, 3).reshape(B, S, H * d)

def layer_norm(x, g, b):
    xf = x.astype(jnp.float32)
    mu = jnp.mean(xf, -1, keepdims=True)
    xc = xf - mu
    var = jnp.mean(xc * xc, -1, keepdims=True)
    return (xc * lax.rsqrt(var + LN_EPS) * g + b).astype(x.dtype)

def rms_norm_2(x, g):
    xf = x.astype(jnp.float32)
    return (xf * lax.rsqrt(jnp.mean(xf * xf, -1, keepdims=True) + RMS_EPS) * g).astype(x.dtype)

def rope(x, pos):
    d = x.shape[-1]
    inv = 1.0 / (ROPE_THETA ** (jnp.arange(0, d, 2, dtype=jnp.float32) / d))
    ang = pos.astype(jnp.float32)[:, None, :, None] * inv
    cos, sin = jnp.cos(ang), jnp.sin(ang)
    x1, x2 = x[..., : d // 2], x[..., d // 2:]
    return jnp.concatenate([x1 * cos - x2 * sin, x1 * sin + x2 * cos], -1).astype(x.dtype)

def retnet_rotate(x, pos):
    d = x.shape[-1]
    inv = 1.0 / (ROPE_THETA ** jnp.linspace(0.0, 1.0, d // 2, dtype=jnp.float32))
    ang = pos.astype(jnp.float32)[:, None, :, None] * inv
    cos, sin = jnp.cos(ang), jnp.sin(ang)
    x1, x2 = x[..., 0::2], x[..., 1::2]
    out = jnp.stack([x1 * cos - x2 * sin, x2 * cos + x1 * sin], -1)
    return out.reshape(x.shape).astype(x.dtype)

def retention_chunkwise(q, k, v):
    B, H, S, dk = q.shape
    dv = v.shape[-1]
    C = RET_CHUNK
    n = S // C
    q = q.astype(jnp.float32)
    k = k.astype(jnp.float32) * (dk ** -0.5)
    v = v.astype(jnp.float32)
    log_g = jnp.log(1.0 - 2.0 ** (-5.0 - jnp.arange(H, dtype=jnp.float32)))
    qc = q.reshape(B, H, n, C, dk)
    kc = k.reshape(B, H, n, C, dk)
    vc = v.reshape(B, H, n, C, dv)
    idx = jnp.arange(C, dtype=jnp.float32)
    rel = idx[:, None] - idx[None, :]
    decay = jnp.where(rel >= 0, jnp.exp(log_g[:, None, None] * jnp.maximum(rel, 0.0)), 0.0)
    inner = jnp.einsum('bhncd,bhnkd->bhnck', qc, kc) * decay[None, :, None]
    o_inner = jnp.einsum('bhnck,bhnkv->bhncv', inner, vc)
    zeta = jnp.exp(log_g[:, None] * (C - 1.0 - idx))
    kv_chunk = jnp.einsum('bhnkd,bhnkv->bhndv', kc * zeta[None, :, None, :, None], vc)
    g_chunk = jnp.exp(log_g * C)[None, :, None, None]

    def step(R, kv):
        return R * g_chunk + kv, R

    _, r_prev = lax.scan(step, jnp.zeros((B, H, dk, dv), jnp.float32), jnp.moveaxis(kv_chunk, 2, 0))
    r_prev = jnp.moveaxis(r_prev, 0, 2)
    xi = jnp.exp(log_g[:, None] * (idx + 1.0))
    o_cross = jnp.einsum('bhncd,bhndv->bhncv', qc, r_prev) * xi[None, :, None, :, None]
    return (o_inner + o_cross).reshape(B, H, S, dv)

def head_group_norm(o):
    of = o.astype(jnp.float32)
    mu = jnp.mean(of, -1, keepdims=True)
    oc = of - mu
    var = jnp.mean(oc * oc, -1, keepdims=True)
    return oc * lax.rsqrt(var + LN_EPS)

def causal_attention(q, k, v, scale):
    B, H, S, d = q.shape
    dv = v.shape[-1]
    nq = S // ATTN_Q_BLOCK
    qb = q.reshape(B, H, nq, ATTN_Q_BLOCK, d).transpose(2, 0, 1, 3, 4)
    kpos = jnp.arange(S)

    def one(args):
        qi, i = args
        s = jnp.einsum('bhqd,bhkd->bhqk', qi, k).astype(jnp.float32) * scale
        qpos = i * ATTN_Q_BLOCK + jnp.arange(ATTN_Q_BLOCK)
        s = jnp.where(kpos[None, :] <= qpos[:, None], s, NEG)
        p = jax.nn.softmax(s, axis=-1).astype(v.dtype)
        return jnp.einsum('bhqk,bhkd->bhqd', p, v)

    out = lax.map(one, (qb, jnp.arange(nq)))
    return out.transpose(1, 2, 0, 3, 4).reshape(B, H, S, dv)

def moba_attention(q, k, v):
    B, H, S, dh = q.shape
    L = MOBA_BLOCK
    nb = -(-S // L)
    pad = nb * L - S
    kp = jnp.pad(k, ((0, 0), (0, 0), (0, pad), (0, 0)))
    vp = jnp.pad(v, ((0, 0), (0, 0), (0, pad), (0, 0)))
    kb = kp.reshape(B, H, nb, L, dh)
    vb = vp.reshape(B, H, nb, L, dh)
    kmean = jnp.mean(kb.astype(jnp.float32), axis=3)
    qblk = jnp.arange(S) // L
    gate = jnp.einsum('bhsd,bhnd->bhsn', q.astype(jnp.float32), kmean)
    past = jnp.arange(nb)[None, :] < qblk[:, None]
    gate = jnp.where(past, gate, NEG)
    k_sel = min(MOBA_TOPK, nb)
    _, sel = lax.top_k(gate, k_sel)
    valid = jnp.arange(k_sel)[None, :] < qblk[:, None]
    scale = dh ** -0.5
    Qc = MOBA_Q_CHUNK
    nc = S // Qc
    qch = jnp.moveaxis(q.reshape(B, H, nc, Qc, dh), 2, 0)
    selch = jnp.moveaxis(sel.reshape(B, H, nc, Qc, k_sel), 2, 0)
    validch = valid.reshape(nc, Qc, k_sel)
    bi = jnp.arange(B)[:, None, None, None]
    hi = jnp.arange(H)[None, :, None, None]

    def one(args):
        qi, si, vi, c = args
        q0 = c * Qc
        qpos = q0 + jnp.arange(Qc)
        own = q0 // L
        kg = kb[bi, hi, si]
        vg = vb[bi, hi, si]
        s_g = jnp.einsum('bhqd,bhqnld->bhqnl', qi, kg).astype(jnp.float32) * scale
        s_g = jnp.where(vi[None, None, :, :, None], s_g, NEG)
        ko = lax.dynamic_slice_in_dim(kp, own * L, L, axis=2)
        vo = lax.dynamic_slice_in_dim(vp, own * L, L, axis=2)
        s_o = jnp.einsum('bhqd,bhld->bhql', qi, ko).astype(jnp.float32) * scale
        kpos = own * L + jnp.arange(L)
        s_o = jnp.where(kpos[None, :] <= qpos[:, None], s_o, NEG)
        s = jnp.concatenate([s_g.reshape(B, H, Qc, k_sel * L), s_o], axis=-1)
        p = jax.nn.softmax(s, axis=-1).astype(v.dtype)
        p_g = p[..., : k_sel * L].reshape(B, H, Qc, k_sel, L)
        p_o = p[..., k_sel * L:]
        return (jnp.einsum('bhqnl,bhqnld->bhqd', p_g, vg)
                + jnp.einsum('bhql,bhld->bhqd', p_o, vo))

    out = lax.map(one, (qch, selch, validch, jnp.arange(nc)))
    return jnp.moveaxis(out, 0, 2).reshape(B, H, S, dh)

def retention_mla_layer(x, pos, w_in, q_norm_g, w_uq, kv_norm_g, w_ukv, w_out):
    B, S, _ = x.shape
    h = x @ w_in
    rq, rk, rv, rg, mq, mkv, mkr, mg = _split(h, EVEN_SPLITS)
    q_r = retnet_rotate(_heads(rq, RET_HEADS), pos)
    k_r = retnet_rotate(_heads(rk, RET_HEADS), pos)
    o_r = head_group_norm(retention_chunkwise(q_r, k_r, _heads(rv, RET_HEADS)))
    ret_out = (_merge(o_r) * jax.nn.silu(rg.astype(jnp.float32))).astype(x.dtype)
    q_m = (rms_norm_2(mq, q_norm_g) @ w_uq).reshape(B, S, MLA_HEADS, MLA_NOPE + MLA_ROPE).transpose(0, 2, 1, 3)
    q_nope, q_pe = q_m[..., :MLA_NOPE], rope(q_m[..., MLA_NOPE:], pos)
    kv = (rms_norm_2(mkv, kv_norm_g) @ w_ukv).reshape(B, S, MLA_HEADS, MLA_NOPE + MLA_V).transpose(0, 2, 1, 3)
    k_nope, v_m = kv[..., :MLA_NOPE], kv[..., MLA_NOPE:]
    k_pe = rope(mkr[:, None], pos)
    q_full = jnp.concatenate([q_nope, q_pe], -1)
    k_full = jnp.concatenate([k_nope, jnp.broadcast_to(k_pe, (B, MLA_HEADS, S, MLA_ROPE))], -1)
    o_m = causal_attention(q_full, k_full, v_m, (MLA_NOPE + MLA_ROPE) ** -0.5)
    mla_out = (_merge(o_m) * jax.nn.silu(mg)).astype(x.dtype)
    return jnp.concatenate([ret_out, mla_out], axis=-1) @ w_out

def moba_layer(x, pos, w_in, w_out):
    h = x @ w_in
    q, k, v, g = _split(h, ODD_SPLITS)
    q = rope(_heads(q, MOBA_HEADS), pos)
    k = rope(_heads(k, MOBA_HEADS), pos)
    o = moba_attention(q, k, _heads(v, MOBA_HEADS))
    return (_merge(o) * jax.nn.silu(g)) @ w_out

def second_inputs(seed: int = 0) -> dict:
    key = jax.random.key(seed)
    ks = jax.random.split(key, 16)
    f32 = jnp.float32
    nrm = lambda k, shape, fan_in, gain=1.0: jax.random.normal(k, shape, f32) * (gain * fan_in ** -0.5)
    x = jax.random.normal(ks[0], (BATCH, SEQ, D_MODEL), f32)
    offs = jax.random.randint(ks[1], (BATCH, 1), 0, 1024, dtype=jnp.int32)
    positions = (offs + jnp.arange(SEQ, dtype=jnp.int32)[None, :]).astype(jnp.int32)
    return {
        "x": x,
        "positions": positions,
        "w_in_even": nrm(ks[2], (N_EVEN, D_MODEL, EVEN_IN), D_MODEL),
        "q_norm_even": 1.0 + 0.02 * jax.random.normal(ks[3], (N_EVEN, MLA_Q_RANK), f32),
        "w_uq_even": nrm(ks[4], (N_EVEN, MLA_Q_RANK, MLA_HEADS * (MLA_NOPE + MLA_ROPE)), MLA_Q_RANK),
        "kv_norm_even": 1.0 + 0.02 * jax.random.normal(ks[5], (N_EVEN, MLA_KV_RANK), f32),
        "w_ukv_even": nrm(ks[6], (N_EVEN, MLA_KV_RANK, MLA_HEADS * (MLA_NOPE + MLA_V)), MLA_KV_RANK),
        "w_out_even": nrm(ks[7], (N_EVEN, RET_W + MLA_W, D_MODEL), RET_W + MLA_W, DN_BETA),
        "w_in_odd": nrm(ks[8], (N_ODD, D_MODEL, ODD_IN), D_MODEL),
        "w_out_odd": nrm(ks[9], (N_ODD, MOBA_W, D_MODEL), MOBA_W, DN_BETA),
        "ln_g": 1.0 + 0.02 * jax.random.normal(ks[10], (DEPTH, D_MODEL), f32),
        "ln_b": 0.02 * jax.random.normal(ks[11], (DEPTH, D_MODEL), f32),
    }

def second_block(x, positions, w_in_even, q_norm_even, w_uq_even, kv_norm_even, w_ukv_even,
              w_out_even, w_in_odd, w_out_odd, ln_g, ln_b):
    for i in range(DEPTH):
        j = i // 2
        if i % 2 == 0:
            y = retention_mla_layer(x, positions, w_in_even[j], q_norm_even[j], w_uq_even[j],
                                    kv_norm_even[j], w_ukv_even[j], w_out_even[j])
        else:
            y = moba_layer(x, positions, w_in_odd[j], w_out_odd[j])
        x = layer_norm(DN_ALPHA * x + y, ln_g[i], ln_b[i])
    return x


DEPTH_3 = 1

W_MIX = 1024
N_BRANCH = 3
W_A = W_MIX
H_A = 4
DH_A = W_A // H_A
MLSTM_CHUNK = 64
QK_CONV = 4
W_B = W_MIX
CONF_K = 31
W_C = W_MIX
H_C = 8
DH_C = W_C // H_C
G_C = 2
HPG_C = H_C // G_C
KV_W = G_C * DH_C
CMP_LEN = 32
CMP_STRIDE = 16
CMP_HIDDEN = 256
SLC_LEN = 64
N_SLC = 16
WINDOW = 512
NSA_QBLOCK = 64
NEG_3 = -1e30

IN_SPLITS = (W_A, W_A, W_A, W_A, W_A, H_A, H_A,
             W_B, W_B, W_B,
             W_C, KV_W, KV_W, KV_W, KV_W, KV_W, KV_W, 3 * H_C, W_C,
             N_BRANCH * D_MODEL)
N_IN = sum(IN_SPLITS)
F_GATE_OFFSET = 5 * W_A + H_A


def split_cols(t):
    return jnp.split(t, np.cumsum(IN_SPLITS)[:-1].tolist(), axis=-1)

def rmsnorm(x, g, eps=1e-6):
    xf = x.astype(jnp.float32)
    y = xf * lax.rsqrt(jnp.mean(xf * xf, axis=-1, keepdims=True) + eps)
    return y.astype(x.dtype) * g

def layernorm(x, g, b, eps=1e-5):
    xf = x.astype(jnp.float32)
    mu = jnp.mean(xf, axis=-1, keepdims=True)
    var = jnp.mean(jnp.square(xf - mu), axis=-1, keepdims=True)
    y = (xf - mu) * lax.rsqrt(var + eps)
    return y.astype(x.dtype) * g + b

def causal_dwconv(x, w, b):
    k = w.shape[0]
    y = lax.conv_general_dilated(x, w[:, None, :].astype(x.dtype), (1,), [(k - 1, 0)],
                                 dimension_numbers=('NWC', 'WIO', 'NWC'),
                                 feature_group_count=x.shape[-1])
    return y + b

def masked_softmax(s, mask):
    s = jnp.where(mask, s, NEG_3)
    p = jnp.exp(s - jnp.max(s, axis=-1, keepdims=True)) * mask
    return p / jnp.maximum(jnp.sum(p, axis=-1, keepdims=True), 1e-30)

def mlstm_chunkwise(q, k, v, ig, lf):
    b, s, h, dk = q.shape
    dv = v.shape[-1]
    nc = s // MLSTM_CHUNK

    def chunks(t):
        t = t.astype(jnp.float32).reshape((b, nc, MLSTM_CHUNK, h) + t.shape[3:])
        return jnp.moveaxis(jnp.moveaxis(t, 1, 0), 3, 2)

    causal = jnp.tril(jnp.ones((MLSTM_CHUNK, MLSTM_CHUNK), bool))

    def step(carry, inp):
        C, n, m = carry
        qc, kc, vc, ic, fc = inp
        bcum = jnp.cumsum(fc, axis=-1)
        dmat = jnp.where(causal, bcum[..., :, None] - bcum[..., None, :] + ic[..., None, :], -jnp.inf)
        m_inter = bcum + m[..., None]
        m_t = jnp.maximum(m_inter, jnp.max(dmat, axis=-1))
        w = jnp.exp(dmat - m_t[..., None])
        a_inter = jnp.exp(m_inter - m_t)
        sqk = jnp.einsum('bhtd,bhsd->bhts', qc, kc) * w
        num = jnp.einsum('bhts,bhse->bhte', sqk, vc) + a_inter[..., None] * jnp.einsum('bhtd,bhde->bhte', qc, C)
        den = jnp.sum(sqk, axis=-1) + a_inter * jnp.einsum('bhtd,bhd->bht', qc, n)
        h_out = num / jnp.maximum(jnp.abs(den), jnp.exp(-m_t))[..., None]
        b_last = bcum[..., -1]
        g = b_last[..., None] - bcum + ic
        m_new = jnp.maximum(b_last + m, jnp.max(g, axis=-1))
        decay = jnp.exp(b_last + m - m_new)
        wk = jnp.exp(g - m_new[..., None])[..., None] * kc
        C = decay[..., None, None] * C + jnp.einsum('bhsd,bhse->bhde', wk, vc)
        n = decay[..., None] * n + jnp.sum(wk, axis=2)
        return (C, n, m_new), h_out

    init = (jnp.zeros((b, h, dk, dv), jnp.float32), jnp.zeros((b, h, dk), jnp.float32),
            jnp.zeros((b, h), jnp.float32))
    _, hs = lax.scan(step, init, (chunks(q), chunks(k), chunks(v), chunks(ig), chunks(lf)))
    return hs.transpose(1, 0, 3, 2, 4).reshape(b, s, h, dv).astype(q.dtype)

def nsa(q, k_cmp, v_cmp, k_slc, v_slc, k_win, v_win, gates, pe, w1, w2):
    b, s = q.shape[:2]
    scale = DH_C ** -0.5

    def compress(t, j):
        tb = t.reshape(b, s // CMP_STRIDE, CMP_STRIDE, G_C, DH_C)
        blk = jnp.concatenate([tb[:, :-1], tb[:, 1:]], axis=2) + pe[j][None, None, :, None, :]
        blk = blk.transpose(0, 1, 3, 2, 4).reshape(b, -1, G_C, CMP_LEN * DH_C)
        return jax.nn.gelu(blk @ w1[j]) @ w2[j]

    kc = compress(k_cmp, 0)
    vc = compress(v_cmp, 1)
    n_cmp = kc.shape[1]
    cmp_start = jnp.arange(n_cmp) * CMP_STRIDE
    cmp_end = cmp_start + CMP_LEN - 1
    n_slc = s // SLC_LEN
    n_sel = min(N_SLC, n_slc)
    slc_start = jnp.arange(n_slc) * SLC_LEN
    overlap = ((cmp_start[:, None] < slc_start[None, :] + SLC_LEN) &
               (cmp_start[:, None] + CMP_LEN > slc_start[None, :])).astype(jnp.float32)
    ks_blocks = k_slc.reshape(b, n_slc, SLC_LEN, G_C, DH_C).transpose(0, 3, 1, 2, 4)
    vs_blocks = v_slc.reshape(b, n_slc, SLC_LEN, G_C, DH_C).transpose(0, 3, 1, 2, 4)
    pad = ((0, 0), (WINDOW, 0), (0, 0), (0, 0))
    kw_pad = jnp.pad(k_win, pad)
    vw_pad = jnp.pad(v_win, pad)
    gather = jax.vmap(jax.vmap(lambda blocks, idx: blocks[idx]))
    jb = jnp.arange(n_slc)

    def block(i):
        qs = i * NSA_QBLOCK
        t = qs + jnp.arange(NSA_QBLOCK)
        qb = lax.dynamic_slice_in_dim(q, qs, NSA_QBLOCK, axis=1).reshape(b, NSA_QBLOCK, G_C, HPG_C, DH_C)
        gb = jax.nn.sigmoid(lax.dynamic_slice_in_dim(gates, qs, NSA_QBLOCK, axis=1)
                            .reshape(b, NSA_QBLOCK, G_C, HPG_C, 3))
        s_c = jnp.einsum('bqgjd,bngd->bgjqn', qb, kc).astype(jnp.float32) * scale
        p_c = masked_softmax(s_c, cmp_end[None, :] <= t[:, None])
        o_c = jnp.einsum('bgjqn,bngd->bqgjd', p_c.astype(vc.dtype), vc)
        imp = jnp.einsum('bgjqn,nm->bgqm', p_c, overlap)
        cur = t // SLC_LEN
        forced = (jb[None] == 0) | (jb[None] == cur[:, None]) | (jb[None] == cur[:, None] - 1)
        imp = jnp.where(jb[None] > cur[:, None], -1e4, jnp.where(forced, 1e4, imp))
        _, idx = lax.top_k(imp, n_sel)
        ks = gather(ks_blocks, idx).reshape(b, G_C, NSA_QBLOCK, n_sel * SLC_LEN, DH_C)
        vs = gather(vs_blocks, idx).reshape(b, G_C, NSA_QBLOCK, n_sel * SLC_LEN, DH_C)
        pos = (idx[..., None] * SLC_LEN + jnp.arange(SLC_LEN)).reshape(b, G_C, NSA_QBLOCK, n_sel * SLC_LEN)
        s_s = jnp.einsum('bqgjd,bgqkd->bgjqk', qb, ks).astype(jnp.float32) * scale
        p_s = masked_softmax(s_s, (pos <= t[:, None])[:, :, None])
        o_s = jnp.einsum('bgjqk,bgqkd->bqgjd', p_s.astype(vs.dtype), vs)
        kw = lax.dynamic_slice_in_dim(kw_pad, qs, NSA_QBLOCK + WINDOW, axis=1)
        vw = lax.dynamic_slice_in_dim(vw_pad, qs, NSA_QBLOCK + WINDOW, axis=1)
        pw = qs - WINDOW + jnp.arange(NSA_QBLOCK + WINDOW)
        dlt = t[:, None] - pw[None, :]
        mask_w = (dlt >= 0) & (dlt < WINDOW) & (pw[None, :] >= 0)
        s_w = jnp.einsum('bqgjd,bkgd->bgjqk', qb, kw).astype(jnp.float32) * scale
        p_w = masked_softmax(s_w, mask_w)
        o_w = jnp.einsum('bgjqk,bkgd->bqgjd', p_w.astype(vw.dtype), vw)
        return gb[..., 0:1] * o_c + gb[..., 1:2] * o_s + gb[..., 2:3] * o_w

    out = lax.map(block, jnp.arange(s // NSA_QBLOCK))
    return out.transpose(1, 0, 2, 3, 4, 5).reshape(b, s, W_C)

def third_inputs(seed: int = 0) -> dict:
    key = jax.random.key(seed)
    ks = jax.random.split(key, 20)
    L = DEPTH_3

    def nrm(k, shape, sc):
        return jax.random.normal(k, shape, jnp.float32) * sc

    b_in = nrm(ks[7], (L, N_IN), 0.02)
    b_in = b_in.at[:, F_GATE_OFFSET:F_GATE_OFFSET + H_A].add(jnp.linspace(3.0, 6.0, H_A))
    return {
        'x': nrm(ks[0], (BATCH, SEQ, D_MODEL), 1.0),
        'c': nrm(ks[1], (BATCH, D_MODEL), 1.0),
        'w_ada': nrm(ks[2], (L, D_MODEL, 3 * D_MODEL), 0.3 * D_MODEL ** -0.5),
        'b_ada': nrm(ks[3], (L, 3 * D_MODEL), 0.02),
        'norm_pre': 1.0 + nrm(ks[4], (L, D_MODEL), 0.02),
        'norm_post': 1.0 + nrm(ks[5], (L, D_MODEL), 0.02),
        'w_in': nrm(ks[6], (L, D_MODEL, N_IN), D_MODEL ** -0.5),
        'b_in': b_in,
        'mlstm_conv_w': nrm(ks[8], (L, QK_CONV, 2 * W_A), QK_CONV ** -0.5),
        'mlstm_conv_b': nrm(ks[9], (L, 2 * W_A), 0.02),
        'mlstm_norm': 1.0 + nrm(ks[10], (L, W_A), 0.02),
        'conf_dw_w': nrm(ks[11], (L, CONF_K, W_B), CONF_K ** -0.5),
        'conf_dw_b': nrm(ks[12], (L, W_B), 0.02),
        'conf_ln_g': 1.0 + nrm(ks[13], (L, W_B), 0.02),
        'conf_ln_b': nrm(ks[14], (L, W_B), 0.02),
        'nsa_cmp_pe': nrm(ks[15], (L, 2, CMP_LEN, DH_C), 0.02),
        'nsa_cmp_w1': nrm(ks[16], (L, 2, CMP_LEN * DH_C, CMP_HIDDEN), (CMP_LEN * DH_C) ** -0.5),
        'nsa_cmp_w2': nrm(ks[17], (L, 2, CMP_HIDDEN, DH_C), CMP_HIDDEN ** -0.5),
        'w_branch': nrm(ks[18], (L, N_BRANCH, W_MIX, D_MODEL), W_MIX ** -0.5),
        'w_out': nrm(ks[19], (L, D_MODEL, D_MODEL), D_MODEL ** -0.5),
    }

def third_block(x, c, w_ada, b_ada, norm_pre, norm_post, w_in, b_in, mlstm_conv_w, mlstm_conv_b,
              mlstm_norm, conf_dw_w, conf_dw_b, conf_ln_g, conf_ln_b, nsa_cmp_pe, nsa_cmp_w1,
              nsa_cmp_w2, w_branch, w_out):
    b, s = x.shape[:2]
    for l in range(DEPTH_3):
        shift, scale, gate = jnp.split(c @ w_ada[l] + b_ada[l], 3, axis=-1)
        h = rmsnorm(x, norm_pre[l]) * (1.0 + scale[:, None]) + shift[:, None]
        proj = h @ w_in[l] + b_in[l]
        (aq, ak, av, ao, az, ai, af, ba, bb, bz,
         cq, ckc, cvc, cks, cvs, ckw, cvw, cg, cz, mg) = split_cols(proj)

        qk = jax.nn.silu(causal_dwconv(jnp.concatenate([aq, ak], axis=-1), mlstm_conv_w[l], mlstm_conv_b[l]))
        mq, mk = jnp.split(qk, 2, axis=-1)
        hcell = mlstm_chunkwise(mq.reshape(b, s, H_A, DH_A) * DH_A ** -0.5, mk.reshape(b, s, H_A, DH_A),
                                av.reshape(b, s, H_A, DH_A), ai, jax.nn.log_sigmoid(af))
        hf = hcell.astype(jnp.float32)
        mu = jnp.mean(hf, axis=-1, keepdims=True)
        hf = (hf - mu) * lax.rsqrt(jnp.mean(jnp.square(hf - mu), axis=-1, keepdims=True) + 1e-5)
        hn = hf.reshape(b, s, W_A).astype(x.dtype) * mlstm_norm[l]
        y_a = jax.nn.sigmoid(ao) * hn * jax.nn.silu(az)

        u = causal_dwconv(ba * jax.nn.sigmoid(bb), conf_dw_w[l], conf_dw_b[l])
        y_b = jax.nn.silu(layernorm(u, conf_ln_g[l], conf_ln_b[l])) * jax.nn.silu(bz)

        hc = nsa(cq.reshape(b, s, H_C, DH_C),
                 ckc.reshape(b, s, G_C, DH_C), cvc.reshape(b, s, G_C, DH_C),
                 cks.reshape(b, s, G_C, DH_C), cvs.reshape(b, s, G_C, DH_C),
                 ckw.reshape(b, s, G_C, DH_C), cvw.reshape(b, s, G_C, DH_C),
                 cg.reshape(b, s, H_C, 3), nsa_cmp_pe[l], nsa_cmp_w1[l], nsa_cmp_w2[l])
        y_c = hc * jax.nn.silu(cz)

        g = jax.nn.sigmoid(mg).reshape(b, s, N_BRANCH, D_MODEL)
        merged = (g[:, :, 0] * (y_a @ w_branch[l, 0]) + g[:, :, 1] * (y_b @ w_branch[l, 1])
                  + g[:, :, 2] * (y_c @ w_branch[l, 2]))
        out = merged @ w_out[l]
        x = x + gate[:, None] * rmsnorm(out, norm_post[l])
    return x


_first_inputs = third_inputs


def third_inputs(seed=0):
    import zlib

    import numpy as np

    out = dict(_first_inputs(seed))
    spreads = {}
    factors = {'norm_pre': 5.99,
     'norm_post': 22.092,
     'mlstm_conv_b': 64.0,
     'mlstm_norm': 47.383,
     'conf_dw_b': 7.761,
     'conf_ln_g': 41.957,
     'conf_ln_b': 43.396,
     'nsa_cmp_pe': 30.331}
    for name, (base, spread) in spreads.items():
        noise = np.random.default_rng([zlib.crc32(name.encode()), seed]).standard_normal(out[name].shape)
        drawn = base * np.exp(spread * noise) if base else spread * noise
        out[name] = __import__('jax').numpy.asarray(drawn.astype(out[name].dtype))
    for name, factor in factors.items():
        out[name] = (out[name] * factor).astype(out[name].dtype)
    return out


_narrow_inputs = third_inputs


def third_inputs(seed=0):

    out = dict(_narrow_inputs(seed))
    wider = {'mlstm_conv_b': 5.91,
     'mlstm_norm': 4.62,
     'conf_ln_g': 4.63,
     'conf_ln_b': 4.63,
     'nsa_cmp_pe': 5.12}
    for name, times in wider.items():
        mean = out[name].mean()
        out[name] = (mean + times * (out[name] - mean)).astype(out[name].dtype)
    return out


def setup_inputs(seed=0):
    out = dict(first_inputs(seed))
    for name, value in second_inputs(seed + 1).items():
        if name != "x":
            out[name + "_2"] = value
    for name, value in third_inputs(seed + 2).items():
        if name != "x":
            out[name + "_3"] = value
    return out


def reference(
    x, mem, a_norm_mix, a_w_in, a_lam_q1, a_lam_k1, a_lam_q2, a_lam_k2, a_subln, a_mem_norm,
    a_w_mem_kv, a_w_out, b_norm_mix, b_w_in, b_lb_logits, b_out_norm, b_mem_norm, b_w_mem_kv,
    b_w_out, dense_norm, dense_w_gate_up, dense_w_down, moe_norm, moe_router, moe_w_gate_up,
    moe_w_down, final_norm, positions_2, w_in_even_2, q_norm_even_2, w_uq_even_2,
    kv_norm_even_2, w_ukv_even_2, w_out_even_2, w_in_odd_2, w_out_odd_2, ln_g_2, ln_b_2, c_3,
    w_ada_3, b_ada_3, norm_pre_3, norm_post_3, w_in_3, b_in_3, mlstm_conv_w_3, mlstm_conv_b_3,
    mlstm_norm_3, conf_dw_w_3, conf_dw_b_3, conf_ln_g_3, conf_ln_b_3, nsa_cmp_pe_3,
    nsa_cmp_w1_3, nsa_cmp_w2_3, w_branch_3, w_out_3,
):
    x = first_block(
        x, mem, a_norm_mix, a_w_in, a_lam_q1, a_lam_k1, a_lam_q2, a_lam_k2, a_subln, a_mem_norm,
        a_w_mem_kv, a_w_out, b_norm_mix, b_w_in, b_lb_logits, b_out_norm, b_mem_norm,
        b_w_mem_kv, b_w_out, dense_norm, dense_w_gate_up, dense_w_down, moe_norm, moe_router,
        moe_w_gate_up, moe_w_down, final_norm,
    )
    x = second_block(
        x, positions_2, w_in_even_2, q_norm_even_2, w_uq_even_2, kv_norm_even_2, w_ukv_even_2,
        w_out_even_2, w_in_odd_2, w_out_odd_2, ln_g_2, ln_b_2,
    )
    return third_block(
        x, c_3, w_ada_3, b_ada_3, norm_pre_3, norm_post_3, w_in_3, b_in_3, mlstm_conv_w_3,
        mlstm_conv_b_3, mlstm_norm_3, conf_dw_w_3, conf_dw_b_3, conf_ln_g_3, conf_ln_b_3,
        nsa_cmp_pe_3, nsa_cmp_w1_3, nsa_cmp_w2_3, w_branch_3, w_out_3,
    )


_drawn_inputs = setup_inputs


def setup_inputs(seed=0):
    import zlib

    import numpy as np

    out = dict(_drawn_inputs(seed))
    spreads = {}
    factors = {'a_mem_norm': 8.0,
     'b_out_norm': 3.324,
     'b_mem_norm': 8.0,
     'q_norm_even_2': 8.0,
     'kv_norm_even_2': 8.0,
     'norm_post_3': 2.958,
     'mlstm_conv_b_3': 2.692}
    for name, (base, spread) in spreads.items():
        noise = np.random.default_rng([zlib.crc32(name.encode()), seed]).standard_normal(out[name].shape)
        drawn = base * np.exp(spread * noise) if base else spread * noise
        out[name] = __import__('jax').numpy.asarray(drawn.astype(out[name].dtype))
    for name, factor in factors.items():
        out[name] = (out[name] * factor).astype(out[name].dtype)
    return out
```

```python
from contextlib import ExitStack, contextmanager

import numpy as np

import concourse.bass as bass
from concourse import mybir

F32 = mybir.dt.float32
I32 = mybir.dt.int32
U32 = mybir.dt.uint32
ACT = mybir.ActivationFunctionType
ALU = mybir.AluOpType
AX_X = mybir.AxisListType.X
ds = bass.ds

P = 128
S = 256
TT = S // P
D = 1024
DC = D // P
SLOTS = 3
SLOT = 4096
STAGE_SEMS = range(190, 232)
NEG = -1e30


def alibi_slopes(n):
    return 2.0 ** (-8.0 * np.arange(1, n + 1) / n)


def constant_arrays():
    t = np.arange(S)
    c = {}
    c["ident"] = np.eye(P)
    c["upper"] = np.triu(np.ones((P, P)))
    c["ones"] = np.ones((P, P))

    def token_major(m):
        return m.reshape(TT, P, -1).transpose(1, 0, 2)

    causal = np.where(t[None, :] <= t[:, None], 0.0, NEG)
    c["causal"] = token_major(causal)
    allowed = (t[None, :] // 64) <= (t[:, None] // 64)
    dist = np.abs(t[:, None] - t[None, :]).astype(np.float32)
    c["alibi"] = np.stack([token_major(np.where(allowed, -np.float32(s) * dist * 8.0, NEG))
                           for s in alibi_slopes(6)], 1)
    rel = (t[None, :] - t[:, None]).astype(np.float64)
    log_g = np.log(1.0 - 2.0 ** (-5.0 - np.arange(4)))
    c["decay"] = np.stack([token_major(np.where(rel >= 0, np.exp(g * np.maximum(rel, 0)) / 16.0, 0.0))
                           for g in log_g], 1)
    j, tt = np.arange(P)[:, None], np.arange(P)[None, :]
    sums, masks = [np.where(j > tt, 1.0, 0.0)], []
    for half in (64, 32, 16, 8, 4, 2, 1):
        mid = (tt // (2 * half)) * 2 * half + half
        sums.append(np.where(tt >= mid, (j >= mid) & (j <= tt), (j > tt) & (j < mid)))
        s_, t_ = np.arange(P)[:, None], np.arange(P)[None, :]
        masks.append((s_ // (2 * half) == t_ // (2 * half)) & (s_ % (2 * half) < half) & (t_ % (2 * half) >= half))
    sums.append(np.where(j <= tt, 1.0, 0.0))
    masks.append(np.eye(P))
    c["levels"] = np.stack(sums, 1)
    c["level_masks"] = np.stack(masks, 1)
    pair = np.zeros((P, P))
    for i in range(0, P, 2):
        pair[i, i + 1], pair[i + 1, i] = -1.0, 1.0
    half = np.zeros((P, P))
    for b in (0, 64):
        for i in range(32):
            half[b + i, b + 32 + i], half[b + 32 + i, b + i] = -1.0, 1.0
    c["pair_rot"], c["half_rot"] = pair.T, half.T
    lin = np.linspace(0.0, 1.0, P, dtype=np.float32)
    ret = (np.float32(1.0) / (np.float32(10000.0) ** lin)).astype(np.float32)
    ang = (np.float32(1.0) / np.float32(10000.0) ** (np.arange(0, 64, 2, dtype=np.float32) / np.float32(64))
           ).astype(np.float32)
    c["freq"] = np.stack([np.repeat(ret[:64], 2), np.repeat(ret[64:], 2), np.tile(ang, 4)], 1)
    n_cmp = S // 16 - 1
    end = np.arange(n_cmp) * 16 + 31
    c["cmp_mask"] = token_major(np.where(end[None, :] <= t[:, None], 0.0, NEG))
    c["experts"] = np.tile(np.arange(8.0), (P, 1))
    return {k: np.ascontiguousarray(v.reshape(v.shape[0], -1), dtype=np.float32) for k, v in c.items()}


def column_table():
    rows, at = [], {}

    def add(key, name, offset, n):
        at[key] = sum(r[2] for r in rows)
        rows.append((name, offset, n))

    for key, n in (("a_norm_mix", 8), ("a_mem_norm", 8), ("b_norm_mix", 8), ("b_mem_norm", 8), ("dense_norm", 8),
                   ("moe_norm", 8), ("a_subln", 1), ("b_out_norm", 1), ("q_norm_even_2", 2), ("kv_norm_even_2", 2),
                   ("norm_pre_3", 8), ("mlstm_norm_3", 8), ("conf_ln_g_3", 8), ("conf_ln_b_3", 8),
                   ("conf_dw_b_3", 8), ("mlstm_conv_b_3", 16)):
        add(key, key, 0, n)
    add("shift", "b_ada_3", 0, 8)
    add("scale", "b_ada_3", 1024, 8)
    for key, off, n in (("qk", 0, 16), ("ao", 3072, 8), ("az", 4096, 8), ("ba", 5128, 8), ("bb", 6152, 8),
                        ("bz", 7176, 8), ("cq", 8200, 8), ("ckc", 9224, 2), ("cvc", 9480, 2), ("cks", 9736, 2),
                        ("ckw", 10248, 2), ("cz", 10784, 8), ("mg", 11808, 24)):
        add(key, "b_in_3", off, n)
    add("conv", "mlstm_conv_w_3", 0, 64)
    add("pe", "nsa_cmp_pe_3", 0, 64)
    add("dw", "conf_dw_w_3", 0, 248)
    return rows, at


COLUMN_ROWS, COL = column_table()
N_COLS = sum(r[2] for r in COLUMN_ROWS)


class Fields:
    pass


class Order:

    def __init__(self, eng, sem):
        self.eng, self.sem, self.n = eng, sem, 0

    def __call__(self, instruction):
        instruction.then_inc(self.sem, 1)
        self.n += 1
        self.eng.wait_ge(self.sem, self.n)


class Stage:

    def __init__(self, nc, block, stack):
        self.nc, self.block, self.stack, self.n = nc, block, stack, 0

    def sem(self, name):
        s = self.stack.enter_context(self.nc.semaphore(name, num=STAGE_SEMS[self.n]))
        self.n += 1
        return s


@contextmanager
def stage(k, name):
    nc = k.nc
    with ExitStack() as stack:
        with nc.Block(no_gpsimd_drain=True) as block:
            st = Stage(nc, block, stack)
            st.name = name
            yield st
        if st.n:
            nc.all_engine_barrier(sems_to_clear=range(STAGE_SEMS[0], STAGE_SEMS[0] + st.n))


def run(kind, w, c0, src, evict, on="act", count=1, width=512, nk=DC, k0=0, acc=1, n=S, tiles=TT,
        loads=None, bias=None):
    half = nk // 2

    def whole(p):
        def part(a, b):
            rows = w[(k0 + a) * P:(k0 + b) * P, :].rearrange("(k p) c -> p k c", p=P)
            cols = c0 + p * width
            return (lambda slot: slot[:, a * width:b * width].rearrange("p (k c) -> p k c", k=b - a),
                    rows[:, :, ds(cols, width)])
        return [part(0, half), part(half, nk)]

    r = Fields()
    r.kind, r.src, r.evict, r.on, r.count, r.width, r.nk = kind, src, evict, on, count, width, nk
    r.acc, r.n, r.tiles, r.loads, r.bias = acc, n, tiles, loads or whole, bias
    return r


def grouped_loads(w, nk, outer, inner, pick):
    def loads(p):
        out = []
        for kk in range(nk):
            rows = pick(w[kk * P:(kk + 1) * P, :], p)
            out.append((lambda slot, kk=kk: slot[:, kk * outer * inner:(kk + 1) * outer * inner]
                        .rearrange("p (g c) -> p g c", g=outer), rows))
        return out
    return loads


class Stream:

    def __init__(self, k):
        self.k = k
        self.jobs = []
        self.starts = []
        self.flat = []
        self.group = 0
        self.at = 0

    def add(self, runs):
        self.jobs.append(runs)
        self.starts.append(len(self.flat))
        for r in runs:
            self.flat += [(r, p) for p in range(r.count)]

    def load(self, sp, r, p, slot, uses, number):
        if isinstance(uses, int) and uses == 0:
            for dst, src in r.loads(p):
                sp.dma_start(dst(self.k.ring[:, slot, :]), src).then_inc(self.k.panel_loaded[slot], 16)
        else:
            self.load_panel(sp, r.loads(p), slot, number)

    def load_range(self, sp, a, b):
        while a < b:
            r, p = self.flat[a]
            n = min(r.count - p, b - a)
            if r.kind == "experts":
                self.load_experts(sp, r, a, p, n)
                a += n
                continue
            trips = n // SLOTS if n >= 2 * SLOTS and a >= SLOTS else 0
            if trips:
                with sp.Fori(0, trips) as i:
                    for j in range(SLOTS):
                        self.load(sp, r, i * SLOTS + (p + j), (a + j) % SLOTS, (a + j) // SLOTS + i,
                                  i * SLOTS + (a + j))
            for m in range(trips * SLOTS, n):
                self.load(sp, r, p + m, (a + m) % SLOTS, (a + m) // SLOTS, a + m)
            a += n

    def load_experts(self, sp, r, a, p, n):
        per = r.per_expert
        turns = n // per if p + n == r.count and a >= SLOTS else 0
        if turns:
            with sp.Fori(0, turns) as e:
                for m in range(per):
                    ahead, c = divmod(p + m, per)
                    self.load_panel(sp, r.expert_loads(e + ahead, c), (a + m) % SLOTS, e * per + (a + m))
        for m in range(turns * per, n):
            self.load(sp, r, p + m, (a + m) % SLOTS, (a + m) // SLOTS, a + m)

    def load_panel(self, sp, loads, slot, number):
        k = self.k
        sp.wait_ge(k.panel_used, number - SLOTS + 1)
        for dst, src in loads:
            sp.dma_start(dst(k.ring[:, slot, :]), src).then_inc(k.panel_loaded[slot], 16)

    def ahead(self, sp):
        i = self.at
        nxt = self.starts[i + 1] if i + 1 < len(self.starts) else len(self.flat)
        self.load_range(sp, self.starts[i] + SLOTS, min(nxt + SLOTS, len(self.flat)))

    def each(self, eng, first, group, r, body):
        trips = r.count // SLOTS if r.count >= 2 * SLOTS and r.acc == 1 and group >= SLOTS and first >= SLOTS else 0
        if trips:
            with eng.Fori(0, trips) as i:
                for j in range(SLOTS):
                    a, g = first + j, group + j
                    body(i * SLOTS + j, i * SLOTS + a, a % SLOTS, i + a // SLOTS, g % SLOTS, i + g // SLOTS)
        for p in range(trips * SLOTS, r.count):
            a, g = first + p, group + p // r.acc
            body(p, a, a % SLOTS, a // SLOTS, g % SLOTS, g // SLOTS)

    def stage(self, name, side=None):
        k, nc = self.k, self.k.nc
        runs, first, group = self.jobs[self.at], self.starts[self.at], self.group
        groups = []
        g = group
        for r in runs:
            groups.append(g)
            g += r.count // r.acc
        firsts = []
        a = first
        for r in runs:
            firsts.append(a)
            a += r.count

        with stage(k, name) as st:
            @st.block.sync
            def _(sp):
                self.ahead(sp)

            @st.block.tensor
            def _(pe):
                for r, f, gg in zip(runs, firsts, groups):
                    def body(p, number, slot, uses, bank, before, r=r):
                        pe.wait_ge(k.panel_loaded[slot], (uses + 1) * 32)
                        begins = not isinstance(p, int) or p % r.acc == 0
                        ends = not isinstance(p, int) or p % r.acc == r.acc - 1
                        if begins and (not isinstance(before, int) or before > 0):
                            pe.wait_ge(k.group_read[bank], before)
                        src = r.src(p) if callable(r.src) else r.src
                        w = k.ring[:, slot, 0:r.nk * r.width].rearrange("p (k c) -> p k c", k=r.nk)
                        for o in range(r.width // P if r.kind == "F" else r.tiles):
                            for c in range(r.nk):
                                if r.kind == "F":
                                    at = o * (r.n if r.acc == 1 else 512)
                                    out = k.ps[:, 2 * bank + at // 512, at % 512:at % 512 + r.n]
                                    lhs, rhs = w[:, c, o * P:(o + 1) * P], src[:, c, :]
                                else:
                                    out = k.ps[:, 2 * bank + o, 0:r.width]
                                    lhs, rhs = src[:, c, o * P:(o + 1) * P], w[:, c, :]
                                last = nc.tensor.matmul(out, lhs, rhs, start=(begins and c == 0),
                                                        stop=(ends and c == r.nk - 1 and r.bias is None))
                            if r.bias is not None and ends:
                                last = nc.tensor.matmul(out, k.ones_row[0:1, 0:P], r.bias(p), start=False, stop=True)
                        last.then_inc(k.panel_used, 1)
                    self.each(pe, f, gg, r, body)

            def evictions(eng, which):
                for r, f, gg in zip(runs, firsts, groups):
                    if r.on != which:
                        continue
                    def body(p, number, slot, uses, bank, before, r=r):
                        if isinstance(p, int) and p % r.acc != r.acc - 1:
                            return
                        eng.wait_ge(k.panel_used, number + 1)
                        banks = k.ps[:, 2 * bank:2 * bank + 2, :]
                        q = p if r.acc == 1 else p // r.acc
                        r.evict(nc, banks, q).then_inc(k.group_read[bank], 1)
                    self.each(eng, f, gg, r, body)

            @st.block.scalar
            def _(act):
                evictions(act, "act")

            @st.block.vector
            def _(dve):
                evictions(dve, "dve")

        self.group = g
        self.at += 1


def to_features(dst, c0=0, func=ACT.Copy, chunks=4, bias=None):
    def evict(nc, banks, p):
        flat = banks.rearrange("p b n -> p (b n)")
        if bias is None:
            return nc.scalar.activation(dst[:, ds(p * 4 + c0, chunks), :].rearrange("p c n -> p (c n)"),
                                        flat[:, 0:chunks * dst.shape[2]], func)
        n = dst.shape[2]
        for c in range(chunks):
            last = nc.scalar.activation(dst[:, ds(p * 4 + (c0 + c), 1), :].rearrange("p c n -> p (c n)"),
                                        flat[:, c * n:(c + 1) * n], func, bias=bias(p * 4 + c))
        return last
    return evict


def to_tokens(dst, f0=0, width=512):
    def evict(nc, banks, p):
        return nc.scalar.activation(dst[:, :, ds(p * 512 + f0, width)], banks[:, :, 0:width], ACT.Copy)
    return evict


def add_to_residual(x, alpha=None):
    def evict(nc, banks, p):
        at = x[:, :, ds(p * 512, 512)]
        if alpha is None:
            return nc.vector.tensor_tensor(at, at, banks[:, :, :], ALU.add)
        return nc.vector.scalar_tensor_tensor(at, at, alpha, banks[:, :, :], ALU.mult, ALU.add)
    return evict


def column(k, key, c=0):
    return k.cols[:, COL[key] + c:COL[key] + c + 1]


def normed_features(k, name, x, out, gain=None, shift=None, eps=1e-6):
    nc = k.nc
    with stage(k, name) as st:
        squares_summed, mean_ready = st.sem("squares_summed"), st.sem("mean_ready")
        root_ready, scaled = st.sem("root_ready"), st.sem("scaled")
        transposed, dve_order = st.sem("transposed"), st.sem("dve_order")
        y = k.xn if gain is not None else x

        @st.block.scalar
        def _(act):
            if gain is not None:
                for t in range(TT):
                    last = nc.scalar.activation(k.xn[:, t, :], x[:, t, :], ACT.Square,
                                                accum_out=k.stat[:, t:t + 1])
                last.then_inc(squares_summed, 1)
                act.wait_ge(mean_ready, 1)
                nc.scalar.activation(k.stat[:, 4:6], k.stat[:, 2:4], ACT.Sqrt).then_inc(root_ready, 1)
            for c in (2, 3, 6, 7):
                act.wait_ge(transposed, c // 2 + 1)
                src = k.ps[:, c // 2, (c % 2) * S:(c % 2 + 1) * S]
                if gain is None:
                    nc.scalar.activation(out[:, c, :], src, ACT.Copy)
                else:
                    nc.scalar.activation(out[:, c, :], src, ACT.Identity, scale=gain(c),
                                         bias=shift(c) if shift else 0.0)

        @st.block.vector
        def _(dve):
            o = Order(dve, dve_order)
            if gain is not None:
                dve.wait_ge(squares_summed, 1)
                nc.vector.tensor_scalar(k.stat[:, 2:4], k.stat[:, 0:2], 1.0 / D, eps, ALU.mult,
                                        ALU.add).then_inc(mean_ready, 1)
                dve.wait_ge(root_ready, 1)
                o(nc.vector.reciprocal(k.stat[:, 6:8], k.stat[:, 4:6]))
                for t in range(TT):
                    nc.vector.tensor_scalar(k.xn[:, t, :], x[:, t, :], k.stat[:, 6 + t:7 + t], None,
                                            ALU.mult).then_inc(scaled, 1)
            for c in (0, 1, 4, 5):
                dve.wait_ge(transposed, c // 2 + 1)
                src = k.ps[:, c // 2, (c % 2) * S:(c % 2 + 1) * S]
                if gain is None:
                    nc.vector.tensor_copy(out[:, c, :], src)
                elif shift:
                    nc.vector.tensor_scalar(out[:, c, :], src, gain(c), shift(c), ALU.mult, ALU.add)
                else:
                    nc.vector.tensor_scalar(out[:, c, :], src, gain(c), None, ALU.mult)

        @st.block.tensor
        def _(pe):
            if gain is not None:
                pe.wait_ge(scaled, TT)
            for c in range(DC):
                for t in range(TT):
                    last = nc.tensor.transpose(k.ps[:, c // 2, (c % 2) * S + t * P:(c % 2) * S + (t + 1) * P],
                                               y[:, t, c * P:(c + 1) * P], k.ident[:, :])
                if c % 2:
                    last.then_inc(transposed, 1)


def feature_norm(k, name, x, heads, per, out, tmp, eps, center=False, gain=None, shift=None, gate=None,
                 silu=False):
    nc = k.nc
    n = heads * per
    rows = heads * S
    banks = -(-rows // 512)
    with stage(k, name) as st:
        ones_ready, sums_ready = st.sem("ones_ready"), st.sem("sums_ready")
        centred, squared, squares_ready = st.sem("centred"), st.sem("squared"), st.sem("squares_ready")
        root_ready, dve_order, affine_ready = st.sem("root_ready"), st.sem("dve_order"), st.sem("affine_ready")
        x4 = x.rearrange("p (h g) n -> p h g n", h=heads)

        def sums(first_bank):
            return k.ps[:, first_bank:first_bank + banks, :].rearrange("p b n -> p (b n)")[:, 0:rows]

        @st.block.tensor
        def _(pe):
            pe.wait_ge(ones_ready, 1)

            def total(src, bank):
                for h in range(heads):
                    out_ = k.ps[:, bank + h // 2, (h % 2) * S:(h % 2 + 1) * S]
                    for g in range(per):
                        last = nc.tensor.matmul(out_, k.ones_n[:, :], src[:, h * per + g, :], start=(g == 0),
                                                stop=(g == per - 1))
                return last
            if center:
                total(x, 0).then_inc(sums_ready, 1)
            pe.wait_ge(squared, 1)
            total(tmp, 4).then_inc(squares_ready, 1)

        @st.block.scalar
        def _(act):
            if center:
                act.wait_ge(centred, 1)
            nc.scalar.activation(tmp.rearrange("p c n -> p (c n)"), x.rearrange("p c n -> p (c n)"),
                                 ACT.Square).then_inc(squared, 1)
            act.wait_ge(squares_ready, 1)
            nc.scalar.activation(k.norm_row[:, 0:rows], sums(4), ACT.Sqrt, bias=k.eps(eps)).then_inc(root_ready, 1)
            if silu:
                act.wait_ge(affine_ready, 1)
                nc.scalar.activation(tmp.rearrange("p c n -> p (c n)"), x.rearrange("p c n -> p (c n)"),
                                     ACT.Silu).then_inc(affine_ready, 1)

        @st.block.vector
        def _(dve):
            o = Order(dve, dve_order)
            nc.vector.tensor_scalar(k.ones_n[:, :], k.ones[:, :], 1.0 / (per * P), None,
                                    ALU.mult).then_inc(ones_ready, 1)
            if center:
                dve.wait_ge(sums_ready, 1)
                mean = sums(0).rearrange("p (h n) -> p h n", h=heads).unsqueeze(2).broadcast_to([P, heads, per, S])
                nc.vector.tensor_tensor(x4, x4, mean, ALU.subtract).then_inc(centred, 1)
                dve.wait_ge(centred, 1)
            dve.wait_ge(root_ready, 1)
            o(nc.vector.reciprocal(k.norm_row[:, 0:rows], k.norm_row[:, 0:rows]))
            inv = k.norm_row[:, 0:rows].rearrange("p (h n) -> p h n", h=heads).unsqueeze(2)
            o(nc.vector.tensor_tensor(x4, x4, inv.broadcast_to([P, heads, per, S]), ALU.mult))
            if gain is None:
                if gate is not None:
                    nc.vector.tensor_tensor(out, x, gate, ALU.mult)
                elif out is not x:
                    nc.vector.tensor_copy(out, x)
                return
            for c in range(n):
                dst = x if silu else out
                if shift is not None:
                    last = nc.vector.tensor_scalar(dst[:, c, :], x[:, c, :], gain(c), shift(c), ALU.mult, ALU.add)
                elif gate is not None and not silu:
                    last = nc.vector.scalar_tensor_tensor(dst[:, c, :], x[:, c, :], gain(c), gate[:, c, :],
                                                          ALU.mult, ALU.mult)
                else:
                    last = nc.vector.tensor_scalar(dst[:, c, :], x[:, c, :], gain(c), None, ALU.mult)
            if silu:
                last.then_inc(affine_ready, 1)
                dve.wait_ge(affine_ready, 2)
                nc.vector.tensor_tensor(out, tmp, gate, ALU.mult)


def unit(scores, values, scale, mask=None, n=S, factor=None, floor=False):
    u = Fields()
    u.scores, u.values, u.scale, u.mask, u.n, u.factor, u.floor = scores, values, scale, mask, n, factor, floor
    return u


def attention(k, name, groups, work):
    nc = k.nc
    units = []
    for g, (us, r0, dv, dst, gate) in enumerate(groups):
        for i, u in enumerate(us):
            units.append((u, g, i == 0, i == len(us) - 1))
    n_units = len(units)
    masked = work[:, 0:4, :].rearrange("p (b t) n -> p b t n", b=2)
    probs = work[:, 4:8, :].rearrange("p (b t) n -> p b t n", b=2)
    probs_t = work[:, 8:12, :].rearrange("p (b s) n -> p b (s n)", b=2)

    with stage(k, name) as st:
        scores_ready, neg_max_ready, exp_done = st.sem("scores_ready"), st.sem("neg_max_ready"), st.sem("exp_done")
        probs_ready, transposed, pt_ready = st.sem("probs_ready"), st.sem("transposed"), st.sem("pt_ready")
        values_done, out_read, dve_order = st.sem("values_done"), st.sem("out_read"), st.sem("dve_order")

        def score_bank(s, n):
            return k.ps[:, s % 2, :].rearrange("p (t n) -> p t n", t=TT)[:, :, 0:n]

        def blocks(u):
            return [(b, min(P, u.n - b * P)) for b in range(-(-u.n // P))]

        @st.block.tensor
        def _(pe):
            for s in range(n_units + 2):
                if s < n_units:
                    u = units[s][0]
                    if s >= 2:
                        pe.wait_ge(exp_done, s - 1)
                    for t in range(TT):
                        for i, (q, key) in enumerate(u.scores):
                            last = nc.tensor.matmul(score_bank(s, u.n)[:, t, :], q[:, t * P:(t + 1) * P], key,
                                                    start=(i == 0), stop=(i == len(u.scores) - 1))
                    last.then_inc(scores_ready, 1)
                if 1 <= s <= n_units:
                    m = s - 1
                    u = units[m][0]
                    pe.wait_ge(probs_ready, m + 1)
                    if m >= 2:
                        pe.wait_ge(pt_ready, m - 1)
                    for b, rows in blocks(u):
                        for t in range(TT):
                            last = nc.tensor.transpose(
                                k.ps[0:rows, 2 + m % 2, b * S + t * P:b * S + (t + 1) * P],
                                probs[:, m % 2, t, b * P:b * P + rows], k.ident[:, :])
                    last.then_inc(transposed, 1)
                if s >= 2:
                    m = s - 2
                    u, g, first, _ = units[m]
                    _, r0, dv, _, _ = groups[g]
                    pe.wait_ge(pt_ready, m + 1)
                    if first and g >= 2:
                        pe.wait_ge(out_read, g - 1)
                    for b, rows in blocks(u):
                        last = nc.tensor.matmul(k.ps[r0:r0 + dv, 4 + g % 2, 0:S], u.values(b),
                                                probs_t[0:rows, m % 2, b * S:(b + 1) * S],
                                                start=(first and b == 0),
                                                stop=(units[m][3] and b == blocks(u)[-1][0]))
                    last.then_inc(values_done, 1)

        @st.block.vector
        def _(dve):
            o = Order(dve, dve_order)

            def outputs(m):
                u, g, _, is_last = units[m]
                if is_last and groups[g][4] is not None:
                    _, r0, dv, dst, gate = groups[g]
                    dve.wait_ge(values_done, m + 1)
                    nc.vector.tensor_tensor(dst, k.ps[r0:r0 + dv, 4 + g % 2, 0:S], gate,
                                            ALU.mult).then_inc(out_read, 1)

            for s in range(n_units + 3):
                if s >= 3:
                    outputs(s - 3)
                if s < n_units:
                    u = units[s][0]
                    dve.wait_ge(scores_ready, s + 1)
                    if s >= 2:
                        dve.wait_ge(exp_done, s - 1)
                    src = score_bank(s, u.n)
                    if u.mask is not None:
                        o(nc.vector.tensor_tensor(masked[:, s % 2, :, 0:u.n], src, u.mask, ALU.add))
                        src = masked[:, s % 2, :, 0:u.n]
                    o(nc.vector.tensor_reduce(k.soft[:, s % 2, 0:2], src, AX_X, ALU.max))
                    if u.floor:
                        nc.vector.tensor_scalar(k.soft[:, s % 2, 2:4], k.soft[:, s % 2, 0:2], -1e20, -u.scale,
                                                ALU.max, ALU.mult).then_inc(neg_max_ready, 1)
                    else:
                        nc.vector.tensor_scalar(k.soft[:, s % 2, 2:4], k.soft[:, s % 2, 0:2], -u.scale, None,
                                                ALU.mult).then_inc(neg_max_ready, 1)
                if 1 <= s <= n_units:
                    m = s - 1
                    u = units[m][0]
                    soft = k.soft[:, m % 2, :]
                    dve.wait_ge(exp_done, m + 1)
                    if u.floor:
                        o(nc.vector.tensor_scalar(soft[:, 4:6], soft[:, 4:6], 1e-30, None, ALU.max))
                    o(nc.vector.reciprocal(soft[:, 6:8], soft[:, 4:6]))
                    if u.factor is not None:
                        o(nc.vector.tensor_tensor(soft[:, 6:8], soft[:, 6:8], u.factor, ALU.mult))
                    p = probs[:, m % 2, :, 0:u.n]
                    nc.vector.tensor_tensor(p, p, soft[:, 6:8].unsqueeze(2).broadcast_to([P, TT, u.n]),
                                            ALU.mult).then_inc(probs_ready, 1)

        @st.block.scalar
        def _(act):
            for s in range(n_units + 3):
                if s >= 3:
                    m = s - 3
                    u, g, _, is_last = units[m]
                    if is_last and groups[g][4] is None:
                        _, r0, dv, dst, _ = groups[g]
                        act.wait_ge(values_done, m + 1)
                        nc.scalar.activation(dst, k.ps[r0:r0 + dv, 4 + g % 2, 0:S], ACT.Copy).then_inc(out_read, 1)
                if s < n_units:
                    u = units[s][0]
                    act.wait_ge(neg_max_ready, s + 1)
                    if s >= 2:
                        act.wait_ge(transposed, s - 1)
                        act.wait_ge(probs_ready, s - 1)
                    src = masked[:, s % 2, :, 0:u.n] if u.mask is not None else score_bank(s, u.n)
                    for t in range(TT):
                        last = nc.scalar.activation(probs[:, s % 2, t, 0:u.n], src[:, t, :], ACT.Exp,
                                                    bias=k.soft[:, s % 2, 2 + t:3 + t], scale=u.scale,
                                                    accum_out=k.soft[:, s % 2, 4 + t:5 + t])
                    last.then_inc(exp_done, 1)
                if 1 <= s <= n_units:
                    m = s - 1
                    u = units[m][0]
                    act.wait_ge(transposed, m + 1)
                    if m >= 2:
                        act.wait_ge(values_done, m - 1)
                    rows = min(P, u.n)
                    width = len(blocks(u)) * S
                    nc.scalar.activation(probs_t[0:rows, m % 2, 0:width], k.ps[0:rows, 2 + m % 2, 0:width],
                                         ACT.Copy).then_inc(pt_ready, 1)


def swiglu_run(w_gate_up, w_down, experts, ff):
    gu = ff // 256
    tiles = ff // P
    down = -(-tiles // 4)
    g_rows = w_gate_up.rearrange("e (k p) n -> p (e k) n", p=P)
    d_rows = w_down.rearrange("e (f p) n -> p (e f) n", p=P)

    def expert_loads(e, c):
        if c < gu:
            return [(lambda slot, h=h: slot.rearrange("p (k h c) -> p k h c", k=DC, h=2)[:, :, h, :],
                     g_rows[:, ds(e * DC, DC), h * ff + c * 256:h * ff + (c + 1) * 256]) for h in range(2)]
        f0 = (c - gu) * 4
        rows = min(4, tiles - f0)
        half = rows // 2
        return [(lambda slot, h=h: slot[:, h * half * D:(h + 1) * half * D].rearrange("p (f c) -> p f c", f=half),
                 d_rows[:, ds(e * tiles + (f0 + h * half), half), :]) for h in range(2)]

    per = gu + down
    r = Fields()
    r.kind, r.count, r.per_expert, r.acc = "experts", experts * per, per, 1
    r.expert_loads, r.loads = expert_loads, lambda p: expert_loads(p // per, p % per)
    r.gu, r.down, r.tiles, r.experts = gu, down, tiles, experts
    return r


def swiglu(k, name, x, hT, hidden, gated, weight=None):
    nc, stream = k.nc, k.stream
    r, start = stream.jobs[stream.at][0], stream.starts[stream.at]
    gu, per = r.gu, r.per_expert
    assert r.experts == 1 or (per % SLOTS == 0 and gu % 2 == 0)

    def over_experts(eng, body):
        body(0)
        if r.experts > 1:
            with eng.Fori(1, r.experts) as e:
                body(e)

    def later(e, c=0):
        return not isinstance(e, int) or e > 0 or c > 0

    with stage(k, name) as st:
        silu_ready, hidden_ready, y_added = st.sem("silu_ready"), st.sem("hidden_ready"), st.sem("y_added")

        @st.block.sync
        def _(sp):
            stream.ahead(sp)

        @st.block.tensor
        def _(pe):
            def expert(e):
                for c in range(per):
                    slot = (start + c) % SLOTS
                    pe.wait_ge(k.panel_loaded[slot], (e * (per // SLOTS) + ((start + c) // SLOTS + 1)) * 32)
                    if c < gu:
                        if later(e, c // 2):
                            pe.wait_ge(hidden_ready, e * gu + (c - 1))
                        w = k.ring[:, slot, :].rearrange("p (k h c) -> p k h c", k=DC, h=2)
                        for h in range(2):
                            for f in range(2):
                                for kk in range(DC):
                                    last = nc.tensor.matmul(k.ps[:, 2 * (c % 2) + h, f * S:(f + 1) * S],
                                                            w[:, kk, h, f * P:(f + 1) * P], hT[:, kk, :],
                                                            start=(kk == 0), stop=(kk == DC - 1))
                    else:
                        f0 = (c - gu) * 4
                        if c == gu and later(e):
                            pe.wait_ge(y_added, e)
                        rows = min(4, r.tiles - f0)
                        pe.wait_ge(hidden_ready, e * gu + (f0 + rows) // 2)
                        w = k.ring[:, slot, 0:rows * D].rearrange("p (f c) -> p f c", f=rows)
                        for f in range(rows):
                            for t in range(TT):
                                for h in range(2):
                                    last = nc.tensor.matmul(k.ps[:, 4 + 2 * t + h, :],
                                                            hidden[:, f0 + f, t * P:(t + 1) * P],
                                                            w[:, f, h * 512:(h + 1) * 512],
                                                            start=(f0 + f == 0), stop=(f0 + f == r.tiles - 1))
                    last.then_inc(k.panel_used, 1)
            over_experts(pe, expert)

        @st.block.scalar
        def _(act):
            def expert(e):
                for c in range(gu):
                    act.wait_ge(k.panel_used, e * per + (start + c + 1))
                    if later(e, c // 2):
                        act.wait_ge(hidden_ready, e * gu + (c - 1))
                    nc.scalar.activation(gated[:, c % 2, :], k.ps[:, 2 * (c % 2), :], ACT.Silu).then_inc(silu_ready, 1)
            over_experts(act, expert)

        @st.block.vector
        def _(dve):
            def expert(e):
                for c in range(gu):
                    dve.wait_ge(silu_ready, e * gu + (c + 1))
                    nc.vector.tensor_tensor(hidden[:, 2 * c:2 * c + 2, :].rearrange("p f n -> p (f n)"),
                                            gated[:, c % 2, :], k.ps[:, 2 * (c % 2) + 1, :],
                                            ALU.mult).then_inc(hidden_ready, 1)
                dve.wait_ge(k.panel_used, e * per + (start + per))
                if later(e):
                    dve.wait_ge(y_added, e)
                for t in range(TT):
                    xt = x[:, t, :].rearrange("p (h n) -> p h n", h=2)
                    y = k.ps[:, 4 + 2 * t:6 + 2 * t, :]
                    if weight is None:
                        last = nc.vector.tensor_tensor(xt, xt, y, ALU.add)
                    else:
                        last = nc.vector.scalar_tensor_tensor(xt, y, weight[:, t, ds(e, 1)], xt, ALU.mult, ALU.add)
                last.then_inc(y_added, 1)
            over_experts(dve, expert)

    stream.at += 1


def top_two_weights(k, logits, weights):
    nc = k.nc
    with stage(k, "top_two") as st:
        dve_order, exp_ready, exps_done = st.sem("dve_order"), st.sem("exp_ready"), st.sem("exps_done")
        top = k.small[:, 0:16].rearrange("p (t e) -> p t e", t=TT)
        index = k.small_u[:, 0:16].rearrange("p (t e) -> p t e", t=TT)
        index_f = k.small[:, 16:32].rearrange("p (t e) -> p t e", t=TT)
        w = k.small[:, 32:40].rearrange("p (t e) -> p t e", t=TT)
        picked = k.small[:, 48:56]

        @st.block.vector
        def _(dve):
            o = Order(dve, dve_order)
            for t in range(TT):
                o(nc.vector.max(top[:, t, :], logits[:, t, :]))
                o(nc.vector.max_index(index[:, t, :], top[:, t, :], logits[:, t, :]))
            o(nc.vector.tensor_copy(index_f, index))
            o(nc.vector.tensor_tensor(w[:, :, 0], top[:, :, 1], top[:, :, 0], ALU.subtract))
            o(nc.vector.memset(k.small[:, 40:41], 0.0))
            nc.vector.tensor_copy(w[:, :, 3], w[:, :, 0]).then_inc(exp_ready, 1)
            dve.wait_ge(exps_done, 1)
            o(nc.vector.tensor_scalar(w[:, :, 2], w[:, :, 1], 1.0, None, ALU.add))
            o(nc.vector.reciprocal(w[:, :, 0], w[:, :, 2]))
            o(nc.vector.tensor_tensor(w[:, :, 1], w[:, :, 1], w[:, :, 0], ALU.mult))
            for t in range(TT):
                o(nc.vector.tensor_scalar(weights[:, t, :], k.experts, index_f[:, t, 0:1], w[:, t, 0:1],
                                          ALU.is_equal, ALU.mult))
                o(nc.vector.tensor_scalar(picked, k.experts, index_f[:, t, 1:2], w[:, t, 1:2],
                                          ALU.is_equal, ALU.mult))
                o(nc.vector.tensor_tensor(weights[:, t, :], weights[:, t, :], picked, ALU.add))

        @st.block.scalar
        def _(act):
            act.wait_ge(exp_ready, 1)
            nc.scalar.activation(w[:, :, 1], w[:, :, 3], ACT.Exp).then_inc(exps_done, 1)


def load(k, name, pairs):
    with stage(k, name) as st:
        loaded = st.sem("loaded")

        @st.block.sync
        def _(sp):
            for dst, src in pairs:
                sp.dma_start(dst, src).then_inc(loaded, 16)
            sp.wait_ge(loaded, 16 * len(pairs))


def final_norm(k, x, gain_row, out):
    nc = k.nc
    with stage(k, "final_norm") as st:
        squares_summed, mean_ready = st.sem("squares_summed"), st.sem("mean_ready")
        root_ready, dve_order = st.sem("root_ready"), st.sem("dve_order")

        @st.block.scalar
        def _(act):
            for t in range(TT):
                last = nc.scalar.activation(k.xn[:, t, :], x[:, t, :], ACT.Square, accum_out=k.stat[:, t:t + 1])
            last.then_inc(squares_summed, 1)
            act.wait_ge(mean_ready, 1)
            nc.scalar.activation(k.stat[:, 4:6], k.stat[:, 2:4], ACT.Sqrt).then_inc(root_ready, 1)

        @st.block.vector
        def _(dve):
            o = Order(dve, dve_order)
            dve.wait_ge(squares_summed, 1)
            nc.vector.tensor_scalar(k.stat[:, 2:4], k.stat[:, 0:2], 1.0 / D, 1e-6, ALU.mult,
                                    ALU.add).then_inc(mean_ready, 1)
            dve.wait_ge(root_ready, 1)
            o(nc.vector.reciprocal(k.stat[:, 6:8], k.stat[:, 4:6]))
            for t in range(TT):
                nc.vector.scalar_tensor_tensor(out[:, t, :], x[:, t, :], k.stat[:, 6 + t:7 + t], gain_row,
                                               ALU.mult, ALU.mult)


LAM_INIT = 0.8 - 0.6 * float(np.exp(-0.3 * 0))
HEADS1 = 6
MEM_HEADS = 4


def plan_block1(k, w):
    a = k.area
    v = Fields()
    v.memT, v.km, v.vm = a(0, 8), [a(2048, 2), a(3072, 2)], [a(2560, 2), a(3584, 2)]
    v.cat, v.work = a(4096, 8), a(6144, 12)
    v.qk, v.v_tok, v.qm = a(9216, 12), a(12288, 2, 768), a(13824, 2)
    v.alibi, v.tmp, v.mem_tok = a(14336, 12), a(17408, 6), a(18944, 2, 1024)
    v.rows = a(20992, 5, P)
    v.gated = a(6144, 2, 512)
    v.hidden = a(9216, 28)
    v.q, v.fz, v.i_tok, v.g, v.qm_b = a(9216, 6), a(10752, 2, 768), a(12288, 2, 768), a(13824, 6), a(15360, 2)
    v.log_f, v.kT, v.levels, v.level_masks = a(15872, 2, 768), a(17408, 6), a(18944, 9, P), a(20096, 8, P)
    v.decays, v.qe, v.ke = a(21120, 16, P), a(23168, 14, P), a(24960, 14, P)
    v.masked, v.attn, v.cross = a(26752, 8, P), a(27776, 6, P), a(28544, 2, P)
    v.k_tok, v.tmp_b = a(6144, 2, 768), a(7680, 6)

    s = k.stream
    for i, m in enumerate("ab"):
        kv = w[f"{m}_w_mem_kv"]
        s.add([run("F", kv, 0, v.memT, to_features(v.km[i], chunks=2), width=256),
               run("T", kv, 256, v.memT, to_tokens(v.vm[i], width=256), width=256)])
    s.add([run("F", w["a_w_in"], 0, k.hT, to_features(v.qk), count=3),
           run("T", w["a_w_in"], 1536, k.hT, to_tokens(v.v_tok)),
           run("T", w["a_w_in"], 2048, k.hT, to_tokens(v.v_tok, 512, 256), width=256),
           run("F", w["a_w_in"], 2304, k.hT, to_features(v.qm, chunks=2), width=256)])
    s.add([run("T", w["a_w_out"], 0, v.cat, add_to_residual(k.x), on="dve", count=2)])
    s.add([swiglu_run(w["dense_w_gate_up"], w["dense_w_down"], 1, 2816)])
    wb = w["b_w_in"]
    s.add([run("F", wb, 0, k.hT, to_features(v.q)),
           run("F", wb, 512, k.hT, to_features(v.q, 4, chunks=2), width=256),
           run("T", wb, 768, k.hT, to_tokens(v.fz)), run("T", wb, 1280, k.hT, to_tokens(v.fz, 512, 256), width=256),
           run("T", wb, 1536, k.hT, to_tokens(v.i_tok)),
           run("T", wb, 2048, k.hT, to_tokens(v.i_tok, 512, 256), width=256),
           run("F", wb, 2304, k.hT, to_features(v.g, func=ACT.Silu)),
           run("F", wb, 2816, k.hT, to_features(v.g, 4, ACT.Silu, chunks=2), width=256),
           run("F", wb, 3072, k.hT, to_features(v.qm_b, chunks=2), width=256)])
    s.add([run("T", w["b_w_out"], 0, v.cat, add_to_residual(k.x), on="dve", count=2)])
    s.add([run("T", w["moe_router"], 0, k.hT, to_tokens(k.logits, width=8), width=8)])
    s.add([swiglu_run(w["moe_w_gate_up"], w["moe_w_down"], 8, 3584)])
    return v


def setup(k, w, c, v):
    nc = k.nc
    small = [(k.ident, "ident"), (k.ones, "ones"), (k.upper, "upper"), (k.causal, "causal"),
             (k.pair_rot, "pair_rot"), (k.half_rot, "half_rot"), (k.freq, "freq"), (k.cmp_mask, "cmp_mask"),
             (k.experts, "experts")]
    pieces, r = [], 0
    for name, offset, n in COLUMN_ROWS:
        done = 0
        while done < n:
            m = min(n - done, P - r % P)
            src = w[name].flatten()[offset + done * P:offset + (done + m) * P].rearrange("(n d) -> n d", d=P)
            pieces.append((v.rows[r % P:r % P + m, r // P, :], src))
            r += m
            done += m
    last_rows = N_COLS % P
    lam = k.lam_in
    with stage(k, "setup") as st:
        loaded, rows_loaded, lam_loaded = st.sem("loaded"), st.sem("rows_loaded"), st.sem("lam_loaded")
        zeroed, transposed, order = st.sem("zeroed"), st.sem("transposed"), st.sem("order")
        lam_sums, lam_exps = st.sem("lam_sums"), st.sem("lam_exps")

        @st.block.sync
        def _(sp):
            sp.dma_start(k.x[:, :, :], w["x"].rearrange("(t p) d -> p t d", p=P)).then_inc(loaded, 16)
            sp.dma_start(v.mem_tok, w["mem"].rearrange("(t p) d -> p t d", p=P)).then_inc(loaded, 16)
            for dst, name in small:
                sp.dma_start(dst[:, :], c[name]).then_inc(loaded, 16)
            k.stream.load_range(sp, 0, SLOTS)
            sp.wait_ge(loaded, 16 * (2 + len(small)))

        @st.block.scalar
        def _(act):
            act.wait_ge(zeroed, 1)
            for dst, src in pieces:
                act.dma_start(dst, src).then_inc(rows_loaded, 16)
            for i, name in enumerate(("a_lam_q1", "a_lam_k1", "a_lam_q2", "a_lam_k2")):
                act.dma_start(lam[:, i, :], w[name].flatten().partition_broadcast(P)).then_inc(lam_loaded, 16)
            act.wait_ge(lam_sums, 1)
            nc.scalar.activation(k.small[:, 2:4], k.small[:, 0:2], ACT.Exp).then_inc(lam_exps, 1)

        @st.block.tensor
        def _(pe):
            pe.wait_ge(rows_loaded, 16 * len(pieces))
            pe.wait_ge(loaded, 16 * (2 + len(small)))
            for i in range(5):
                last = nc.tensor.transpose(k.ps[:, i // 4, (i % 4) * P:(i % 4 + 1) * P], v.rows[:, i, :], k.ident[:, :])
            last.then_inc(transposed, 1)

        @st.block.vector
        def _(dve):
            o = Order(dve, order)
            nc.vector.memset(v.rows[:, 4, :], 0.0).then_inc(zeroed, 1)
            o(nc.vector.memset(k.eps_cols[:, 0:1], 1e-6))
            o(nc.vector.memset(k.eps_cols[:, 1:2], 1e-5))
            o(nc.vector.memset(k.ones_row[:, :], 1.0))
            o(nc.vector.memset(k.small[:, :], 0.0))
            dve.wait_ge(lam_loaded, 64)
            for i in range(2):
                o(nc.vector.tensor_tensor(lam[:, 2 * i, :], lam[:, 2 * i, :], lam[:, 2 * i + 1, :], ALU.mult))
                o(nc.vector.tensor_reduce(k.small[:, i:i + 1], lam[:, 2 * i, :], AX_X, ALU.add))
            nc.vector.memset(k.small[:, 4:5], 0.0).then_inc(lam_sums, 1)
            dve.wait_ge(lam_exps, 1)
            o(nc.vector.tensor_tensor(k.neg_lam[:, 0:1], k.small[:, 3:4], k.small[:, 2:3], ALU.subtract))
            o(nc.vector.tensor_scalar(k.neg_lam[:, 0:1], k.neg_lam[:, 0:1], LAM_INIT, None, ALU.subtract))
            o(nc.vector.tensor_copy(k.neg_lam[:, 1:2], k.neg_lam[:, 0:1]))
            dve.wait_ge(transposed, 1)
            o(nc.vector.tensor_copy(k.cols[:, 0:512], k.ps[:, 0, :]))
            o(nc.vector.tensor_copy(k.cols[:, 512:640], k.ps[:, 1, 0:P]))
            at = COL["a_subln"]
            o(nc.vector.tensor_scalar(k.cols[:, at:at + 1], k.cols[:, at:at + 1], 1.0 - LAM_INIT, None, ALU.mult))


def memory_groups(k, qm, km, vm, cat):
    groups = []
    for h in range(MEM_HEADS):
        r = 64 * (h % 2)
        u = unit([(qm[r:r + 64, h // 2, :], km[r:r + 64, h // 2, :])],
                 lambda b, h=h: vm[:, b, h * 64:(h + 1) * 64], 0.125)
        groups.append(([u], r, 64, cat[r:r + 64, 6 + h // 2, :], None))
    return groups


def hgrn_gates(k, v):
    nc = k.nc
    with stage(k, "hgrn_gates") as st:
        act_order, log_ready, keys_ready = st.sem("act_order"), st.sem("log_ready"), st.sem("keys_ready")
        transposed, dve_order = st.sem("transposed"), st.sem("dve_order")
        t1 = v.tmp_b.rearrange("p c n -> p (c n)")
        fz = v.fz.rearrange("p t n -> p (t n)")

        @st.block.scalar
        def _(act):
            o = Order(act, act_order)
            nc.scalar.activation(v.k_tok.rearrange("p t n -> p (t n)"), fz, ACT.Sigmoid,
                                 scale=-1.0).then_inc(keys_ready, 1)
            o(nc.scalar.activation(t1, fz, ACT.Abs))
            o(nc.scalar.activation(t1, t1, ACT.Exp, scale=-1.0))
            nc.scalar.activation(t1, t1, ACT.Ln, bias=1.0).then_inc(log_ready, 1)

        @st.block.tensor
        def _(pe):
            pe.wait_ge(keys_ready, 1)
            for h in range(HEADS1):
                for t in range(TT):
                    last = nc.tensor.transpose(k.ps[:, h // 2, (h % 2) * S + t * P:(h % 2) * S + (t + 1) * P],
                                               v.k_tok[:, t, h * P:(h + 1) * P], k.ident[:, :])
            last.then_inc(transposed, 1)

        @st.block.vector
        def _(dve):
            dve.wait_ge(transposed, 1)
            nc.vector.tensor_copy(v.kT.rearrange("p c n -> p (c n)"),
                                  k.ps[:, 0:3, :].rearrange("p b n -> p (b n)"))
            dve.wait_ge(log_ready, 1)
            nc.vector.scalar_tensor_tensor(v.log_f.rearrange("p t n -> p (t n)"), fz, 0.0, t1, ALU.min,
                                           ALU.subtract)


def hgrn_attention(k, v):
    nc = k.nc
    n = HEADS1 * TT
    with stage(k, "hgrn_attention") as st:
        sums_ready, exp_done, decayed = st.sem("sums_ready"), st.sem("exp_done"), st.sem("decayed")
        scores_done, attn_ready = st.sem("scores_done"), st.sem("attn_ready")
        out_ready, out_read, dve_order = st.sem("out_ready"), st.sem("out_read"), st.sem("dve_order")
        levels = v.levels.rearrange("p l t -> p (l t)")

        def halves(m, x):
            return x[:, (m % 2) * 7:(m % 2) * 7 + 7, :]

        @st.block.tensor
        def _(pe):
            def exponents(m):
                h, t = divmod(m, TT)
                if m >= 2:
                    pe.wait_ge(exp_done, m - 1)
                for b in range(2):
                    last = nc.tensor.matmul(k.ps[:, 2 * (m % 2) + b, :], v.log_f[:, t, h * P:(h + 1) * P],
                                            levels[:, t * P + b * 512:t * P + (b + 1) * 512], start=True, stop=True)
                last.then_inc(sums_ready, 1)

            def outputs(h):
                pe.wait_ge(attn_ready, TT * (h + 1))
                if h >= 1:
                    pe.wait_ge(out_read, h)
                at = (h % 2) * S
                vals = [v.i_tok[:, t, h * P:(h + 1) * P] for t in range(TT)]
                a = v.attn[:, (h % 2) * 3:(h % 2) * 3 + 3, :]
                nc.tensor.matmul(k.ps[:, 7, at:at + P], vals[0], a[:, 0, :], start=True, stop=True)
                nc.tensor.matmul(k.ps[:, 7, at + P:at + S], vals[0], a[:, 2, :], start=True, stop=False)
                nc.tensor.matmul(k.ps[:, 7, at + P:at + S], vals[1], a[:, 1, :], start=False,
                                 stop=True).then_inc(out_ready, 1)

            exponents(0)
            for m in range(n):
                h, t = divmod(m, TT)
                if m + 1 < n:
                    exponents(m + 1)
                pe.wait_ge(decayed, m + 1)
                if m >= 1:
                    pe.wait_ge(attn_ready, m)
                for lv in range(7):
                    nc.tensor.matmul(k.ps[:, 4 + lv // 4, (lv % 4) * P:(lv % 4 + 1) * P], halves(m, v.ke)[:, lv, :],
                                     halves(m, v.qe)[:, lv, :], start=True, stop=True)
                last = nc.tensor.matmul(k.ps[:, 5, 3 * P:4 * P], v.kT[:, h, t * P:(t + 1) * P],
                                        v.q[:, h, t * P:(t + 1) * P], start=True, stop=True)
                if t:
                    last = nc.tensor.matmul(k.ps[:, 6, 0:P], v.cross[:, 0, :], v.cross[:, 1, :], start=True, stop=True)
                last.then_inc(scores_done, 1)
                if t == 0 and h:
                    outputs(h - 1)
            outputs(HEADS1 - 1)

        @st.block.scalar
        def _(act):
            def copy_out(h):
                act.wait_ge(out_ready, h + 1)
                nc.scalar.activation(v.cat[:, h, :], k.ps[:, 7, (h % 2) * S:(h % 2 + 1) * S], ACT.Copy).then_inc(out_read, 1)

            for m in range(n):
                act.wait_ge(sums_ready, m + 1)
                if m >= 2:
                    act.wait_ge(decayed, m - 1)
                nc.scalar.activation(v.decays[:, (m % 2) * 8:(m % 2) * 8 + 8, :].rearrange("p l t -> p (l t)"),
                                     k.ps[:, 2 * (m % 2):2 * (m % 2) + 2, :].rearrange("p b n -> p (b n)"),
                                     ACT.Exp).then_inc(exp_done, 1)
                if m % 2 and m > 2:
                    copy_out((m - 3) // 2)
            copy_out(HEADS1 - 1)

        @st.block.vector
        def _(dve):
            o = Order(dve, dve_order)

            def decay(m):
                h, t = divmod(m, TT)
                dve.wait_ge(exp_done, m + 1)
                if m >= 2:
                    dve.wait_ge(scores_done, m - 1)
                e = v.decays[:, (m % 2) * 8:(m % 2) * 8 + 8, :]
                lv = e[:, 1 - t:8 - t, :]
                q1, k1 = (x[:, h:h + 1, t * P:(t + 1) * P] for x in (v.q, v.kT))
                nc.vector.tensor_tensor(halves(m, v.qe), lv, q1.broadcast_to([P, 7, P]), ALU.mult)
                nc.vector.tensor_tensor(halves(m, v.ke), lv, k1.broadcast_to([P, 7, P]), ALU.mult)
                if t == 0 and m >= 2:
                    dve.wait_ge(scores_done, m)
                if t == 0:
                    nc.vector.tensor_tensor(v.cross[:, 0:1, :], e[:, 0:1, :], k1, ALU.mult).then_inc(decayed, 1)
                else:
                    nc.vector.tensor_tensor(v.cross[:, 1:2, :], e[:, 7:8, :], q1, ALU.mult).then_inc(decayed, 1)

            def mask(m):
                h, t = divmod(m, TT)
                dve.wait_ge(scores_done, m + 1)
                if h >= 2 and t == 0:
                    dve.wait_ge(out_ready, h - 1)
                o(nc.vector.tensor_tensor(v.masked.rearrange("p l t -> p (l t)"),
                                          k.ps[:, 4:6, :].rearrange("p b n -> p (b n)"),
                                          v.level_masks.rearrange("p l t -> p (l t)"), ALU.mult))
                a = v.attn[:, (h % 2) * 3:(h % 2) * 3 + 3, :]
                if t:
                    o(nc.vector.tensor_copy(a[:, 2, :], k.ps[:, 6, 0:P]))
                nc.vector.tensor_reduce(a[:, t, :], v.masked.rearrange("p l t -> p t l"), AX_X,
                                        ALU.add).then_inc(attn_ready, 1)

            decay(0)
            for m in range(n):
                if m + 1 < n:
                    if (m + 1) % TT == 0:
                        mask(m)
                        decay(m + 1)
                    else:
                        decay(m + 1)
                        mask(m)
                else:
                    mask(m)


def block1(k, w, c, v):
    nc, s = k.nc, k.stream
    normed_features(k, "mem_norm_a", v.mem_tok, v.memT, lambda i: column(k, "a_mem_norm", i))
    s.stage("mem_kv_a")
    normed_features(k, "mem_norm_b", v.mem_tok, v.memT, lambda i: column(k, "b_mem_norm", i))
    s.stage("mem_kv_b")
    load(k, "load_alibi", [(v.alibi.rearrange("p c n -> p (c n)"), c["alibi"])])
    normed_features(k, "norm_mix_a", k.x, k.hT, lambda i: column(k, "a_norm_mix", i))
    s.stage("in_a")
    groups = []
    for h in range(HEADS1):
        us = []
        for m in range(2):
            r = 64 * m
            us.append(unit([(v.qk[r:r + 64, h, :], v.qk[r:r + 64, 6 + h, :])],
                           lambda b, h=h: v.v_tok[:, b, h * P:(h + 1) * P], 0.125,
                           mask=v.alibi[:, 2 * h:2 * h + 2, :], factor=k.neg_lam[:, :] if m else None))
        groups.append((us, 0, P, v.cat[:, h, :], None))
    attention(k, "diff_attention", groups + memory_groups(k, v.qm, v.km[0], v.vm[0], v.cat), v.work)
    feature_norm(k, "subln", v.cat[:, 0:6, :], 6, 1, v.cat[:, 0:6, :], v.tmp, 1e-6,
                 gain=lambda i: column(k, "a_subln"))
    s.stage("out_a")
    normed_features(k, "dense_norm", k.x, k.hT, lambda i: column(k, "dense_norm", i))
    swiglu(k, "dense", k.x, k.hT, v.hidden, v.gated)
    normed_features(k, "norm_mix_b", k.x, k.hT, lambda i: column(k, "b_norm_mix", i))
    s.stage("in_b")
    load(k, "load_levels", [(v.levels.rearrange("p c n -> p (c n)"), c["levels"]),
                            (v.level_masks.rearrange("p c n -> p (c n)"), c["level_masks"])])
    hgrn_gates(k, v)
    hgrn_attention(k, v)
    attention(k, "memory_attention_b", memory_groups(k, v.qm_b, v.km[1], v.vm[1], v.cat), v.work)
    feature_norm(k, "out_norm_b", v.cat[:, 0:6, :], 6, 1, v.cat[:, 0:6, :], v.tmp_b, 1e-6,
                 gain=lambda i: column(k, "b_out_norm"), gate=v.g)
    s.stage("out_b")
    normed_features(k, "moe_norm", k.x, k.hT, lambda i: column(k, "moe_norm", i))
    s.stage("router")
    top_two_weights(k, k.logits, k.expert_weights)
    swiglu(k, "experts", k.x, k.hT, v.hidden, v.gated, weight=k.expert_weights)
    load(k, "load_final_norm", [(k.rows[:, 0, :], w["final_norm"].flatten().partition_broadcast(P))])
    final_norm(k, k.x, k.rows[:, 0, :], k.x)


RET_HEADS, RET_DV = 4, 512
MLA_HEADS, MLA_NOPE, MLA_ROPE, MLA_V = 8, 128, 64, 128
MOBA_HEADS, MOBA_DH = 16, 64
DN_ALPHA = 4.0 ** 0.25


def rows_of_eight(w, width=512):
    def loads(p):
        c0, k0 = (p // 3) * width, (p % 3) * 8
        return [(lambda slot, h=h: slot[:, h * 4 * width:(h + 1) * 4 * width].rearrange("p (k c) -> p k c", k=4),
                 w[(k0 + 4 * h) * P:(k0 + 4 * h + 4) * P, c0:c0 + width].rearrange("(k p) c -> p k c", p=P))
                for h in range(2)]
    return loads


def plan_block2(k, w):
    a = k.area
    v = Fields()
    v.rq, v.rk, v.rv, v.rg = a(0, 8), a(2048, 8), a(4096, 2, 2048), a(8192, 16)
    v.squares = a(0, 16)
    v.cat, v.decay = a(12288, 24), a(18432, 8)
    v.angle, v.cos, v.sin = a(20480, 3), a(21248, 3), a(22016, 3)
    v.turned = a(22784, 8)
    v.mq, v.mkv, v.kpe, v.mg = a(24832, 2), a(25344, 2), a(25856, 1), a(26112, 8)
    v.weights = a(28160, 4)
    v.qn, v.kn, v.work = a(0, 8), a(2048, 8), a(4096, 12)
    v.qpe, v.vm, v.qm_squares = a(8192, 4), a(9216, 2, 1024), a(11264, 2)
    v.q2, v.k2, v.v2, v.g2, v.cat2 = a(0, 8), a(2048, 8), a(7168, 2, 1024), a(9216, 8), a(12288, 8)
    s = k.stream
    wi = w["w_in_even_2"]

    def twice(p):
        src = wi[:, 6656:6720].rearrange("(k p) c -> p k c", p=P)
        return [(lambda slot, h=h: slot[:, 0:DC * P].rearrange("p (k c) -> p k c", k=DC)[:, :, h * 64:(h + 1) * 64],
                 src) for h in range(2)]

    s.add([run("F", wi, 0, k.hT, to_features(v.rq), count=2), run("F", wi, 1024, k.hT, to_features(v.rk), count=2),
           run("T", wi, 2048, k.hT, to_tokens(v.rv), count=4),
           run("F", wi, 4096, k.hT, to_features(v.rg, func=ACT.Silu), count=4),
           run("F", wi, 6144, k.hT, to_features(v.mq, chunks=2), width=256),
           run("F", wi, 6400, k.hT, to_features(v.mkv, chunks=2), width=256),
           run("F", wi, 6656, k.hT, to_features(v.kpe, chunks=1), width=P, loads=twice),
           run("F", wi, 6720, k.hT, to_features(v.mg, func=ACT.Silu), count=2)])

    def split(w_, head, lo, hi, heads):
        return grouped_loads(w_, 2, heads, hi - lo, lambda rows, p: rows.rearrange("p (h c) -> p h c", c=head)[
            :, heads * p:heads * (p + 1), lo:hi])

    uq, ukv = w["w_uq_even_2"], w["w_ukv_even_2"]
    s.add([run("F", uq, 0, v.mq, to_features(v.qn), count=2, nk=2, loads=split(uq, 192, 0, 128, 4)),
           run("F", uq, 0, v.mq, to_features(v.qpe), nk=2, loads=split(uq, 192, 128, 192, 8)),
           run("F", ukv, 0, v.mkv, to_features(v.kn), count=2, nk=2, loads=split(ukv, 256, 0, 128, 4)),
           run("T", ukv, 0, v.mkv, to_tokens(v.vm), count=2, nk=2, loads=split(ukv, 256, 128, 256, 4))])
    s.add([run("T", None, 0, lambda p: v.cat[:, (p % 3) * 8:(p % 3) * 8 + 8, :], add_to_residual(k.x, DN_ALPHA),
               on="dve", count=6, acc=3, loads=rows_of_eight(w["w_out_even_2"]))])
    wo = w["w_in_odd_2"]
    s.add([run("F", wo, 0, k.hT, to_features(v.q2), count=2), run("F", wo, 1024, k.hT, to_features(v.k2), count=2),
           run("T", wo, 2048, k.hT, to_tokens(v.v2), count=2),
           run("F", wo, 3072, k.hT, to_features(v.g2, func=ACT.Silu), count=2)])
    s.add([run("T", w["w_out_odd_2"], 0, v.cat2, add_to_residual(k.x, DN_ALPHA), on="dve", count=2)])
    return v


def rotation_tables(k, w, v):
    nc = k.nc
    two_pi = 2.0 * np.pi
    c1 = 6.28125
    c2 = float(np.float32(two_pi - c1))
    c2 = float(np.float32(np.round(c2 * 2 ** 20) / 2 ** 20))
    c3 = float(np.float32(two_pi - c1 - c2))
    magic = 1.5 * 2.0 ** 23
    limit = 3.1415925
    with stage(k, "rotation_tables") as st:
        loaded, order, reduced, done = st.sem("loaded"), st.sem("order"), st.sem("reduced"), st.sem("done")
        flat = lambda x: x.rearrange("p c n -> p (c n)")
        angle, cos, sin = flat(v.angle), flat(v.cos), flat(v.sin)

        @st.block.scalar
        def _(act):
            act.dma_start(k.pos[:, :], w["positions_2"].flatten().partition_broadcast(P)).then_inc(loaded, 16)
            act.wait_ge(reduced, 1)
            nc.scalar.activation(sin, sin, ACT.Sin).then_inc(done, 1)
            nc.scalar.activation(cos, cos, ACT.Sin).then_inc(done, 1)

        @st.block.vector
        def _(dve):
            o = Order(dve, order)
            dve.wait_ge(loaded, 16)
            o(nc.vector.tensor_copy(v.cos[:, 0, :], k.pos[:, :]))
            for j in range(3):
                o(nc.vector.tensor_scalar(v.angle[:, j, :], v.cos[:, 0, :], k.freq[:, j:j + 1], None, ALU.mult))
            o(nc.vector.tensor_scalar(cos, angle, 1.0 / two_pi, None, ALU.mult))
            o(nc.vector.tensor_scalar(cos, cos, magic, None, ALU.add))
            o(nc.vector.tensor_scalar(cos, cos, magic, None, ALU.subtract))
            for part in (c1, c2, c3):
                o(nc.vector.scalar_tensor_tensor(angle, cos, -part, angle, ALU.mult, ALU.add))
            o(nc.vector.tensor_scalar(sin, angle, limit, -limit, ALU.min, ALU.max))
            o(nc.vector.tensor_scalar(cos, angle, np.pi / 2, -two_pi, ALU.is_gt, ALU.mult))
            o(nc.vector.scalar_tensor_tensor(cos, angle, np.pi / 2, cos, ALU.add, ALU.add))
            nc.vector.tensor_scalar(cos, cos, limit, -limit, ALU.min, ALU.max).then_inc(reduced, 1)


def rotate(k, name, pieces, partner, cos, sin, turned):
    nc = k.nc
    j = cos.shape[1]
    with stage(k, name) as st:
        turned_ready, order, piece_done = st.sem("turned_ready"), st.sem("order"), st.sem("piece_done")

        @st.block.tensor
        def _(pe):
            for i, x in enumerate(pieces):
                if i >= 2:
                    pe.wait_ge(piece_done, i - 1)
                for c in range(x.shape[1]):
                    last = nc.tensor.matmul(k.ps[:, 4 * (i % 2) + c // 2, (c % 2) * S:(c % 2 + 1) * S], partner[:, :],
                                            x[:, c, :], start=True, stop=True)
                last.then_inc(turned_ready, 1)

        @st.block.vector
        def _(dve):
            o = Order(dve, order)
            for i, x in enumerate(pieces):
                n = x.shape[1]
                reps = n // j

                def tabled(t):
                    if j == 1:
                        return t.broadcast_to([P, n, S])
                    return t.unsqueeze(1).broadcast_to([P, reps, j, S])

                def grouped(y):
                    return y if j == 1 else y.rearrange("p (a j) n -> p a j n", j=j)
                banks = k.ps[:, 4 * (i % 2):4 * (i % 2) + 4, :].rearrange("p b (h n) -> p (b h) n", h=2)[:, 0:n, :]
                dve.wait_ge(turned_ready, i + 1)
                nc.vector.tensor_tensor(grouped(turned[:, 0:n, :]), grouped(banks), tabled(sin), ALU.mult)
                o(nc.vector.tensor_tensor(grouped(x), grouped(x), tabled(cos), ALU.mult))
                o(nc.vector.tensor_tensor(x, x, turned[:, 0:n, :], ALU.add))
                nc.vector.memset(k.small[:, 63:64], 0.0).then_inc(piece_done, 1)


def retention(k, v):
    nc = k.nc
    with stage(k, "retention") as st:
        scores_ready, decayed = st.sem("scores_ready"), st.sem("decayed")
        out_ready, out_read = st.sem("out_ready"), st.sem("out_read")

        @st.block.tensor
        def _(pe):
            def scores(h):
                if h >= 2:
                    pe.wait_ge(decayed, h - 1)
                for b in range(TT):
                    for c in range(2):
                        last = nc.tensor.matmul(k.ps[:, h % 2, b * S:(b + 1) * S],
                                                v.rk[:, 2 * h + c, b * P:(b + 1) * P], v.rq[:, 2 * h + c, :],
                                                start=(c == 0), stop=(c == 1))
                last.then_inc(scores_ready, 1)

            scores(0)
            for h in range(RET_HEADS):
                if h + 1 < RET_HEADS:
                    scores(h + 1)
                pe.wait_ge(decayed, h + 1)
                if h >= 2:
                    pe.wait_ge(out_read, h - 1)
                for c in range(RET_DV // P):
                    for b in range(TT):
                        last = nc.tensor.matmul(k.ps[:, 4 + 2 * (h % 2) + c // 2, (c % 2) * S:(c % 2 + 1) * S],
                                                v.rv[:, b, h * RET_DV + c * P:h * RET_DV + (c + 1) * P],
                                                v.weights[:, 2 * (h % 2) + b, :], start=(b == 0), stop=(b == 1))
                last.then_inc(out_ready, 1)

        @st.block.vector
        def _(dve):
            for h in range(RET_HEADS):
                dve.wait_ge(scores_ready, h + 1)
                if h >= 2:
                    dve.wait_ge(out_ready, h - 1)
                nc.vector.tensor_tensor(v.weights[:, 2 * (h % 2):2 * (h % 2) + 2, :],
                                        k.ps[:, h % 2, :].rearrange("p (b n) -> p b n", b=2),
                                        v.decay[:, 2 * h:2 * h + 2, :], ALU.mult).then_inc(decayed, 1)

        @st.block.scalar
        def _(act):
            for h in range(RET_HEADS):
                act.wait_ge(out_ready, h + 1)
                nc.scalar.activation(v.cat[:, 4 * h:4 * h + 4, :].rearrange("p c n -> p (c n)"),
                                     k.ps[:, 4 + 2 * (h % 2):6 + 2 * (h % 2), :].rearrange("p b n -> p (b n)"),
                                     ACT.Copy).then_inc(out_read, 1)


def layer_norm_rows(k, name, w_gain, w_bias, x):
    nc = k.nc
    with stage(k, name) as st:
        loaded, order, mean_ready = st.sem("loaded"), st.sem("order"), st.sem("mean_ready")
        squares_summed, variance_ready, root_ready = (st.sem("squares_summed"), st.sem("variance_ready"),
                                                      st.sem("root_ready"))

        @st.block.scalar
        def _(act):
            act.dma_start(k.rows[:, 0, :], w_gain.partition_broadcast(P)).then_inc(loaded, 16)
            act.dma_start(k.rows[:, 1, :], w_bias.partition_broadcast(P)).then_inc(loaded, 16)
            act.wait_ge(mean_ready, 1)
            for t in range(TT):
                last = nc.scalar.activation(k.xn[:, t, :], x[:, t, :], ACT.Square, bias=k.stat[:, 2 + t:3 + t],
                                            accum_out=k.stat[:, 4 + t:5 + t])
            last.then_inc(squares_summed, 1)
            act.wait_ge(variance_ready, 1)
            nc.scalar.activation(k.stat[:, 6:8], k.stat[:, 0:2], ACT.Sqrt).then_inc(root_ready, 1)

        @st.block.vector
        def _(dve):
            o = Order(dve, order)
            o(nc.vector.tensor_reduce(k.stat[:, 0:2], x, AX_X, ALU.add))
            nc.vector.tensor_scalar(k.stat[:, 2:4], k.stat[:, 0:2], -1.0 / D, None, ALU.mult).then_inc(mean_ready, 1)
            dve.wait_ge(mean_ready, 1)
            for t in range(TT):
                o(nc.vector.tensor_scalar(k.hT[:, 4 * t:4 * t + 4, :].rearrange("p c n -> p (c n)"), x[:, t, :],
                                          k.stat[:, 2 + t:3 + t], None, ALU.add))
            dve.wait_ge(squares_summed, 1)
            nc.vector.tensor_scalar(k.stat[:, 0:2], k.stat[:, 4:6], 1.0 / D, 1e-5, ALU.mult,
                                    ALU.add).then_inc(variance_ready, 1)
            dve.wait_ge(root_ready, 1)
            o(nc.vector.reciprocal(k.stat[:, 6:8], k.stat[:, 6:8]))
            dve.wait_ge(loaded, 32)
            for t in range(TT):
                o(nc.vector.scalar_tensor_tensor(x[:, t, :], k.hT[:, 4 * t:4 * t + 4, :].rearrange("p c n -> p (c n)"),
                                                 k.stat[:, 6 + t:7 + t], k.rows[:, 0, :], ALU.mult, ALU.mult))
                o(nc.vector.tensor_tensor(x[:, t, :], x[:, t, :], k.rows[:, 1, :], ALU.add))


def block2(k, w, c, v):
    s = k.stream
    causal = k.causal[:, :].rearrange("p (t n) -> p t n", t=TT)
    normed_features(k, "features_even", k.x, k.hT)
    load(k, "load_decay", [(v.decay.rearrange("p c n -> p (c n)"), c["decay"])])
    rotation_tables(k, w, v)
    s.stage("in_even")
    rotate(k, "rotate_retention", [v.rq, v.rk], k.pair_rot, v.cos[:, 0:2, :], v.sin[:, 0:2, :], v.turned)
    retention(k, v)
    feature_norm(k, "retention_norm", v.cat[:, 0:16, :], RET_HEADS, 4, v.cat[:, 0:16, :], v.squares, 1e-5,
                 center=True, gate=v.rg)
    feature_norm(k, "q_norm", v.mq, 1, 2, v.mq, v.qm_squares, 1e-6, gain=lambda i: column(k, "q_norm_even_2", i))
    feature_norm(k, "kv_norm", v.mkv, 1, 2, v.mkv, v.qm_squares, 1e-6, gain=lambda i: column(k, "kv_norm_even_2", i))
    s.stage("mla_up")
    rotate(k, "rotate_mla", [v.qpe, v.kpe], k.half_rot, v.cos[:, 2:3, :], v.sin[:, 2:3, :], v.turned)
    groups = []
    for h in range(MLA_HEADS):
        r = 64 * (h % 2)
        u = unit([(v.qn[:, h, :], v.kn[:, h, :]), (v.qpe[r:r + 64, h // 2, :], v.kpe[r:r + 64, 0, :])],
                 lambda b, h=h: v.vm[:, b, h * P:(h + 1) * P], (MLA_NOPE + MLA_ROPE) ** -0.5, mask=causal)
        groups.append(([u], 0, P, v.cat[:, 16 + h, :], v.mg[:, h, :]))
    attention(k, "latent_attention", groups, v.work)
    s.stage("out_even")
    layer_norm_rows(k, "layer_norm_even", w["ln_g_2"][0], w["ln_b_2"][0], k.x)
    normed_features(k, "features_odd", k.x, k.hT)
    s.stage("in_odd")
    rotate(k, "rotate_moba", [v.q2, v.k2], k.half_rot, v.cos[:, 2:3, :], v.sin[:, 2:3, :], v.turned)
    groups = []
    for h in range(MOBA_HEADS):
        r = 64 * (h % 2)
        u = unit([(v.q2[r:r + 64, h // 2, :], v.k2[r:r + 64, h // 2, :])],
                 lambda b, h=h: v.v2[:, b, h * MOBA_DH:(h + 1) * MOBA_DH], 0.125, mask=causal)
        groups.append(([u], r, MOBA_DH, v.cat2[r:r + 64, h // 2, :], v.g2[r:r + 64, h // 2, :]))
    attention(k, "block_attention", groups, v.work)
    s.stage("out_odd")
    layer_norm_rows(k, "layer_norm_odd", w["ln_g_2"][1], w["ln_b_2"][1], k.x)


LSTM_HEADS, QK_CONV, CONF_K = 4, 4, 31
NSA_HEADS, NSA_GROUPS, N_CMP = 8, 2, S // 16 - 1


def plan_block3(k, w):
    a = k.area
    v = Fields()
    v.ya, v.yb, v.yc, v.gate = a(0, 8), a(2048, 8), a(4096, 8), a(6144, 1, 1024)
    v.c, v.ada = k.c_cols[:, 0:8].unsqueeze(2), k.c_cols[:, 8:24].unsqueeze(2)
    v.c_all = a(9792, 8, P)
    row = lambda at, n: a(7168 + at, 1, n)[0:1, 0, :]
    v.row_gate, v.row_av, v.row_if = row(0, 1024), row(1024, 1024), row(2048, 8)
    v.row_vs, v.row_vw, v.row_g = row(2056, 256), row(2312, 256), row(2568, 24)
    v.qk_pad, v.qk, v.av = a(9792, 16, S + QK_CONV - 1), a(13936, 16), a(18032, 2, 1024)
    v.ao, v.az, v.i_f = a(20080, 8), a(22128, 8), k.i_f
    v.decays, v.sqk, v.probs_t, v.a_all = a(9792, 8), a(11840, 8), a(24176, 8), a(26224, 8, P)
    v.squares_a = a(9792, 8)
    v.u_pad, v.ba, v.bb = a(9792, 8, S + CONF_K - 1), a(12080, 8), a(14128, 8)
    v.u, v.bz, v.squares_b = a(16176, 8), a(18224, 8), a(20272, 8)
    v.cq, v.ckv, v.ks, v.kw = a(9792, 8), a(11840, 4), a(12864, 2), a(13376, 2)
    v.vs, v.vw, v.cz = a(13888, 2), a(14400, 2), a(14912, 8)
    v.work, v.blocks = a(16960, 12), a(20032, 64, 2 * N_CMP)
    v.w2, v.hidden = a(21952, 4, P), a(22464, 4, 2 * N_CMP)
    v.kc, v.vc = a(22584, 1, 2 * N_CMP), a(22614, 2, P)
    v.g3 = k.g3
    v.mg, v.merged, v.o_tok = a(9792, 24), a(15936, 8), a(17984, 2, 1024)

    s, wi = k.stream, w["w_in_3"]

    def biased(key):
        return lambda c: k.cols[:, ds(COL[key] + c, 1)]

    def F(c0, dst, key, func=ACT.Identity, count=1, chunks=4, width=512):
        return run("F", wi, c0, k.hT, to_features(dst, func=func, chunks=chunks, bias=biased(key)), count=count,
                   width=width)

    def T(c0, dst, row_, count=1, width=512):
        return run("T", wi, c0, k.hT, to_tokens(dst, width=width), count=count, width=width,
                   bias=lambda p: row_[:, p * width:(p + 1) * width])

    def gate_out(nc, banks, p):
        return nc.scalar.activation(v.gate[:, :, ds(p * 512, 512)], banks[:, 0:1, :], ACT.Copy)

    s.add([run("F", w["w_ada_3"], 0, v.c, to_features(v.ada), count=4, n=1),
           run("T", w["w_ada_3"], 2048, v.c_all, gate_out, count=2, tiles=1,
               bias=lambda p: v.row_gate[:, p * 512:(p + 1) * 512])])
    s.add([F(0, v.qk_pad[:, :, QK_CONV - 1:], "qk", count=4), T(2048, v.av, v.row_av, count=2),
           F(3072, v.ao, "ao", ACT.Sigmoid, 2), F(4096, v.az, "az", ACT.Silu, 2),
           T(5120, v.i_f, v.row_if, width=8)])
    s.add([F(5128, v.ba, "ba", count=2), F(6152, v.bb, "bb", ACT.Sigmoid, 2), F(7176, v.bz, "bz", ACT.Silu, 2)])
    s.add([F(8200, v.cq, "cq", count=2), F(9224, v.ckv, "ckc"), F(9736, v.ks, "cks", chunks=2, width=256),
           T(9992, v.vs, v.row_vs, width=256), F(10248, v.kw, "ckw", chunks=2, width=256),
           T(10504, v.vw, v.row_vw, width=256), T(10760, v.g3, v.row_g, width=24),
           F(10784, v.cz, "cz", ACT.Silu, 2)])

    w1 = w["nsa_cmp_w1_3"].rearrange("j k c -> (j k) c")

    def w1_rows(p):
        return [(lambda slot, h=h: slot[:, h * 8 * 256:(h + 1) * 8 * 256].rearrange("p (k c) -> p k c", k=8),
                 w1[(p * 16 + h * 8) * P:(p * 16 + h * 8 + 8) * P, :].rearrange("(k p) c -> p k c", p=P))
                for h in range(2)]

    def gelu_out(nc, banks, q):
        return nc.scalar.activation(v.hidden[:, 2 * q:2 * q + 2, :], banks[:, :, 0:2 * N_CMP], ACT.Gelu_apprx_tanh)

    s.add([run("F", None, 0, lambda p: v.blocks[:, p * 16:(p + 1) * 16, :], gelu_out, count=4, acc=2, n=2 * N_CMP,
               width=256, nk=16, loads=w1_rows)])
    s.add([F(11808, v.mg, "mg", ACT.Sigmoid, count=6)])

    def gated(b):
        def evict(nc, banks, p):
            at = v.mg[:, ds(p * 4 + b * 8, 4), :]
            return nc.vector.tensor_tensor(at, at, banks.rearrange("p b (h n) -> p (b h) n", h=2), ALU.mult)
        return evict
    s.add([run("F", w["w_branch_3"][b], 0, y, gated(b), on="dve", count=2)
           for b, y in enumerate((v.ya, v.yb, v.yc))])
    s.add([run("T", w["w_out_3"], 0, v.merged, to_tokens(v.o_tok), count=2)])
    return v


def load_block3(k, w, v):
    nc = k.nc
    b_in = w["b_in_3"].flatten()
    rows = [(v.row_gate, w["b_ada_3"].flatten()[2048:3072])]
    rows += [(r, b_in[at:at + n]) for r, at, n in ((v.row_av, 2048, 1024), (v.row_if, 5120, 8),
                                                  (v.row_vs, 9992, 256), (v.row_vw, 10504, 256),
                                                  (v.row_g, 10760, 24))]
    with stage(k, "load_block3") as st:
        loaded = st.sem("loaded")

        @st.block.scalar
        def _(act):
            with nc.allow_non_contiguous_dma(reason="1024 values of c, one to a partition and chunk"):
                act.dma_start(k.c_cols[:, 0:8], w["c_3"].flatten().rearrange("(k p) -> p k", p=P)).then_inc(loaded, 16)
            for dst, src in rows:
                act.dma_start(dst, src.unsqueeze(0)).then_inc(loaded, 16)
            act.wait_ge(loaded, 16 * (1 + len(rows)))

        @st.block.vector
        def _(dve):
            dve.wait_ge(loaded, 16 * (1 + len(rows)))
            nc.vector.tensor_copy(v.c_all, v.c.broadcast_to([P, DC, P]))


def modulation(k, v):
    nc = k.nc
    ada = k.c_cols[:, 8:24]
    with stage(k, "modulation") as st:
        order = st.sem("order")

        @st.block.vector
        def _(dve):
            o = Order(dve, order)
            o(nc.vector.tensor_tensor(ada, ada, k.cols[:, COL["shift"]:COL["shift"] + 16], ALU.add))
            o(nc.vector.scalar_tensor_tensor(ada[:, 8:16], ada[:, 8:16], 1.0,
                                             k.cols[:, COL["norm_pre_3"]:COL["norm_pre_3"] + 8], ALU.add, ALU.mult))
            nc.vector.memset(v.qk_pad[:, :, 0:QK_CONV - 1], 0.0)


def causal_conv(k, name, x_pad, out, taps, key, bias=None, silu_bias=None):
    nc = k.nc
    n = out.shape[1]
    with stage(k, name) as st:
        tap_done = st.sem("tap_done")

        @st.block.vector
        def _(dve):
            for tap in range(taps):
                for c in range(n):
                    w = column(k, key, tap * n + c)
                    src = x_pad[:, c, tap:tap + S]
                    if tap == 0:
                        if bias is None:
                            ins = nc.vector.tensor_scalar(out[:, c, :], src, w, None, ALU.mult)
                        else:
                            ins = nc.vector.tensor_scalar(out[:, c, :], src, w, bias(c), ALU.mult, ALU.add)
                    else:
                        dve.wait_ge(tap_done, (tap - 1) * n + c + 1)
                        ins = nc.vector.scalar_tensor_tensor(out[:, c, :], src, w, out[:, c, :], ALU.mult, ALU.add)
                    ins.then_inc(tap_done, 1)

        @st.block.scalar
        def _(act):
            if silu_bias is not None:
                for c in range(n):
                    act.wait_ge(tap_done, (taps - 1) * n + c + 1)
                    nc.scalar.activation(out[:, c, :], out[:, c, :], ACT.Silu, bias=silu_bias(c))


def mlstm(k, v):
    nc = k.nc
    small = k.lstm
    lf, f_sum, a = small[:, 0:8], small[:, 8:16], small[:, 16:24]
    neg_m, neg_stab, den, pos = small[:, 24:32], small[:, 32:40], small[:, 40:48], small[:, 48:56]
    i_gate, f_gate = v.i_f[:, :, 0:4], v.i_f[:, :, 4:8]
    th = lambda x: x.rearrange("p (t h) -> p t h", t=TT)
    with stage(k, "mlstm") as st:
        act_order, dve_order, logs_ready = st.sem("act_order"), st.sem("dve_order"), st.sem("logs_ready")
        lf_ready, sums_ready, a_ready = st.sem("lf_ready"), st.sem("sums_ready"), st.sem("a_ready")
        rows_ready, max_ready, exp_done = st.sem("rows_ready"), st.sem("max_ready"), st.sem("exp_done")
        scores_ready, probs_ready = st.sem("scores_ready"), st.sem("probs_ready")
        transposed, pt_ready, out_ready = st.sem("transposed"), st.sem("pt_ready"), st.sem("out_ready")
        heads = lambda x: x.rearrange("p (h t) n -> p h t n", t=TT)
        banks = lambda b: k.ps[:, b:b + 4, :].rearrange("p b (t n) -> p b t n", t=TT)

        @st.block.scalar
        def _(act):
            o = Order(act, act_order)
            t1 = th(pos)
            o(nc.scalar.activation(t1, f_gate, ACT.Abs))
            o(nc.scalar.activation(t1, t1, ACT.Exp, scale=-1.0))
            nc.scalar.activation(t1, t1, ACT.Ln, bias=1.0).then_inc(logs_ready, 1)
            act.wait_ge(max_ready, 1)
            for i in range(8):
                nc.scalar.activation(v.decays[:, i, :], v.decays[:, i, :], ACT.Exp, bias=neg_m[:, i:i + 1])
            nc.scalar.activation(neg_stab, neg_stab, ACT.Exp).then_inc(exp_done, 1)
            act.wait_ge(transposed, 1)
            nc.scalar.activation(v.probs_t.rearrange("p c n -> p (c n)"),
                                 k.ps[:, 0:4, :].rearrange("p b n -> p (b n)"), ACT.Copy).then_inc(pt_ready, 1)
            act.wait_ge(out_ready, 1)
            nc.scalar.activation(v.ya.rearrange("p c n -> p (c n)"),
                                 k.ps[:, 4:8, :].rearrange("p b n -> p (b n)"), ACT.Copy)

        @st.block.tensor
        def _(pe):
            for h in range(LSTM_HEADS):
                for t in range(TT):
                    for c in range(2):
                        last = nc.tensor.matmul(k.ps[:, 4 + h, t * S:(t + 1) * S],
                                                v.qk[:, 2 * h + c, t * P:(t + 1) * P], v.qk[:, 8 + 2 * h + c, :],
                                                start=(c == 0), stop=(c == 1))
            last.then_inc(scores_ready, 1)
            pe.wait_ge(lf_ready, 1)
            nc.tensor.matmul(k.ps[:, 0, 0:4], k.upper[:, :], lf[:, 0:4], start=True, stop=True)
            nc.tensor.matmul(k.ps[:, 0, 4:8], k.ones[:, :], lf[:, 0:4], start=True, stop=False)
            nc.tensor.matmul(k.ps[:, 0, 4:8], k.upper[:, :], lf[:, 4:8], start=False, stop=True).then_inc(sums_ready, 1)
            pe.wait_ge(a_ready, 1)
            for h in range(LSTM_HEADS):
                for b in range(TT):
                    last = nc.tensor.matmul(k.ps[:, 1 + h // 2, (h % 2) * S + b * P:(h % 2) * S + (b + 1) * P],
                                            v.a_all[:, b * 4 + h, :], k.ident[:, :], start=True, stop=True)
            last.then_inc(rows_ready, 1)
            pe.wait_ge(probs_ready, 1)
            for h in range(LSTM_HEADS):
                for b in range(TT):
                    for t in range(TT):
                        last = nc.tensor.transpose(k.ps[:, h, b * S + t * P:b * S + (t + 1) * P],
                                                   v.sqk[:, 2 * h + t, b * P:(b + 1) * P], k.ident[:, :])
            last.then_inc(transposed, 1)
            pe.wait_ge(pt_ready, 1)
            for h in range(LSTM_HEADS):
                for c in range(2):
                    for b in range(TT):
                        last = nc.tensor.matmul(k.ps[:, 4 + h, c * S:(c + 1) * S],
                                                v.av[:, b, h * 256 + c * P:h * 256 + (c + 1) * P],
                                                v.probs_t[:, 2 * h + b, :], start=(b == 0), stop=(b == 1))
            last.then_inc(out_ready, 1)

        @st.block.vector
        def _(dve):
            o = Order(dve, dve_order)
            o(nc.vector.tensor_tensor(v.ao, v.ao, v.az, ALU.mult))
            dve.wait_ge(logs_ready, 1)
            nc.vector.scalar_tensor_tensor(th(lf), f_gate, 0.0, th(pos), ALU.min, ALU.subtract).then_inc(lf_ready, 1)
            dve.wait_ge(sums_ready, 1)
            o(nc.vector.tensor_copy(f_sum, k.ps[:, 0, 0:8]))
            o(nc.vector.tensor_tensor(th(a), i_gate, th(f_sum), ALU.subtract))
            nc.vector.tensor_copy(v.a_all, a.unsqueeze(2).broadcast_to([P, 8, P])).then_inc(a_ready, 1)
            dve.wait_ge(rows_ready, 1)
            mask = k.causal[:, :].rearrange("p (t n) -> p t n", t=TT)
            for h in range(LSTM_HEADS):
                row = k.ps[:, 1 + h // 2, (h % 2) * S:(h % 2 + 1) * S].unsqueeze(1).broadcast_to([P, TT, S])
                o(nc.vector.tensor_tensor(v.decays[:, 2 * h:2 * h + 2, :], row, mask, ALU.add))
            o(nc.vector.tensor_reduce(neg_m, v.decays, AX_X, ALU.max))
            o(nc.vector.tensor_scalar(neg_m, neg_m, 0.0, -1.0, ALU.max, ALU.mult))
            f_ht = f_sum.rearrange("p (t h) -> p h t", t=TT)
            ht = lambda x: x.rearrange("p (h t) -> p h t", t=TT)
            nc.vector.tensor_tensor(ht(neg_stab), ht(neg_m), f_ht, ALU.subtract).then_inc(max_ready, 1)
            dve.wait_ge(scores_ready, 1)
            dve.wait_ge(exp_done, 1)
            o(nc.vector.scalar_tensor_tensor(v.sqk.rearrange("p c n -> p (c n)"),
                                             k.ps[:, 4:8, :].rearrange("p b n -> p (b n)"), 1.0 / 16,
                                             v.decays.rearrange("p c n -> p (c n)"), ALU.mult, ALU.mult))
            o(nc.vector.tensor_reduce(den, v.sqk, AX_X, ALU.add))
            o(nc.vector.tensor_scalar(pos, den, -1.0, None, ALU.mult))
            o(nc.vector.tensor_tensor(den, den, pos, ALU.max))
            o(nc.vector.tensor_tensor(den, den, neg_stab, ALU.max))
            o(nc.vector.reciprocal(den, den))
            nc.vector.tensor_tensor(v.sqk, v.sqk, den.unsqueeze(2).broadcast_to([P, 8, S]),
                                    ALU.mult).then_inc(probs_ready, 1)


def glu_input(k, v):
    nc = k.nc
    with stage(k, "glu_input") as st:
        @st.block.vector
        def _(dve):
            nc.vector.memset(v.u_pad[:, :, 0:CONF_K - 1], 0.0)
            nc.vector.tensor_tensor(v.u_pad[:, :, CONF_K - 1:], v.ba, v.bb, ALU.mult)


def compression_blocks(k, w, v):
    nc = k.nc
    with stage(k, "compression_blocks") as st:
        loaded = st.sem("loaded")

        @st.block.vector
        def _(dve):
            for j in range(2):
                for g in range(NSA_GROUPS):
                    t = v.ckv[:, 2 * j + g, :].rearrange("p (n l) -> p l n", l=16)
                    pe_ = k.cols[:, COL["pe"] + 32 * j:COL["pe"] + 32 * j + 32].unsqueeze(2)
                    for half in range(2):
                        nc.vector.tensor_tensor(
                            v.blocks[:, 32 * j + 16 * half:32 * j + 16 * half + 16, g * N_CMP:(g + 1) * N_CMP],
                            t[:, :, half:half + N_CMP],
                            pe_[:, 16 * half:16 * half + 16, :].broadcast_to([P, 16, N_CMP]), ALU.add)

        @st.block.scalar
        def _(act):
            act.dma_start(v.w2, w["nsa_cmp_w2_3"].rearrange("j (k p) c -> p (j k) c", p=P)).then_inc(loaded, 16)
            nc.scalar.activation(v.g3, v.g3, ACT.Sigmoid)
            act.wait_ge(loaded, 16)


def compressed_keys(k, v):
    nc = k.nc
    with stage(k, "compressed_keys") as st:
        ready = st.sem("ready")

        @st.block.tensor
        def _(pe):
            for c in range(2):
                last = nc.tensor.matmul(k.ps[:, 0, 0:2 * N_CMP], v.w2[:, c, :], v.hidden[:, c, :], start=(c == 0),
                                        stop=(c == 1))
            last.then_inc(ready, 1)
            for g in range(NSA_GROUPS):
                for c in range(2):
                    last = nc.tensor.matmul(k.ps[0:N_CMP, 1, g * P:(g + 1) * P],
                                            v.hidden[:, 2 + c, g * N_CMP:(g + 1) * N_CMP], v.w2[:, 2 + c, :],
                                            start=(c == 0), stop=(c == 1))
            last.then_inc(ready, 1)

        @st.block.vector
        def _(dve):
            dve.wait_ge(ready, 1)
            nc.vector.tensor_copy(v.kc[:, 0, :], k.ps[:, 0, 0:2 * N_CMP])
            dve.wait_ge(ready, 2)
            nc.vector.tensor_copy(v.vc[0:N_CMP, :, :].rearrange("p g n -> p (g n)"), k.ps[0:N_CMP, 1, 0:2 * P])


def merge(k, v):
    nc = k.nc
    with stage(k, "merge") as st:
        order = st.sem("order")

        @st.block.vector
        def _(dve):
            o = Order(dve, order)
            o(nc.vector.tensor_tensor(v.merged, v.mg[:, 0:8, :], v.mg[:, 8:16, :], ALU.add))
            o(nc.vector.tensor_tensor(v.merged, v.merged, v.mg[:, 16:24, :], ALU.add))


def add_gated(k, v):
    nc = k.nc
    with stage(k, "add_gated") as st:
        order = st.sem("order")

        @st.block.vector
        def _(dve):
            o = Order(dve, order)
            o(nc.vector.tensor_tensor(v.o_tok, v.o_tok, v.gate.broadcast_to([P, TT, D]), ALU.mult))
            o(nc.vector.tensor_tensor(k.x, k.x, v.o_tok, ALU.add))


def block3(k, w, c, v):
    s = k.stream
    load_block3(k, w, v)
    s.stage("ada")
    modulation(k, v)
    normed_features(k, "norm_pre", k.x, k.hT, lambda i: k.c_cols[:, 16 + i:17 + i],
                    lambda i: k.c_cols[:, 8 + i:9 + i])
    s.stage("in_lstm")
    causal_conv(k, "qk_conv", v.qk_pad, v.qk, QK_CONV, "conv", silu_bias=lambda i: column(k, "mlstm_conv_b_3", i))
    mlstm(k, v)
    feature_norm(k, "mlstm_norm", v.ya, LSTM_HEADS, 2, v.ya, v.squares_a, 1e-5, center=True,
                 gain=lambda i: column(k, "mlstm_norm_3", i), gate=v.ao)
    s.stage("in_conv")
    glu_input(k, v)
    causal_conv(k, "conformer_conv", v.u_pad, v.u, CONF_K, "dw", bias=lambda i: column(k, "conf_dw_b_3", i))
    feature_norm(k, "conformer_norm", v.u, 1, 8, v.yb, v.squares_b, 1e-5, center=True, silu=True,
                 gain=lambda i: column(k, "conf_ln_g_3", i), shift=lambda i: column(k, "conf_ln_b_3", i), gate=v.bz)
    s.stage("in_sparse")
    compression_blocks(k, w, v)
    s.stage("compress")
    compressed_keys(k, v)
    causal = k.causal[:, :].rearrange("p (t n) -> p t n", t=TT)
    cmp_mask = k.cmp_mask[:, :].rearrange("p (t n) -> p t n", t=TT)
    groups = []
    for h in range(NSA_HEADS):
        g, q = h // (NSA_HEADS // NSA_GROUPS), v.cq[:, h, :]
        us = [unit([(q, v.kc[:, 0, g * N_CMP:(g + 1) * N_CMP])], lambda b, g=g: v.vc[0:N_CMP, g, :], P ** -0.5,
                   mask=cmp_mask, n=N_CMP, factor=v.g3[:, :, 3 * h], floor=True)]
        for i, (keys, vals) in enumerate(((v.ks, v.vs), (v.kw, v.vw))):
            us.append(unit([(q, keys[:, g, :])], lambda b, g=g, vals=vals: vals[:, b, g * P:(g + 1) * P], P ** -0.5,
                           mask=causal, factor=v.g3[:, :, 3 * h + 1 + i]))
        groups.append((us, 0, P, v.yc[:, h, :], v.cz[:, h, :]))
    attention(k, "sparse_attention", groups, v.work)
    s.stage("merge_gates")
    s.stage("branches")
    merge(k, v)
    s.stage("out_merged")
    load(k, "load_norm_post", [(k.rows[:, 0, :], w["norm_post_3"].flatten().partition_broadcast(P))])
    final_norm(k, v.o_tok, k.rows[:, 0, :], v.o_tok)
    add_gated(k, v)


def build(nc, w, c, out, parts=(1, 2, 3)):
    k = Fields()
    k.nc = nc

    def sb(name, shape, dt=F32):
        return nc.alloc_sbuf_tensor(name, shape, dt)

    k.ring = sb("ring", [P, SLOTS, SLOT])
    k.x_t, k.hT_t, k.xn_t = sb("x_tokens", [P, TT, D]), sb("hT", [P, DC, S]), sb("xn", [P, TT, D])
    k.x, k.hT, k.xn = k.x_t[:, :, :], k.hT_t[:, :, :], k.xn_t[:, :, :]
    arena = sb("arena", [P, 29600])
    k.area = lambda at, chunks, n=S: arena[:, at:at + chunks * n].rearrange("p (c n) -> p c n", c=chunks)
    k.ident, k.ones, k.upper = sb("ident", [P, P]), sb("ones", [P, P]), sb("upper", [P, P])
    k.pair_rot, k.half_rot = sb("pair_rot", [P, P]), sb("half_rot", [P, P])
    k.ones_n, k.causal, k.freq = sb("ones_n", [P, P]), sb("causal", [P, TT * S]), sb("freq", [P, 3])
    k.cmp_mask, k.experts = sb("cmp_mask", [P, TT * 15]), sb("experts", [P, 8])[:, :]
    k.cols, k.norm_row = sb("cols", [P, 640]), sb("norm_row", [P, 8 * S])
    k.rows = k.norm_row[:, :].rearrange("p (r n) -> p r n", r=2)
    k.stat, k.soft = sb("stat", [P, 8]), sb("soft", [P, 2, 8])[:, :, :]
    k.small, k.small_u = sb("small", [P, 64]), sb("small_u", [P, 16], U32)
    k.eps_cols, k.ones_row, k.neg_lam = sb("eps_cols", [P, 2]), sb("ones_row", [1, P]), sb("neg_lam", [P, TT])
    k.eps = lambda e: k.eps_cols[:, 0:1] if e == 1e-6 else k.eps_cols[:, 1:2]
    k.lam_in = k.xn_t[:, 0, 0:256].rearrange("p (i n) -> p i n", i=4)
    k.logits, k.expert_weights = sb("logits", [P, TT, 8])[:, :, :], sb("expert_weights", [P, TT, 8])[:, :, :]
    k.pos = sb("positions", [P, S], I32)
    k.c_cols, k.lstm = sb("c_cols", [P, 24]), sb("lstm", [P, 56])
    k.i_f, k.g3 = sb("i_f", [P, TT, 8])[:, :, :], sb("g3", [P, TT, 24])[:, :, :]
    k.ps = nc.alloc_psum_tensor("ps", [P, 8, 512], F32)
    k.panel_used = nc.alloc_semaphore("panel_used")
    k.panel_loaded = [nc.alloc_semaphore(f"panel_loaded{i}") for i in range(SLOTS)]
    k.group_read = [nc.alloc_semaphore(f"group_read{i}") for i in range(SLOTS)]
    k.stream = Stream(k)

    v1 = plan_block1(k, w)
    v2 = plan_block2(k, w) if 2 in parts else None
    v3 = plan_block3(k, w) if 3 in parts else None
    if 1 not in parts:
        k.stream.jobs, k.stream.starts, k.stream.flat = [], [], []
        v2 = plan_block2(k, w) if 2 in parts else None
        v3 = plan_block3(k, w) if 3 in parts else None
    setup(k, w, c, v1)
    if 1 in parts:
        block1(k, w, c, v1)
    if 2 in parts:
        block2(k, w, c, v2)
    if 3 in parts:
        block3(k, w, c, v3)

    stored = nc.alloc_semaphore("stored")
    with stage(k, "store") as st:
        @st.block.sync
        def _(sp):
            sp.dma_start(out.rearrange("(t p) d -> p t d", p=P), k.x).then_inc(stored, 16)
            sp.wait_ge(stored, 16)


def laid_out(name, a):
    a = np.ascontiguousarray(a)
    if name in ("x", "mem"):
        return a.reshape(S, D)
    if name in ("moe_w_gate_up", "moe_w_down"):
        return a.reshape(a.shape[1:])
    if name.startswith("dense_w"):
        return a
    if a.ndim >= 3:
        return a.reshape(a.shape[1:])
    return a


def kernel(**inputs):
    import concourse.bacc as bacc
    from concourse.bass_utils import run_bass_kernel_spmd

    nc = bacc.Bacc("TRN2", target_bir_lowering=False, num_devices=1)
    arrays, w, c = {}, {}, {}
    for name, a in inputs.items():
        if name == "b_lb_logits":
            continue
        a = laid_out(name, a)
        arrays[f"in_{name}"] = a
        w[name] = nc.dram_tensor(f"in_{name}", a.shape, mybir.dt.from_np(a.dtype), kind="ExternalInput").ap()
    for name, a in constant_arrays().items():
        arrays[f"const_{name}"] = a
        c[name] = nc.dram_tensor(f"const_{name}", a.shape, F32, kind="ExternalInput").ap()
    out = nc.dram_tensor("out", [S, D], F32, kind="ExternalOutput").ap()
    build(nc, w, c, out)
    r = run_bass_kernel_spmd(nc, [arrays], core_ids=[0])
    return r.results[0]["out"].reshape(1, S, D)
```

```python
from contextlib import ExitStack, contextmanager

import numpy as np

import concourse.bass as bass
from concourse import mybir

F32 = mybir.dt.float32
F32R = mybir.dt.float32r
I32 = mybir.dt.int32
U32 = mybir.dt.uint32
ACT = mybir.ActivationFunctionType
ALU = mybir.AluOpType
AX_X = mybir.AxisListType.X
ds = bass.ds

P = 128
S = 256
TT = S // P
D = 1024
DC = D // P
SLOTS = 3
SLOT = 4096
STAGE_SEMS = range(190, 232)
NEG = -1e30


def alibi_slopes(n):
    return 2.0 ** (-8.0 * np.arange(1, n + 1) / n)


def constant_arrays():
    t = np.arange(S)
    c = {}
    c["ident"] = np.eye(P)
    c["upper"] = np.triu(np.ones((P, P)))
    c["ones"] = np.ones((P, P))

    def token_major(m):
        return m.reshape(TT, P, -1).transpose(1, 0, 2)

    causal = np.where(t[None, :] <= t[:, None], 0.0, NEG)
    c["causal"] = token_major(causal)
    allowed = (t[None, :] // 64) <= (t[:, None] // 64)
    dist = np.abs(t[:, None] - t[None, :]).astype(np.float32)
    c["alibi"] = np.stack([token_major(np.where(allowed, -np.float32(s) * dist * 8.0, NEG))
                           for s in alibi_slopes(6)], 1)
    rel = (t[None, :] - t[:, None]).astype(np.float64)
    log_g = np.log(1.0 - 2.0 ** (-5.0 - np.arange(4)))
    c["decay"] = np.stack([token_major(np.where(rel >= 0, np.exp(g * np.maximum(rel, 0)) / 16.0, 0.0))
                           for g in log_g], 1)
    j, tt = np.arange(P)[:, None], np.arange(P)[None, :]
    sums, masks = [np.where(j > tt, 1.0, 0.0)], []
    for half in (64, 32, 16, 8, 4, 2, 1):
        mid = (tt // (2 * half)) * 2 * half + half
        sums.append(np.where(tt >= mid, (j >= mid) & (j <= tt), (j > tt) & (j < mid)))
        s_, t_ = np.arange(P)[:, None], np.arange(P)[None, :]
        masks.append((s_ // (2 * half) == t_ // (2 * half)) & (s_ % (2 * half) < half) & (t_ % (2 * half) >= half))
    sums.append(np.where(j <= tt, 1.0, 0.0))
    masks.append(np.eye(P))
    c["levels"] = np.stack(sums, 1)
    c["level_masks"] = np.stack(masks, 1)
    pair = np.zeros((P, P))
    for i in range(0, P, 2):
        pair[i, i + 1], pair[i + 1, i] = -1.0, 1.0
    half = np.zeros((P, P))
    for b in (0, 64):
        for i in range(32):
            half[b + i, b + 32 + i], half[b + 32 + i, b + i] = -1.0, 1.0
    c["pair_rot"], c["half_rot"] = pair.T, half.T
    lin = np.linspace(0.0, 1.0, P, dtype=np.float32)
    ret = (np.float32(1.0) / (np.float32(10000.0) ** lin)).astype(np.float32)
    ang = (np.float32(1.0) / np.float32(10000.0) ** (np.arange(0, 64, 2, dtype=np.float32) / np.float32(64))
           ).astype(np.float32)
    c["freq"] = np.stack([np.repeat(ret[:64], 2), np.repeat(ret[64:], 2), np.tile(ang, 4)], 1)
    n_cmp = S // 16 - 1
    end = np.arange(n_cmp) * 16 + 31
    c["cmp_mask"] = token_major(np.where(end[None, :] <= t[:, None], 0.0, NEG))
    c["experts"] = np.tile(np.arange(8.0), (P, 1))
    return {k: np.ascontiguousarray(v.reshape(v.shape[0], -1), dtype=np.float32) for k, v in c.items()}


def column_table():
    rows, at = [], {}

    def add(key, name, offset, n):
        at[key] = sum(r[2] for r in rows)
        rows.append((name, offset, n))

    for key, n in (("a_norm_mix", 8), ("a_mem_norm", 8), ("b_norm_mix", 8), ("b_mem_norm", 8), ("dense_norm", 8),
                   ("moe_norm", 8), ("a_subln", 1), ("b_out_norm", 1), ("q_norm_even_2", 2), ("kv_norm_even_2", 2),
                   ("norm_pre_3", 8), ("mlstm_norm_3", 8), ("conf_ln_g_3", 8), ("conf_ln_b_3", 8),
                   ("conf_dw_b_3", 8), ("mlstm_conv_b_3", 16)):
        add(key, key, 0, n)
    add("shift", "b_ada_3", 0, 8)
    add("scale", "b_ada_3", 1024, 8)
    for key, off, n in (("qk", 0, 16), ("ao", 3072, 8), ("az", 4096, 8), ("ba", 5128, 8), ("bb", 6152, 8),
                        ("bz", 7176, 8), ("cq", 8200, 8), ("ckc", 9224, 2), ("cvc", 9480, 2), ("cks", 9736, 2),
                        ("ckw", 10248, 2), ("cz", 10784, 8), ("mg", 11808, 24)):
        add(key, "b_in_3", off, n)
    add("conv", "mlstm_conv_w_3", 0, 64)
    add("pe", "nsa_cmp_pe_3", 0, 64)
    add("dw", "conf_dw_w_3", 0, 248)
    return rows, at


COLUMN_ROWS, COL = column_table()
N_COLS = sum(r[2] for r in COLUMN_ROWS)


class Fields:
    pass


class Order:

    def __init__(self, eng, sem):
        self.eng, self.sem, self.n = eng, sem, 0

    def __call__(self, instruction):
        instruction.then_inc(self.sem, 1)
        self.n += 1
        self.eng.wait_ge(self.sem, self.n)


class Stage:

    def __init__(self, nc, block, stack):
        self.nc, self.block, self.stack, self.n = nc, block, stack, 0

    def sem(self, name):
        s = self.stack.enter_context(self.nc.semaphore(name, num=STAGE_SEMS[self.n]))
        self.n += 1
        return s


@contextmanager
def stage(k, name):
    nc = k.nc
    with ExitStack() as stack:
        with nc.Block(no_gpsimd_drain=True) as block:
            st = Stage(nc, block, stack)
            st.name = name
            yield st
        if st.n:
            nc.all_engine_barrier(sems_to_clear=range(STAGE_SEMS[0], STAGE_SEMS[0] + st.n))


def run(kind, w, c0, src, evict, on="act", count=1, width=512, nk=DC, k0=0, acc=1, n=S, tiles=TT,
        loads=None, bias=None):
    half = nk // 2

    def whole(p):
        def part(a, b):
            rows = w[(k0 + a) * P:(k0 + b) * P, :].rearrange("(k p) c -> p k c", p=P)
            cols = c0 + p * width
            return (lambda slot: slot[:, a * width:b * width].rearrange("p (k c) -> p k c", k=b - a),
                    rows[:, :, ds(cols, width)])
        return [part(0, half), part(half, nk)]

    r = Fields()
    r.kind, r.src, r.evict, r.on, r.count, r.width, r.nk = kind, src, evict, on, count, width, nk
    r.acc, r.n, r.tiles, r.loads, r.bias = acc, n, tiles, loads or whole, bias
    r.split = isinstance(src, tuple)
    r.parts = (2 if width >= 2 * P else 1) if r.split else 0
    r.per_turn = SLOTS
    w_ = width // max(r.parts, 1)
    r.part_view = lambda slot, p, h: slot[:, 0:nk * width].rearrange("p (k c) -> p k c", k=nk)[:, :, h * w_:(h + 1) * w_]
    r.part_shape = lambda p: (nk, w_)
    return r


def grouped_loads(w, nk, outer, inner, pick):
    def loads(p):
        out = []
        for kk in range(nk):
            rows = pick(w[kk * P:(kk + 1) * P, :], p)
            out.append((lambda slot, kk=kk: slot[:, kk * outer * inner:(kk + 1) * outer * inner]
                        .rearrange("p (g c) -> p g c", g=outer), rows))
        return out
    return loads


def nonzero(value):
    return not isinstance(value, int) or value > 0


class Stream:

    def __init__(self, k):
        self.k = k
        self.jobs = []
        self.starts = []
        self.flat = []
        self.groups = self.halves = self.pairs = 0
        self.at = 0

    def add(self, runs):
        self.jobs.append(runs)
        self.starts.append(len(self.flat))
        for r in runs:
            r.first, r.group, r.halves, r.pairs = len(self.flat), self.groups, self.halves, self.pairs
            self.flat += [(r, p) for p in range(r.count)]
            self.groups += r.count // r.acc if r.kind != "experts" else 0
            self.halves += r.count * r.parts
            self.pairs += r.count * (r.parts == 2)

    def place(self, r, i, j):
        m, per = Fields(), r.per_turn
        m.r, m.j, m.i = r, j, i
        m.p = i * per + j
        m.number = i * per + (r.first + j)
        m.slot = (r.first + j) % SLOTS
        m.uses = i * (per // SLOTS) + (r.first + j) // SLOTS
        group = r.group + j // r.acc
        m.bank, m.before = group % SLOTS, i + group // SLOTS
        m.halves = i * (per * r.parts) + (r.halves + j * r.parts)
        m.pairs = i * (per * (r.parts == 2)) + (r.pairs + j * (r.parts == 2))
        return m

    def load(self, sp, r, i, j):
        m = self.place(r, i, j)
        if nonzero(m.uses):
            sp.wait_ge(self.k.panel_used, m.number - (SLOTS - 1))
        for dst, src in (r.loads(m.p) if r.kind != "experts" else r.expert_loads(i + j // r.per_turn, j % r.per_turn)):
            sp.dma_start(dst(self.k.ring[:, m.slot, :]), src).then_inc(self.k.panel_loaded[m.slot], 16)

    def load_range(self, sp, a, b):
        while a < b:
            r, p = self.flat[a]
            n = min(r.count - p, b - a)
            trips = n // r.per_turn if n >= 2 * r.per_turn and a >= SLOTS else 0
            if trips:
                with sp.Fori(0, trips) as i:
                    for j in range(r.per_turn):
                        self.load(sp, r, i, p + j)
            for m in range(trips * r.per_turn, n):
                self.load(sp, r, 0, p + m)
            a += n

    def ahead(self, sp):
        i = self.at
        nxt = self.starts[i + 1] if i + 1 < len(self.starts) else len(self.flat)
        self.load_range(sp, self.starts[i] + SLOTS, min(nxt + SLOTS, len(self.flat)))

    def round_weights(self, act, m):
        k = self.k
        for h in range(m.r.parts):
            if h == 0:
                act.wait_ge(k.panel_loaded[m.slot], (m.uses + 1) * 32)
            if h == 0 and m.r.parts == 2:
                if nonzero(m.pairs):
                    act.wait_ge(k.first_half_used, m.pairs)
            elif nonzero(m.number):
                act.wait_ge(k.panel_used, m.number)
            b = h + 2 - m.r.parts
            src = m.r.part_view(k.ring[:, m.slot, :], m.j, h)
            k.nc.scalar.activation(self.part(k.w_hi, b, m), src, ACT.Copy).then_inc(k.hi_ready, 1)

    def rest_of_weights(self, dve, m):
        k = self.k
        for h in range(m.r.parts):
            dve.wait_ge(k.hi_ready, m.halves + (h + 1))
            b = h + 2 - m.r.parts
            src = m.r.part_view(k.ring[:, m.slot, :], m.j, h)
            k.nc.vector.tensor_tensor(self.part(k.w_lo, b, m), src, self.part(k.w_hi, b, m).bitcast(F32),
                                      ALU.subtract).then_inc(k.lo_ready, 1)

    def part(self, tensor, b, m):
        nk, width = m.r.part_shape(m.j)
        return tensor[:, b, 0:nk * width].rearrange("p (k c) -> p k c", k=nk)

    def each(self, eng, r, body):
        trips = r.count // SLOTS if r.count >= 2 * SLOTS and r.acc == 1 and r.group >= SLOTS else 0
        if trips:
            with eng.Fori(0, trips) as i:
                for j in range(SLOTS):
                    body(self.place(r, i, j))
        for p in range(trips * SLOTS, r.count):
            body(self.place(r, 0, p))

    def each_with_next(self, eng, runs, prepare, body):
        prepare(self.place(runs[0], 0, 0))
        for n, r in enumerate(runs):
            trips = (r.count - 1) // SLOTS if r.count > 2 * SLOTS and r.acc == 1 and r.group >= SLOTS else 0
            if trips:
                with eng.Fori(0, trips) as i:
                    for j in range(SLOTS):
                        prepare(self.place(r, i, j + 1))
                        body(self.place(r, i, j))
            for p in range(trips * SLOTS, r.count):
                if p + 1 < r.count:
                    prepare(self.place(r, 0, p + 1))
                elif n + 1 < len(runs):
                    prepare(self.place(runs[n + 1], 0, 0))
                body(self.place(r, 0, p))

    def products(self, pe, m):
        k, nc, r = self.k, self.k.nc, m.r
        begins, ends = m.j % r.acc == 0, m.j % r.acc == r.acc - 1
        if not r.split:
            pe.wait_ge(k.panel_loaded[m.slot], (m.uses + 1) * 32)
        if begins and nonzero(m.before):
            pe.wait_ge(k.group_read[m.bank], m.before)
        src = r.src(m.p) if callable(r.src) else r.src
        nk, width = r.part_shape(m.j)
        for h in range(max(r.parts, 1)):
            if r.split:
                pe.wait_ge(k.lo_ready, m.halves + (h + 1))
                b = h + 2 - r.parts
                w_hi, w_lo = self.part(k.w_hi, b, m), self.part(k.w_lo, b, m)
                passes = ((w_hi, src[0]), (w_hi, src[1]), (w_lo, src[0])) if r.kind == "F" else \
                    ((w_hi, src[0]), (w_lo, src[0]), (w_hi, src[1]))
            else:
                passes = ((k.ring[:, m.slot, 0:nk * width].rearrange("p (k c) -> p k c", k=nk), src),)
            for o in range(width // P if r.kind == "F" else r.tiles):
                if r.kind == "F":
                    at = (h * (width // P) + o) * (r.n if r.acc == 1 else 512)
                    out = k.ps[:, 2 * m.bank + at // 512, at % 512:at % 512 + r.n]
                else:
                    out = k.ps[:, 2 * m.bank + o, h * width:(h + 1) * width]
                for c in range(nk):
                    for i, (w, x) in enumerate(passes):
                        if r.kind == "F":
                            lhs, rhs = w[:, c, o * P:(o + 1) * P], x[:, c, :]
                        else:
                            lhs, rhs = x[:, c, o * P:(o + 1) * P], w[:, c, :]
                        last = nc.tensor.matmul(out, lhs, rhs, start=(begins and c == 0 and i == 0),
                                                stop=(ends and c == nk - 1 and i == len(passes) - 1
                                                      and r.bias is None))
                if r.bias is not None and ends:
                    row = r.bias(m.p)[:, h * width:(h + 1) * width]
                    last = nc.tensor.matmul(out, k.ones_row[0:1, 0:P], row, start=False, stop=True)
            if h == 0 and r.parts == 2:
                last.then_inc(k.first_half_used, 1)
        last.then_inc(k.panel_used, 1)

    def stage(self, name):
        k, nc, runs = self.k, self.k.nc, self.jobs[self.at]

        def evict(eng, m, which):
            r = m.r
            if r.on == which and m.j % r.acc == r.acc - 1:
                eng.wait_ge(k.panel_used, m.number + 1)
                q = m.p if r.acc == 1 else m.j // r.acc
                r.evict(nc, k.ps[:, 2 * m.bank:2 * m.bank + 2, :], q).then_inc(k.group_read[m.bank], 1)

        with stage(k, name) as st:
            @st.block.sync
            def _(sp):
                self.ahead(sp)

            @st.block.tensor
            def _(pe):
                for r in runs:
                    self.each(pe, r, lambda m: self.products(pe, m))

            @st.block.scalar
            def _(act):
                self.each_with_next(act, runs, lambda m: self.round_weights(act, m),
                                    lambda m: evict(act, m, "act"))

            @st.block.vector
            def _(dve):
                self.each_with_next(dve, runs, lambda m: self.rest_of_weights(dve, m),
                                    lambda m: evict(dve, m, "dve"))

        self.at += 1


def to_features(dst, c0=0, func=ACT.Copy, chunks=4, bias=None):
    def evict(nc, banks, p):
        flat = banks.rearrange("p b n -> p (b n)")
        if bias is None:
            return nc.scalar.activation(dst[:, ds(p * 4 + c0, chunks), :].rearrange("p c n -> p (c n)"),
                                        flat[:, 0:chunks * dst.shape[2]], func)
        n = dst.shape[2]
        for c in range(chunks):
            last = nc.scalar.activation(dst[:, ds(p * 4 + (c0 + c), 1), :].rearrange("p c n -> p (c n)"),
                                        flat[:, c * n:(c + 1) * n], func, bias=bias(p * 4 + c))
        return last
    return evict


def to_tokens(dst, f0=0, width=512):
    def evict(nc, banks, p):
        return nc.scalar.activation(dst[:, :, ds(p * 512 + f0, width)], banks[:, :, 0:width], ACT.Copy)
    return evict


def add_to_residual(x, alpha=None):
    def evict(nc, banks, p):
        at = x[:, :, ds(p * 512, 512)]
        if alpha is None:
            return nc.vector.tensor_tensor(at, at, banks[:, :, :], ALU.add)
        return nc.vector.scalar_tensor_tensor(at, at, alpha, banks[:, :, :], ALU.mult, ALU.add)
    return evict


def column(k, key, c=0):
    return k.cols[:, COL[key] + c:COL[key] + c + 1]


def normed_features(k, name, x, out, gain=None, shift=None, eps=1e-6):
    nc = k.nc
    with stage(k, name) as st:
        squares_summed, mean_ready = st.sem("squares_summed"), st.sem("mean_ready")
        root_ready, scaled = st.sem("root_ready"), st.sem("scaled")
        transposed, dve_order = st.sem("transposed"), st.sem("dve_order")
        high_ready = st.sem("high_ready")
        y = k.xn if gain is not None else x
        split = isinstance(out, tuple)
        high = out[0] if split else out

        def chunk(c):
            return k.ps[:, c // 2, (c % 2) * S:(c % 2 + 1) * S]

        @st.block.scalar
        def _(act):
            if gain is not None:
                for t in range(TT):
                    squares = k.ps[:, 4 + 2 * t:6 + 2 * t, :].rearrange("p b n -> p (b n)")
                    last = nc.scalar.activation(squares, x[:, t, :], ACT.Square, accum_out=k.stat[:, t:t + 1])
                last.then_inc(squares_summed, 1)
                act.wait_ge(mean_ready, 1)
                nc.scalar.activation(k.stat[:, 4:6], k.stat[:, 2:4], ACT.Sqrt).then_inc(root_ready, 1)
            for c in range(DC):
                act.wait_ge(transposed, c // 2 + 1)
                if gain is None:
                    last = nc.scalar.activation(high[:, c, :], chunk(c), ACT.Copy)
                else:
                    last = nc.scalar.activation(high[:, c, :], chunk(c), ACT.Identity, scale=gain(c),
                                                bias=shift(c) if shift else 0.0)
                if c % 2:
                    last.then_inc(high_ready, 1)

        @st.block.vector
        def _(dve):
            o = Order(dve, dve_order)
            if gain is not None:
                dve.wait_ge(squares_summed, 1)
                nc.vector.tensor_scalar(k.stat[:, 2:4], k.stat[:, 0:2], 1.0 / D, eps, ALU.mult,
                                        ALU.add).then_inc(mean_ready, 1)
                dve.wait_ge(root_ready, 1)
                o(nc.vector.reciprocal(k.stat[:, 6:8], k.stat[:, 4:6]))
                for t in range(TT):
                    nc.vector.tensor_scalar(k.xn[:, t, :], x[:, t, :], k.stat[:, 6 + t:7 + t], None,
                                            ALU.mult).then_inc(scaled, 1)
            if not split:
                return
            for c in range(DC):
                dve.wait_ge(high_ready, c // 2 + 1)
                low, hi = out[1][:, c, :], out[0][:, c, :].bitcast(F32)
                if gain is None:
                    nc.vector.tensor_tensor(low, chunk(c), hi, ALU.subtract)
                elif shift is None:
                    nc.vector.scalar_tensor_tensor(low, chunk(c), gain(c), hi, ALU.mult, ALU.subtract)
                else:
                    o(nc.vector.tensor_scalar(chunk(c), chunk(c), gain(c), shift(c), ALU.mult, ALU.add))
                    nc.vector.tensor_tensor(low, chunk(c), hi, ALU.subtract)

        @st.block.tensor
        def _(pe):
            if gain is not None:
                pe.wait_ge(scaled, TT)
            for c in range(DC):
                for t in range(TT):
                    last = nc.tensor.transpose(k.ps[:, c // 2, (c % 2) * S + t * P:(c % 2) * S + (t + 1) * P],
                                               y[:, t, c * P:(c + 1) * P], k.ident[:, :])
                if c % 2:
                    last.then_inc(transposed, 1)


def feature_norm(k, name, x, heads, per, out, tmp, eps, center=False, gain=None, shift=None, gate=None,
                 silu=False):
    nc = k.nc
    n = heads * per
    rows = heads * S
    banks = -(-rows // 512)
    with stage(k, name) as st:
        ones_ready, sums_ready = st.sem("ones_ready"), st.sem("sums_ready")
        centred, squared, squares_ready = st.sem("centred"), st.sem("squared"), st.sem("squares_ready")
        root_ready, dve_order, affine_ready = st.sem("root_ready"), st.sem("dve_order"), st.sem("affine_ready")
        x4 = x.rearrange("p (h g) n -> p h g n", h=heads)

        def sums(first_bank):
            return k.ps[:, first_bank:first_bank + banks, :].rearrange("p b n -> p (b n)")[:, 0:rows]

        @st.block.tensor
        def _(pe):
            pe.wait_ge(ones_ready, 1)

            def total(src, bank):
                for h in range(heads):
                    out_ = k.ps[:, bank + h // 2, (h % 2) * S:(h % 2 + 1) * S]
                    for g in range(per):
                        last = nc.tensor.matmul(out_, k.ones_n[:, :], src[:, h * per + g, :], start=(g == 0),
                                                stop=(g == per - 1))
                return last
            if center:
                total(x, 0).then_inc(sums_ready, 1)
            pe.wait_ge(squared, 1)
            total(tmp, 4).then_inc(squares_ready, 1)

        @st.block.scalar
        def _(act):
            if center:
                act.wait_ge(centred, 1)
            nc.scalar.activation(tmp.rearrange("p c n -> p (c n)"), x.rearrange("p c n -> p (c n)"),
                                 ACT.Square).then_inc(squared, 1)
            act.wait_ge(squares_ready, 1)
            nc.scalar.activation(k.norm_row[:, 0:rows], sums(4), ACT.Sqrt, bias=k.eps(eps)).then_inc(root_ready, 1)
            if silu:
                act.wait_ge(affine_ready, 1)
                nc.scalar.activation(tmp.rearrange("p c n -> p (c n)"), x.rearrange("p c n -> p (c n)"),
                                     ACT.Silu).then_inc(affine_ready, 1)

        @st.block.vector
        def _(dve):
            o = Order(dve, dve_order)
            nc.vector.tensor_scalar(k.ones_n[:, :], k.ones[:, :], 1.0 / (per * P), None,
                                    ALU.mult).then_inc(ones_ready, 1)
            if center:
                dve.wait_ge(sums_ready, 1)
                mean = sums(0).rearrange("p (h n) -> p h n", h=heads).unsqueeze(2).broadcast_to([P, heads, per, S])
                nc.vector.tensor_tensor(x4, x4, mean, ALU.subtract).then_inc(centred, 1)
                dve.wait_ge(centred, 1)
            dve.wait_ge(root_ready, 1)
            o(nc.vector.reciprocal(k.norm_row[:, 0:rows], k.norm_row[:, 0:rows]))
            inv = k.norm_row[:, 0:rows].rearrange("p (h n) -> p h n", h=heads).unsqueeze(2)
            o(nc.vector.tensor_tensor(x4, x4, inv.broadcast_to([P, heads, per, S]), ALU.mult))
            if gain is None:
                if gate is not None:
                    nc.vector.tensor_tensor(out, x, gate, ALU.mult)
                elif out is not x:
                    nc.vector.tensor_copy(out, x)
                return
            for c in range(n):
                dst = x if silu else out
                if shift is not None:
                    last = nc.vector.tensor_scalar(dst[:, c, :], x[:, c, :], gain(c), shift(c), ALU.mult, ALU.add)
                elif gate is not None and not silu:
                    last = nc.vector.scalar_tensor_tensor(dst[:, c, :], x[:, c, :], gain(c), gate[:, c, :],
                                                          ALU.mult, ALU.mult)
                else:
                    last = nc.vector.tensor_scalar(dst[:, c, :], x[:, c, :], gain(c), None, ALU.mult)
            if silu:
                last.then_inc(affine_ready, 1)
                dve.wait_ge(affine_ready, 2)
                nc.vector.tensor_tensor(out, tmp, gate, ALU.mult)


def unit(scores, values, scale, mask=None, n=S, factor=None, floor=False):
    u = Fields()
    u.scores, u.values, u.scale, u.mask, u.n, u.factor, u.floor = scores, values, scale, mask, n, factor, floor
    return u


def attention(k, name, groups, work):
    nc = k.nc
    units = []
    for g, (us, r0, dv, dst, gate) in enumerate(groups):
        for i, u in enumerate(us):
            units.append((u, g, i == 0, i == len(us) - 1))
    n_units = len(units)
    scratch = k.xn.rearrange("p t (c n) -> p (t c) n", n=S)
    masked = scratch[:, 0:4, :].rearrange("p (b t) n -> p b t n", b=2)
    probs = scratch[:, 4:8, :].rearrange("p (b t) n -> p b t n", b=2)
    probs_t = work.rearrange("p (b s) n -> p b (s n)", b=2)

    with stage(k, name) as st:
        scores_ready, neg_max_ready, exp_done = st.sem("scores_ready"), st.sem("neg_max_ready"), st.sem("exp_done")
        probs_ready, transposed, pt_ready = st.sem("probs_ready"), st.sem("transposed"), st.sem("pt_ready")
        values_done, out_read, dve_order = st.sem("values_done"), st.sem("out_read"), st.sem("dve_order")

        def score_bank(s, n):
            return k.ps[:, s % 2, :].rearrange("p (t n) -> p t n", t=TT)[:, :, 0:n]

        def blocks(u):
            return [(b, min(P, u.n - b * P)) for b in range(-(-u.n // P))]

        @st.block.tensor
        def _(pe):
            for s in range(n_units + 2):
                if s < n_units:
                    u = units[s][0]
                    if s >= 2:
                        pe.wait_ge(exp_done, s - 1)
                    for t in range(TT):
                        for i, (q, key) in enumerate(u.scores):
                            last = nc.tensor.matmul(score_bank(s, u.n)[:, t, :], q[:, t * P:(t + 1) * P], key,
                                                    start=(i == 0), stop=(i == len(u.scores) - 1))
                    last.then_inc(scores_ready, 1)
                if 1 <= s <= n_units:
                    m = s - 1
                    u = units[m][0]
                    pe.wait_ge(probs_ready, m + 1)
                    if m >= 2:
                        pe.wait_ge(pt_ready, m - 1)
                    for b, rows in blocks(u):
                        for t in range(TT):
                            last = nc.tensor.transpose(
                                k.ps[0:rows, 2 + m % 2, b * S + t * P:b * S + (t + 1) * P],
                                probs[:, m % 2, t, b * P:b * P + rows], k.ident[:, :])
                    last.then_inc(transposed, 1)
                if s >= 2:
                    m = s - 2
                    u, g, first, _ = units[m]
                    _, r0, dv, _, _ = groups[g]
                    pe.wait_ge(pt_ready, m + 1)
                    if first and g >= 2:
                        pe.wait_ge(out_read, g - 1)
                    for b, rows in blocks(u):
                        last = nc.tensor.matmul(k.ps[r0:r0 + dv, 4 + g % 2, 0:S], u.values(b),
                                                probs_t[0:rows, m % 2, b * S:(b + 1) * S],
                                                start=(first and b == 0),
                                                stop=(units[m][3] and b == blocks(u)[-1][0]))
                    last.then_inc(values_done, 1)

        @st.block.vector
        def _(dve):
            o = Order(dve, dve_order)

            def outputs(m):
                u, g, _, is_last = units[m]
                if is_last and groups[g][4] is not None:
                    _, r0, dv, dst, gate = groups[g]
                    dve.wait_ge(values_done, m + 1)
                    nc.vector.tensor_tensor(dst, k.ps[r0:r0 + dv, 4 + g % 2, 0:S], gate,
                                            ALU.mult).then_inc(out_read, 1)

            for s in range(n_units + 3):
                if s >= 3:
                    outputs(s - 3)
                if s < n_units:
                    u = units[s][0]
                    dve.wait_ge(scores_ready, s + 1)
                    if s >= 2:
                        dve.wait_ge(exp_done, s - 1)
                    src = score_bank(s, u.n)
                    if u.mask is not None:
                        o(nc.vector.tensor_tensor(masked[:, s % 2, :, 0:u.n], src, u.mask, ALU.add))
                        src = masked[:, s % 2, :, 0:u.n]
                    o(nc.vector.tensor_reduce(k.soft[:, s % 2, 0:2], src, AX_X, ALU.max))
                    if u.floor:
                        nc.vector.tensor_scalar(k.soft[:, s % 2, 2:4], k.soft[:, s % 2, 0:2], -1e20, -u.scale,
                                                ALU.max, ALU.mult).then_inc(neg_max_ready, 1)
                    else:
                        nc.vector.tensor_scalar(k.soft[:, s % 2, 2:4], k.soft[:, s % 2, 0:2], -u.scale, None,
                                                ALU.mult).then_inc(neg_max_ready, 1)
                if 1 <= s <= n_units:
                    m = s - 1
                    u = units[m][0]
                    soft = k.soft[:, m % 2, :]
                    dve.wait_ge(exp_done, m + 1)
                    if u.floor:
                        o(nc.vector.tensor_scalar(soft[:, 4:6], soft[:, 4:6], 1e-30, None, ALU.max))
                    o(nc.vector.reciprocal(soft[:, 6:8], soft[:, 4:6]))
                    if u.factor is not None:
                        o(nc.vector.tensor_tensor(soft[:, 6:8], soft[:, 6:8], u.factor, ALU.mult))
                    p = probs[:, m % 2, :, 0:u.n]
                    nc.vector.tensor_tensor(p, p, soft[:, 6:8].unsqueeze(2).broadcast_to([P, TT, u.n]),
                                            ALU.mult).then_inc(probs_ready, 1)

        @st.block.scalar
        def _(act):
            for s in range(n_units + 3):
                if s >= 3:
                    m = s - 3
                    u, g, _, is_last = units[m]
                    if is_last and groups[g][4] is None:
                        _, r0, dv, dst, _ = groups[g]
                        act.wait_ge(values_done, m + 1)
                        nc.scalar.activation(dst, k.ps[r0:r0 + dv, 4 + g % 2, 0:S], ACT.Copy).then_inc(out_read, 1)
                if s < n_units:
                    u = units[s][0]
                    act.wait_ge(neg_max_ready, s + 1)
                    if s >= 2:
                        act.wait_ge(transposed, s - 1)
                        act.wait_ge(probs_ready, s - 1)
                    src = masked[:, s % 2, :, 0:u.n] if u.mask is not None else score_bank(s, u.n)
                    for t in range(TT):
                        last = nc.scalar.activation(probs[:, s % 2, t, 0:u.n], src[:, t, :], ACT.Exp,
                                                    bias=k.soft[:, s % 2, 2 + t:3 + t], scale=u.scale,
                                                    accum_out=k.soft[:, s % 2, 4 + t:5 + t])
                    last.then_inc(exp_done, 1)
                if 1 <= s <= n_units:
                    m = s - 1
                    u = units[m][0]
                    act.wait_ge(transposed, m + 1)
                    if m >= 2:
                        act.wait_ge(values_done, m - 1)
                    rows = min(P, u.n)
                    width = len(blocks(u)) * S
                    nc.scalar.activation(probs_t[0:rows, m % 2, 0:width], k.ps[0:rows, 2 + m % 2, 0:width],
                                         ACT.Copy).then_inc(pt_ready, 1)


def swiglu_run(w_gate_up, w_down, experts, ff):
    gu = ff // 256
    tiles = ff // P
    down = -(-tiles // 4)
    per = gu + down
    g_rows = w_gate_up.rearrange("e (k p) n -> p (e k) n", p=P)
    d_rows = w_down.rearrange("e (f p) n -> p (e f) n", p=P)

    def rows(c):
        return min(4, tiles - (c - gu) * 4)

    def expert_loads(e, c):
        if c < gu:
            return [(lambda slot, h=h: slot.rearrange("p (k h c) -> p k h c", k=DC, h=2)[:, :, h, :],
                     g_rows[:, ds(e * DC, DC), h * ff + c * 256:h * ff + (c + 1) * 256]) for h in range(2)]
        f0, half = (c - gu) * 4, rows(c) // 2
        return [(lambda slot, h=h: slot[:, h * half * D:(h + 1) * half * D].rearrange("p (f c) -> p f c", f=half),
                 d_rows[:, ds(e * tiles + (f0 + h * half), half), :]) for h in range(2)]

    def part_view(slot, j, h):
        c = j % per
        if c < gu:
            return slot.rearrange("p (k h c) -> p k h c", k=DC, h=2)[:, :, h, :]
        return slot[:, 0:rows(c) * D].rearrange("p (f c) -> p f c", f=rows(c))[:, :, h * 512:(h + 1) * 512]

    r = Fields()
    r.kind, r.count, r.per_turn, r.acc, r.parts = "experts", experts * per, per, 1, 2
    r.expert_loads, r.part_view = expert_loads, part_view
    r.part_shape = lambda j: (DC, 256) if j % per < gu else (rows(j % per), 512)
    r.gu, r.tiles, r.experts, r.rows = gu, tiles, experts, rows
    return r


def swiglu(k, name, x, h_in, hidden, gated, raw, weight=None):
    nc, stream = k.nc, k.stream
    r = stream.jobs[stream.at][0]
    gu, per = r.gu, r.per_turn
    assert r.experts == 1 or (per % SLOTS == 0 and gu % 2 == 0)

    def over_experts(eng, body):
        body(0)
        if r.experts > 1:
            with eng.Fori(1, r.experts - 1) as e:
                body(e)
            body(r.experts - 1)

    def later(e, c=0):
        return not isinstance(e, int) or e > 0 or c > 0

    def with_next(e, prepare, panel):
        last = isinstance(e, int) and e == r.experts - 1
        for c in range(per):
            if c + 1 < per or not last:
                prepare(stream.place(r, e, c + 1))
            panel(c)

    with stage(k, name) as st:
        silu_ready, product_ready, hidden_ready = st.sem("silu_ready"), st.sem("product_ready"), st.sem("hidden_ready")
        hidden_high_ready, y_added = st.sem("hidden_high_ready"), st.sem("y_added")

        @st.block.sync
        def _(sp):
            stream.ahead(sp)

        @st.block.tensor
        def _(pe):
            def expert(e):
                for c in range(per):
                    m = stream.place(r, e, c)
                    for h in range(2):
                        pe.wait_ge(k.lo_ready, m.halves + (h + 1))
                        w_hi, w_lo = stream.part(k.w_hi, h, m), stream.part(k.w_lo, h, m)
                        if c < gu:
                            if h == 0 and later(e, c // 2):
                                pe.wait_ge(product_ready, e * gu + (c - 1))
                            passes = ((w_hi, h_in[0]), (w_hi, h_in[1]), (w_lo, h_in[0]))
                            for f in range(2):
                                for kk in range(DC):
                                    for i, (w, src) in enumerate(passes):
                                        last = nc.tensor.matmul(k.ps[:, 2 * (c % 2) + h, f * S:(f + 1) * S],
                                                                w[:, kk, f * P:(f + 1) * P], src[:, kk, :],
                                                                start=(kk == 0 and i == 0),
                                                                stop=(kk == DC - 1 and i == 2))
                        else:
                            f0, rows = (c - gu) * 4, r.rows(c)
                            if h == 0:
                                if c == gu and later(e):
                                    pe.wait_ge(y_added, e)
                                pe.wait_ge(hidden_ready, e * gu + (f0 + rows) // 2)
                            passes = ((hidden[0], w_hi), (hidden[0], w_lo), (hidden[1], w_hi))
                            for f in range(rows):
                                for t in range(TT):
                                    for i, (src, w) in enumerate(passes):
                                        last = nc.tensor.matmul(k.ps[:, 4 + 2 * t + h, :],
                                                                src[:, f0 + f, t * P:(t + 1) * P], w[:, f, :],
                                                                start=(f0 + f == 0 and i == 0),
                                                                stop=(f0 + f == r.tiles - 1 and i == 2))
                        last.then_inc(k.first_half_used if h == 0 else k.panel_used, 1)
            over_experts(pe, expert)

        @st.block.scalar
        def _(act):
            def expert(e):
                def panel(c):
                    if c < gu:
                        act.wait_ge(k.panel_used, e * per + (r.first + c + 1))
                        if later(e, c // 2):
                            act.wait_ge(product_ready, e * gu + (c - 1))
                        nc.scalar.activation(gated[:, c % 2, :], k.ps[:, 2 * (c % 2), :],
                                             ACT.Silu).then_inc(silu_ready, 1)
                with_next(e, lambda m: stream.round_weights(act, m), panel)
            stream.round_weights(act, stream.place(r, 0, 0))
            over_experts(act, expert)

        @st.block.vector
        def _(dve):
            def expert(e):
                def panel(c):
                    if c < gu:
                        tile = lambda t: t[:, 2 * c:2 * c + 2, :].rearrange("p f n -> p (f n)")
                        dve.wait_ge(silu_ready, e * gu + (c + 1))
                        if later(e, c // 2):
                            dve.wait_ge(hidden_ready, e * gu + (c - 1))
                        nc.vector.tensor_tensor(raw[:, c % 2, :], gated[:, c % 2, :], k.ps[:, 2 * (c % 2) + 1, :],
                                                ALU.mult).then_inc(product_ready, 1)
                        dve.wait_ge(product_ready, e * gu + (c + 1))
                        nc.vector.tensor_copy(tile(hidden[0]), raw[:, c % 2, :]).then_inc(hidden_high_ready, 1)
                        dve.wait_ge(hidden_high_ready, e * gu + (c + 1))
                        nc.vector.tensor_tensor(tile(hidden[1]), raw[:, c % 2, :], tile(hidden[0]).bitcast(F32),
                                                ALU.subtract).then_inc(hidden_ready, 1)
                with_next(e, lambda m: stream.rest_of_weights(dve, m), panel)
                dve.wait_ge(k.panel_used, e * per + (r.first + per))
                if later(e):
                    dve.wait_ge(y_added, e)
                for t in range(TT):
                    xt = x[:, t, :].rearrange("p (h n) -> p h n", h=2)
                    y = k.ps[:, 4 + 2 * t:6 + 2 * t, :]
                    if weight is None:
                        last = nc.vector.tensor_tensor(xt, xt, y, ALU.add)
                    else:
                        last = nc.vector.scalar_tensor_tensor(xt, y, weight[:, t, ds(e, 1)], xt, ALU.mult, ALU.add)
                last.then_inc(y_added, 1)
            stream.rest_of_weights(dve, stream.place(r, 0, 0))
            over_experts(dve, expert)

    stream.at += 1


def top_two_weights(k, logits, weights):
    nc = k.nc
    with stage(k, "top_two") as st:
        dve_order, exp_ready, exps_done = st.sem("dve_order"), st.sem("exp_ready"), st.sem("exps_done")
        top = k.small[:, 0:16].rearrange("p (t e) -> p t e", t=TT)
        index = k.small_u[:, 0:16].rearrange("p (t e) -> p t e", t=TT)
        index_f = k.small[:, 16:32].rearrange("p (t e) -> p t e", t=TT)
        w = k.small[:, 32:40].rearrange("p (t e) -> p t e", t=TT)
        picked = k.small[:, 48:56]

        @st.block.vector
        def _(dve):
            o = Order(dve, dve_order)
            for t in range(TT):
                o(nc.vector.max(top[:, t, :], logits[:, t, :]))
                o(nc.vector.max_index(index[:, t, :], top[:, t, :], logits[:, t, :]))
            o(nc.vector.tensor_copy(index_f, index))
            o(nc.vector.tensor_tensor(w[:, :, 0], top[:, :, 1], top[:, :, 0], ALU.subtract))
            o(nc.vector.memset(k.small[:, 40:41], 0.0))
            nc.vector.tensor_copy(w[:, :, 3], w[:, :, 0]).then_inc(exp_ready, 1)
            dve.wait_ge(exps_done, 1)
            o(nc.vector.tensor_scalar(w[:, :, 2], w[:, :, 1], 1.0, None, ALU.add))
            o(nc.vector.reciprocal(w[:, :, 0], w[:, :, 2]))
            o(nc.vector.tensor_tensor(w[:, :, 1], w[:, :, 1], w[:, :, 0], ALU.mult))
            for t in range(TT):
                o(nc.vector.tensor_scalar(weights[:, t, :], k.experts, index_f[:, t, 0:1], w[:, t, 0:1],
                                          ALU.is_equal, ALU.mult))
                o(nc.vector.tensor_scalar(picked, k.experts, index_f[:, t, 1:2], w[:, t, 1:2],
                                          ALU.is_equal, ALU.mult))
                o(nc.vector.tensor_tensor(weights[:, t, :], weights[:, t, :], picked, ALU.add))

        @st.block.scalar
        def _(act):
            act.wait_ge(exp_ready, 1)
            nc.scalar.activation(w[:, :, 1], w[:, :, 3], ACT.Exp).then_inc(exps_done, 1)


def load(k, name, pairs):
    with stage(k, name) as st:
        loaded = st.sem("loaded")

        @st.block.sync
        def _(sp):
            for dst, src in pairs:
                sp.dma_start(dst, src).then_inc(loaded, 16)
            sp.wait_ge(loaded, 16 * len(pairs))


def final_norm(k, x, gain_row, out):
    nc = k.nc
    with stage(k, "final_norm") as st:
        squares_summed, mean_ready = st.sem("squares_summed"), st.sem("mean_ready")
        root_ready, dve_order = st.sem("root_ready"), st.sem("dve_order")

        @st.block.scalar
        def _(act):
            for t in range(TT):
                squares = k.ps[:, 2 * t:2 * t + 2, :].rearrange("p b n -> p (b n)")
                last = nc.scalar.activation(squares, x[:, t, :], ACT.Square, accum_out=k.stat[:, t:t + 1])
            last.then_inc(squares_summed, 1)
            act.wait_ge(mean_ready, 1)
            nc.scalar.activation(k.stat[:, 4:6], k.stat[:, 2:4], ACT.Sqrt).then_inc(root_ready, 1)

        @st.block.vector
        def _(dve):
            o = Order(dve, dve_order)
            dve.wait_ge(squares_summed, 1)
            nc.vector.tensor_scalar(k.stat[:, 2:4], k.stat[:, 0:2], 1.0 / D, 1e-6, ALU.mult,
                                    ALU.add).then_inc(mean_ready, 1)
            dve.wait_ge(root_ready, 1)
            o(nc.vector.reciprocal(k.stat[:, 6:8], k.stat[:, 4:6]))
            for t in range(TT):
                nc.vector.scalar_tensor_tensor(out[:, t, :], x[:, t, :], k.stat[:, 6 + t:7 + t], gain_row,
                                               ALU.mult, ALU.mult)


LAM_INIT = 0.8 - 0.6 * float(np.exp(-0.3 * 0))
HEADS1 = 6
MEM_HEADS = 4


def plan_block1(k, w):
    a = k.area
    v = Fields()
    v.km, v.vm, v.cat = [a(0, 2), a(1024, 2)], [a(512, 2), a(1536, 2)], a(2048, 8)
    v.memT, v.mem_tok = a(4096, 8), a(6144, 2, 1024)
    v.qk, v.v_tok, v.qm = a(4096, 12), a(7168, 2, 768), a(8704, 2)
    v.alibi, v.work, v.tmp, v.rows = a(9216, 12), a(12288, 4), a(13312, 6), a(14848, 5, P)
    v.dense_hidden = (k.pair_part("dense_hidden_hi", 4096, 22), k.pair_part("dense_hidden_lo", 9728, 22))
    v.dense_gated, v.dense_raw = a(15360, 2, 512), a(16384, 2, 512)
    v.q, v.fz, v.i_tok, v.g = a(4096, 6), a(5632, 2, 768), a(7168, 2, 768), a(8704, 6)
    v.log_f, v.kT, v.qm_b = v.fz, a(10240, 6), a(11776, 2)
    v.levels, v.level_masks, v.decays = a(12288, 9, P), a(13440, 8, P), a(14464, 16, P)
    v.qe, v.ke, v.attn, v.cross = a(16512, 14, P), a(18304, 14, P), a(20096, 6, P), a(20864, 2, P)
    v.k_tok, v.tmp_b, v.work_b = a(14464, 2, 768), a(16000, 6), a(17536, 4)
    v.hidden = (k.pair_part("hidden_hi", 0, 28), k.pair_part("hidden_lo", 7168, 28))
    v.gated, v.raw = a(14336, 2, 512), a(15360, 2, 512)

    s = k.stream
    for i, m in enumerate("ab"):
        kv = w[f"{m}_w_mem_kv"]
        s.add([run("F", kv, 0, v.memT, to_features(v.km[i], chunks=2), width=256),
               run("T", kv, 256, v.memT, to_tokens(v.vm[i], width=256), width=256)])
    s.add([run("F", w["a_w_in"], 0, k.h, to_features(v.qk), count=3),
           run("T", w["a_w_in"], 1536, k.h, to_tokens(v.v_tok)),
           run("T", w["a_w_in"], 2048, k.h, to_tokens(v.v_tok, 512, 256), width=256),
           run("F", w["a_w_in"], 2304, k.h, to_features(v.qm, chunks=2), width=256)])
    s.add([run("T", w["a_w_out"], 0, v.cat, add_to_residual(k.x), on="dve", count=2)])
    s.add([swiglu_run(w["dense_w_gate_up"], w["dense_w_down"], 1, 2816)])
    wb = w["b_w_in"]
    s.add([run("F", wb, 0, k.h, to_features(v.q)),
           run("F", wb, 512, k.h, to_features(v.q, 4, chunks=2), width=256),
           run("T", wb, 768, k.h, to_tokens(v.fz)), run("T", wb, 1280, k.h, to_tokens(v.fz, 512, 256), width=256),
           run("T", wb, 1536, k.h, to_tokens(v.i_tok)),
           run("T", wb, 2048, k.h, to_tokens(v.i_tok, 512, 256), width=256),
           run("F", wb, 2304, k.h, to_features(v.g, func=ACT.Silu)),
           run("F", wb, 2816, k.h, to_features(v.g, 4, ACT.Silu, chunks=2), width=256),
           run("F", wb, 3072, k.h, to_features(v.qm_b, chunks=2), width=256)])
    s.add([run("T", w["b_w_out"], 0, v.cat, add_to_residual(k.x), on="dve", count=2)])
    s.add([run("T", w["moe_router"], 0, k.h, to_tokens(k.logits, width=8), width=8)])
    s.add([swiglu_run(w["moe_w_gate_up"], w["moe_w_down"], 8, 3584)])
    return v


def setup(k, w, c, v):
    nc = k.nc
    small = [(k.ident, "ident"), (k.ones, "ones"), (k.upper, "upper"), (k.causal, "causal"),
             (k.pair_rot, "pair_rot"), (k.half_rot, "half_rot"), (k.freq, "freq"), (k.cmp_mask, "cmp_mask"),
             (k.experts, "experts")]
    pieces, r = [], 0
    for name, offset, n in COLUMN_ROWS:
        done = 0
        while done < n:
            m = min(n - done, P - r % P)
            src = w[name].flatten()[offset + done * P:offset + (done + m) * P].rearrange("(n d) -> n d", d=P)
            pieces.append((v.rows[r % P:r % P + m, r // P, :], src))
            r += m
            done += m
    last_rows = N_COLS % P
    lam = k.lam_in
    with stage(k, "setup") as st:
        loaded, rows_loaded, lam_loaded = st.sem("loaded"), st.sem("rows_loaded"), st.sem("lam_loaded")
        zeroed, transposed, order = st.sem("zeroed"), st.sem("transposed"), st.sem("order")
        lam_sums, lam_exps = st.sem("lam_sums"), st.sem("lam_exps")

        @st.block.sync
        def _(sp):
            sp.dma_start(k.x[:, :, :], w["x"].rearrange("(t p) d -> p t d", p=P)).then_inc(loaded, 16)
            sp.dma_start(v.mem_tok, w["mem"].rearrange("(t p) d -> p t d", p=P)).then_inc(loaded, 16)
            for dst, name in small:
                sp.dma_start(dst[:, :], c[name]).then_inc(loaded, 16)
            k.stream.load_range(sp, 0, SLOTS)
            sp.wait_ge(loaded, 16 * (2 + len(small)))

        @st.block.scalar
        def _(act):
            act.wait_ge(zeroed, 1)
            for dst, src in pieces:
                act.dma_start(dst, src).then_inc(rows_loaded, 16)
            for i, name in enumerate(("a_lam_q1", "a_lam_k1", "a_lam_q2", "a_lam_k2")):
                act.dma_start(lam[:, i, :], w[name].flatten().partition_broadcast(P)).then_inc(lam_loaded, 16)
            act.wait_ge(lam_sums, 1)
            nc.scalar.activation(k.small[:, 2:4], k.small[:, 0:2], ACT.Exp).then_inc(lam_exps, 1)

        @st.block.tensor
        def _(pe):
            pe.wait_ge(rows_loaded, 16 * len(pieces))
            pe.wait_ge(loaded, 16 * (2 + len(small)))
            for i in range(5):
                last = nc.tensor.transpose(k.ps[:, i // 4, (i % 4) * P:(i % 4 + 1) * P], v.rows[:, i, :], k.ident[:, :])
            last.then_inc(transposed, 1)

        @st.block.vector
        def _(dve):
            o = Order(dve, order)
            nc.vector.memset(v.rows[:, 4, :], 0.0).then_inc(zeroed, 1)
            o(nc.vector.memset(k.eps_cols[:, 0:1], 1e-6))
            o(nc.vector.memset(k.eps_cols[:, 1:2], 1e-5))
            o(nc.vector.memset(k.ones_row[:, :], 1.0))
            o(nc.vector.memset(k.small[:, :], 0.0))
            dve.wait_ge(lam_loaded, 64)
            for i in range(2):
                o(nc.vector.tensor_tensor(lam[:, 2 * i, :], lam[:, 2 * i, :], lam[:, 2 * i + 1, :], ALU.mult))
                o(nc.vector.tensor_reduce(k.small[:, i:i + 1], lam[:, 2 * i, :], AX_X, ALU.add))
            nc.vector.memset(k.small[:, 4:5], 0.0).then_inc(lam_sums, 1)
            dve.wait_ge(lam_exps, 1)
            o(nc.vector.tensor_tensor(k.neg_lam[:, 0:1], k.small[:, 3:4], k.small[:, 2:3], ALU.subtract))
            o(nc.vector.tensor_scalar(k.neg_lam[:, 0:1], k.neg_lam[:, 0:1], LAM_INIT, None, ALU.subtract))
            o(nc.vector.tensor_copy(k.neg_lam[:, 1:2], k.neg_lam[:, 0:1]))
            dve.wait_ge(transposed, 1)
            o(nc.vector.tensor_copy(k.cols[:, 0:512], k.ps[:, 0, :]))
            o(nc.vector.tensor_copy(k.cols[:, 512:640], k.ps[:, 1, 0:P]))
            at = COL["a_subln"]
            o(nc.vector.tensor_scalar(k.cols[:, at:at + 1], k.cols[:, at:at + 1], 1.0 - LAM_INIT, None, ALU.mult))


def memory_groups(k, qm, km, vm, cat):
    groups = []
    for h in range(MEM_HEADS):
        r = 64 * (h % 2)
        u = unit([(qm[r:r + 64, h // 2, :], km[r:r + 64, h // 2, :])],
                 lambda b, h=h: vm[:, b, h * 64:(h + 1) * 64], 0.125)
        groups.append(([u], r, 64, cat[r:r + 64, 6 + h // 2, :], None))
    return groups


def hgrn_gates(k, v):
    nc = k.nc
    with stage(k, "hgrn_gates") as st:
        act_order, log_ready, keys_ready = st.sem("act_order"), st.sem("log_ready"), st.sem("keys_ready")
        transposed, dve_order = st.sem("transposed"), st.sem("dve_order")
        t1 = v.tmp_b.rearrange("p c n -> p (c n)")
        fz = v.fz.rearrange("p t n -> p (t n)")

        @st.block.scalar
        def _(act):
            o = Order(act, act_order)
            nc.scalar.activation(v.k_tok.rearrange("p t n -> p (t n)"), fz, ACT.Sigmoid,
                                 scale=-1.0).then_inc(keys_ready, 1)
            o(nc.scalar.activation(t1, fz, ACT.Abs))
            o(nc.scalar.activation(t1, t1, ACT.Exp, scale=-1.0))
            nc.scalar.activation(t1, t1, ACT.Ln, bias=1.0).then_inc(log_ready, 1)

        @st.block.tensor
        def _(pe):
            pe.wait_ge(keys_ready, 1)
            for h in range(HEADS1):
                for t in range(TT):
                    last = nc.tensor.transpose(k.ps[:, h // 2, (h % 2) * S + t * P:(h % 2) * S + (t + 1) * P],
                                               v.k_tok[:, t, h * P:(h + 1) * P], k.ident[:, :])
            last.then_inc(transposed, 1)

        @st.block.vector
        def _(dve):
            dve.wait_ge(transposed, 1)
            nc.vector.tensor_copy(v.kT.rearrange("p c n -> p (c n)"),
                                  k.ps[:, 0:3, :].rearrange("p b n -> p (b n)"))
            dve.wait_ge(log_ready, 1)
            nc.vector.scalar_tensor_tensor(v.log_f.rearrange("p t n -> p (t n)"), fz, 0.0, t1, ALU.min,
                                           ALU.subtract)


def hgrn_attention(k, v):
    nc = k.nc
    n = HEADS1 * TT
    with stage(k, "hgrn_attention") as st:
        sums_ready, exp_done, decayed = st.sem("sums_ready"), st.sem("exp_done"), st.sem("decayed")
        scores_done, attn_ready = st.sem("scores_done"), st.sem("attn_ready")
        out_ready, out_read, dve_order = st.sem("out_ready"), st.sem("out_read"), st.sem("dve_order")
        levels = v.levels.rearrange("p l t -> p (l t)")

        def halves(m, x):
            return x[:, (m % 2) * 7:(m % 2) * 7 + 7, :]

        @st.block.tensor
        def _(pe):
            def exponents(m):
                h, t = divmod(m, TT)
                if m >= 2:
                    pe.wait_ge(exp_done, m - 1)
                for b in range(2):
                    last = nc.tensor.matmul(k.ps[:, 2 * (m % 2) + b, :], v.log_f[:, t, h * P:(h + 1) * P],
                                            levels[:, t * P + b * 512:t * P + (b + 1) * 512], start=True, stop=True)
                last.then_inc(sums_ready, 1)

            def outputs(h):
                pe.wait_ge(attn_ready, TT * (h + 1))
                if h >= 1:
                    pe.wait_ge(out_read, h)
                at = (h % 2) * S
                vals = [v.i_tok[:, t, h * P:(h + 1) * P] for t in range(TT)]
                a = v.attn[:, (h % 2) * 3:(h % 2) * 3 + 3, :]
                nc.tensor.matmul(k.ps[:, 7, at:at + P], vals[0], a[:, 0, :], start=True, stop=True)
                nc.tensor.matmul(k.ps[:, 7, at + P:at + S], vals[0], a[:, 2, :], start=True, stop=False)
                nc.tensor.matmul(k.ps[:, 7, at + P:at + S], vals[1], a[:, 1, :], start=False,
                                 stop=True).then_inc(out_ready, 1)

            exponents(0)
            for m in range(n):
                h, t = divmod(m, TT)
                if m + 1 < n:
                    exponents(m + 1)
                pe.wait_ge(decayed, m + 1)
                if m >= 1:
                    pe.wait_ge(attn_ready, m)
                for lv in range(7):
                    nc.tensor.matmul(k.ps[:, 4 + lv // 4, (lv % 4) * P:(lv % 4 + 1) * P], halves(m, v.ke)[:, lv, :],
                                     halves(m, v.qe)[:, lv, :], start=True, stop=True)
                last = nc.tensor.matmul(k.ps[:, 5, 3 * P:4 * P], v.kT[:, h, t * P:(t + 1) * P],
                                        v.q[:, h, t * P:(t + 1) * P], start=True, stop=True)
                if t:
                    last = nc.tensor.matmul(k.ps[:, 6, 0:P], v.cross[:, 0, :], v.cross[:, 1, :], start=True, stop=True)
                last.then_inc(scores_done, 1)
                if t == 0 and h:
                    outputs(h - 1)
            outputs(HEADS1 - 1)

        @st.block.scalar
        def _(act):
            def copy_out(h):
                act.wait_ge(out_ready, h + 1)
                nc.scalar.activation(v.cat[:, h, :], k.ps[:, 7, (h % 2) * S:(h % 2 + 1) * S], ACT.Copy).then_inc(out_read, 1)

            for m in range(n):
                act.wait_ge(sums_ready, m + 1)
                if m >= 2:
                    act.wait_ge(decayed, m - 1)
                nc.scalar.activation(v.decays[:, (m % 2) * 8:(m % 2) * 8 + 8, :].rearrange("p l t -> p (l t)"),
                                     k.ps[:, 2 * (m % 2):2 * (m % 2) + 2, :].rearrange("p b n -> p (b n)"),
                                     ACT.Exp).then_inc(exp_done, 1)
                if m % 2 and m > 2:
                    copy_out((m - 3) // 2)
            copy_out(HEADS1 - 1)

        @st.block.vector
        def _(dve):
            o = Order(dve, dve_order)

            def decay(m):
                h, t = divmod(m, TT)
                dve.wait_ge(exp_done, m + 1)
                if m >= 2:
                    dve.wait_ge(scores_done, m - 1)
                e = v.decays[:, (m % 2) * 8:(m % 2) * 8 + 8, :]
                lv = e[:, 1 - t:8 - t, :]
                q1, k1 = (x[:, h:h + 1, t * P:(t + 1) * P] for x in (v.q, v.kT))
                nc.vector.tensor_tensor(halves(m, v.qe), lv, q1.broadcast_to([P, 7, P]), ALU.mult)
                nc.vector.tensor_tensor(halves(m, v.ke), lv, k1.broadcast_to([P, 7, P]), ALU.mult)
                if t == 0 and m >= 2:
                    dve.wait_ge(scores_done, m)
                if t == 0:
                    nc.vector.tensor_tensor(v.cross[:, 0:1, :], e[:, 0:1, :], k1, ALU.mult).then_inc(decayed, 1)
                else:
                    nc.vector.tensor_tensor(v.cross[:, 1:2, :], e[:, 7:8, :], q1, ALU.mult).then_inc(decayed, 1)

            def mask(m):
                h, t = divmod(m, TT)
                dve.wait_ge(scores_done, m + 1)
                if h >= 2 and t == 0:
                    dve.wait_ge(out_ready, h - 1)
                scores = k.ps[:, 4:6, :].rearrange("p b n -> p (b n)")
                o(nc.vector.tensor_tensor(scores, scores, v.level_masks.rearrange("p l t -> p (l t)"), ALU.mult))
                a = v.attn[:, (h % 2) * 3:(h % 2) * 3 + 3, :]
                if t:
                    o(nc.vector.tensor_copy(a[:, 2, :], k.ps[:, 6, 0:P]))
                nc.vector.tensor_reduce(a[:, t, :], scores.rearrange("p (l t) -> p t l", l=8), AX_X,
                                        ALU.add).then_inc(attn_ready, 1)

            decay(0)
            for m in range(n):
                if m + 1 < n:
                    if (m + 1) % TT == 0:
                        mask(m)
                        decay(m + 1)
                    else:
                        decay(m + 1)
                        mask(m)
                else:
                    mask(m)


def block1(k, w, c, v):
    nc, s = k.nc, k.stream
    normed_features(k, "mem_norm_a", v.mem_tok, v.memT, lambda i: column(k, "a_mem_norm", i))
    s.stage("mem_kv_a")
    normed_features(k, "mem_norm_b", v.mem_tok, v.memT, lambda i: column(k, "b_mem_norm", i))
    s.stage("mem_kv_b")
    load(k, "load_alibi", [(v.alibi.rearrange("p c n -> p (c n)"), c["alibi"])])
    normed_features(k, "norm_mix_a", k.x, k.h, lambda i: column(k, "a_norm_mix", i))
    s.stage("in_a")
    groups = []
    for h in range(HEADS1):
        us = []
        for m in range(2):
            r = 64 * m
            us.append(unit([(v.qk[r:r + 64, h, :], v.qk[r:r + 64, 6 + h, :])],
                           lambda b, h=h: v.v_tok[:, b, h * P:(h + 1) * P], 0.125,
                           mask=v.alibi[:, 2 * h:2 * h + 2, :], factor=k.neg_lam[:, :] if m else None))
        groups.append((us, 0, P, v.cat[:, h, :], None))
    attention(k, "diff_attention", groups + memory_groups(k, v.qm, v.km[0], v.vm[0], v.cat), v.work)
    feature_norm(k, "subln", v.cat[:, 0:6, :], 6, 1, v.cat[:, 0:6, :], v.tmp, 1e-6,
                 gain=lambda i: column(k, "a_subln"))
    s.stage("out_a")
    normed_features(k, "dense_norm", k.x, k.h, lambda i: column(k, "dense_norm", i))
    swiglu(k, "dense", k.x, k.h, v.dense_hidden, v.dense_gated, v.dense_raw)
    normed_features(k, "norm_mix_b", k.x, k.h, lambda i: column(k, "b_norm_mix", i))
    s.stage("in_b")
    load(k, "load_levels", [(v.levels.rearrange("p c n -> p (c n)"), c["levels"]),
                            (v.level_masks.rearrange("p c n -> p (c n)"), c["level_masks"])])
    hgrn_gates(k, v)
    hgrn_attention(k, v)
    attention(k, "memory_attention_b", memory_groups(k, v.qm_b, v.km[1], v.vm[1], v.cat), v.work_b)
    feature_norm(k, "out_norm_b", v.cat[:, 0:6, :], 6, 1, v.cat[:, 0:6, :], v.tmp_b, 1e-6,
                 gain=lambda i: column(k, "b_out_norm"), gate=v.g)
    s.stage("out_b")
    normed_features(k, "moe_norm", k.x, k.h, lambda i: column(k, "moe_norm", i))
    s.stage("router")
    top_two_weights(k, k.logits, k.expert_weights)
    swiglu(k, "experts", k.x, k.h, v.hidden, v.gated, v.raw, weight=k.expert_weights)
    load(k, "load_final_norm", [(k.rows[:, 0, :], w["final_norm"].flatten().partition_broadcast(P))])
    final_norm(k, k.x, k.rows[:, 0, :], k.x)


RET_HEADS, RET_DV = 4, 512
MLA_HEADS, MLA_NOPE, MLA_ROPE, MLA_V = 8, 128, 64, 128
MOBA_HEADS, MOBA_DH = 16, 64
DN_ALPHA = 4.0 ** 0.25


def rows_of_eight(w, width=512):
    def loads(p):
        c0, k0 = (p // 3) * width, (p % 3) * 8
        return [(lambda slot, h=h: slot[:, h * 4 * width:(h + 1) * 4 * width].rearrange("p (k c) -> p k c", k=4),
                 w[(k0 + 4 * h) * P:(k0 + 4 * h + 4) * P, c0:c0 + width].rearrange("(k p) c -> p k c", p=P))
                for h in range(2)]
    return loads


def plan_block2(k, w):
    a = k.area
    v = Fields()
    v.rq, v.rk, v.rv, v.rg = a(0, 8), a(2048, 8), a(4096, 2, 2048), a(8192, 16)
    v.squares, v.cat, v.decay = a(0, 16), a(12288, 24), a(16384, 8)
    v.angle, v.turned, v.cos, v.sin = a(12288, 3), a(12288, 8), a(18432, 3), a(19200, 3)
    v.mq, v.mkv, v.kpe = a(19968, 2), a(20480, 2), a(20992, 1)
    v.weights = k.xn[:, 0, :].rearrange("p (c n) -> p c n", c=4)
    v.qn, v.kn, v.qpe, v.vm, v.mg = a(0, 8), a(2048, 8), a(4096, 4), a(5120, 2, 1024), a(7168, 8)
    v.work, v.turned_pe, v.qm_squares = a(9216, 4), a(10240, 8), a(10240, 2)
    v.q2, v.k2, v.v2, v.g2, v.cat2 = a(0, 8), a(2048, 8), a(4096, 2, 1024), a(6144, 8), a(8192, 8)
    v.work2 = a(10240, 4)
    s = k.stream
    wi = w["w_in_even_2"]

    def twice(p):
        src = wi[:, 6656:6720].rearrange("(k p) c -> p k c", p=P)
        return [(lambda slot, h=h: slot[:, 0:DC * P].rearrange("p (k c) -> p k c", k=DC)[:, :, h * 64:(h + 1) * 64],
                 src) for h in range(2)]

    s.add([run("F", wi, 0, k.h, to_features(v.rq), count=2), run("F", wi, 1024, k.h, to_features(v.rk), count=2),
           run("T", wi, 2048, k.h, to_tokens(v.rv), count=4),
           run("F", wi, 4096, k.h, to_features(v.rg, func=ACT.Silu), count=4),
           run("F", wi, 6144, k.h, to_features(v.mq, chunks=2), width=256),
           run("F", wi, 6400, k.h, to_features(v.mkv, chunks=2), width=256),
           run("F", wi, 6656, k.h, to_features(v.kpe, chunks=1), width=P, loads=twice)])

    def split(w_, head, lo, hi, heads):
        return grouped_loads(w_, 2, heads, hi - lo, lambda rows, p: rows.rearrange("p (h c) -> p h c", c=head)[
            :, heads * p:heads * (p + 1), lo:hi])

    uq, ukv = w["w_uq_even_2"], w["w_ukv_even_2"]
    s.add([run("F", wi, 6720, k.h, to_features(v.mg, func=ACT.Silu), count=2),
           run("F", uq, 0, v.mq, to_features(v.qn), count=2, nk=2, loads=split(uq, 192, 0, 128, 4)),
           run("F", uq, 0, v.mq, to_features(v.qpe), nk=2, loads=split(uq, 192, 128, 192, 8)),
           run("F", ukv, 0, v.mkv, to_features(v.kn), count=2, nk=2, loads=split(ukv, 256, 0, 128, 4)),
           run("T", ukv, 0, v.mkv, to_tokens(v.vm), count=2, nk=2, loads=split(ukv, 256, 128, 256, 4))])
    s.add([run("T", None, 0, lambda p: v.cat[:, (p % 3) * 8:(p % 3) * 8 + 8, :], add_to_residual(k.x, DN_ALPHA),
               on="dve", count=6, acc=3, loads=rows_of_eight(w["w_out_even_2"]))])
    wo = w["w_in_odd_2"]
    s.add([run("F", wo, 0, k.h, to_features(v.q2), count=2), run("F", wo, 1024, k.h, to_features(v.k2), count=2),
           run("T", wo, 2048, k.h, to_tokens(v.v2), count=2),
           run("F", wo, 3072, k.h, to_features(v.g2, func=ACT.Silu), count=2)])
    s.add([run("T", w["w_out_odd_2"], 0, v.cat2, add_to_residual(k.x, DN_ALPHA), on="dve", count=2)])
    return v


def rotation_tables(k, w, v):
    nc = k.nc
    two_pi = 2.0 * np.pi
    c1 = 6.28125
    c2 = float(np.float32(two_pi - c1))
    c2 = float(np.float32(np.round(c2 * 2 ** 20) / 2 ** 20))
    c3 = float(np.float32(two_pi - c1 - c2))
    magic = 1.5 * 2.0 ** 23
    limit = 3.1415925
    with stage(k, "rotation_tables") as st:
        loaded, order, reduced, done = st.sem("loaded"), st.sem("order"), st.sem("reduced"), st.sem("done")
        flat = lambda x: x.rearrange("p c n -> p (c n)")
        angle, cos, sin = flat(v.angle), flat(v.cos), flat(v.sin)

        @st.block.scalar
        def _(act):
            act.dma_start(k.pos[:, :], w["positions_2"].flatten().partition_broadcast(P)).then_inc(loaded, 16)
            act.wait_ge(reduced, 1)
            nc.scalar.activation(sin, sin, ACT.Sin).then_inc(done, 1)
            nc.scalar.activation(cos, cos, ACT.Sin).then_inc(done, 1)

        @st.block.vector
        def _(dve):
            o = Order(dve, order)
            dve.wait_ge(loaded, 16)
            o(nc.vector.tensor_copy(v.cos[:, 0, :], k.pos[:, :]))
            for j in range(3):
                o(nc.vector.tensor_scalar(v.angle[:, j, :], v.cos[:, 0, :], k.freq[:, j:j + 1], None, ALU.mult))
            o(nc.vector.tensor_scalar(cos, angle, 1.0 / two_pi, None, ALU.mult))
            o(nc.vector.tensor_scalar(cos, cos, magic, None, ALU.add))
            o(nc.vector.tensor_scalar(cos, cos, magic, None, ALU.subtract))
            for part in (c1, c2, c3):
                o(nc.vector.scalar_tensor_tensor(angle, cos, -part, angle, ALU.mult, ALU.add))
            o(nc.vector.tensor_scalar(sin, angle, limit, -limit, ALU.min, ALU.max))
            o(nc.vector.tensor_scalar(cos, angle, np.pi / 2, -two_pi, ALU.is_gt, ALU.mult))
            o(nc.vector.scalar_tensor_tensor(cos, angle, np.pi / 2, cos, ALU.add, ALU.add))
            nc.vector.tensor_scalar(cos, cos, limit, -limit, ALU.min, ALU.max).then_inc(reduced, 1)


def rotate(k, name, pieces, partner, cos, sin, turned):
    nc = k.nc
    j = cos.shape[1]
    with stage(k, name) as st:
        turned_ready, order, piece_done = st.sem("turned_ready"), st.sem("order"), st.sem("piece_done")

        @st.block.tensor
        def _(pe):
            for i, x in enumerate(pieces):
                if i >= 2:
                    pe.wait_ge(piece_done, i - 1)
                for c in range(x.shape[1]):
                    last = nc.tensor.matmul(k.ps[:, 4 * (i % 2) + c // 2, (c % 2) * S:(c % 2 + 1) * S], partner[:, :],
                                            x[:, c, :], start=True, stop=True)
                last.then_inc(turned_ready, 1)

        @st.block.vector
        def _(dve):
            o = Order(dve, order)
            for i, x in enumerate(pieces):
                n = x.shape[1]
                reps = n // j

                def tabled(t):
                    if j == 1:
                        return t.broadcast_to([P, n, S])
                    return t.unsqueeze(1).broadcast_to([P, reps, j, S])

                def grouped(y):
                    return y if j == 1 else y.rearrange("p (a j) n -> p a j n", j=j)
                banks = k.ps[:, 4 * (i % 2):4 * (i % 2) + 4, :].rearrange("p b (h n) -> p (b h) n", h=2)[:, 0:n, :]
                dve.wait_ge(turned_ready, i + 1)
                nc.vector.tensor_tensor(grouped(turned[:, 0:n, :]), grouped(banks), tabled(sin), ALU.mult)
                o(nc.vector.tensor_tensor(grouped(x), grouped(x), tabled(cos), ALU.mult))
                o(nc.vector.tensor_tensor(x, x, turned[:, 0:n, :], ALU.add))
                nc.vector.memset(k.small[:, 63:64], 0.0).then_inc(piece_done, 1)


def retention(k, v):
    nc = k.nc
    with stage(k, "retention") as st:
        scores_ready, decayed = st.sem("scores_ready"), st.sem("decayed")
        out_ready, out_read = st.sem("out_ready"), st.sem("out_read")

        @st.block.tensor
        def _(pe):
            def scores(h):
                if h >= 2:
                    pe.wait_ge(decayed, h - 1)
                for b in range(TT):
                    for c in range(2):
                        last = nc.tensor.matmul(k.ps[:, h % 2, b * S:(b + 1) * S],
                                                v.rk[:, 2 * h + c, b * P:(b + 1) * P], v.rq[:, 2 * h + c, :],
                                                start=(c == 0), stop=(c == 1))
                last.then_inc(scores_ready, 1)

            scores(0)
            for h in range(RET_HEADS):
                if h + 1 < RET_HEADS:
                    scores(h + 1)
                pe.wait_ge(decayed, h + 1)
                if h >= 2:
                    pe.wait_ge(out_read, h - 1)
                for c in range(RET_DV // P):
                    for b in range(TT):
                        last = nc.tensor.matmul(k.ps[:, 4 + 2 * (h % 2) + c // 2, (c % 2) * S:(c % 2 + 1) * S],
                                                v.rv[:, b, h * RET_DV + c * P:h * RET_DV + (c + 1) * P],
                                                v.weights[:, 2 * (h % 2) + b, :], start=(b == 0), stop=(b == 1))
                last.then_inc(out_ready, 1)

        @st.block.vector
        def _(dve):
            for h in range(RET_HEADS):
                dve.wait_ge(scores_ready, h + 1)
                if h >= 2:
                    dve.wait_ge(out_ready, h - 1)
                nc.vector.tensor_tensor(v.weights[:, 2 * (h % 2):2 * (h % 2) + 2, :],
                                        k.ps[:, h % 2, :].rearrange("p (b n) -> p b n", b=2),
                                        v.decay[:, 2 * h:2 * h + 2, :], ALU.mult).then_inc(decayed, 1)

        @st.block.scalar
        def _(act):
            for h in range(RET_HEADS):
                act.wait_ge(out_ready, h + 1)
                nc.scalar.activation(v.cat[:, 4 * h:4 * h + 4, :].rearrange("p c n -> p (c n)"),
                                     k.ps[:, 4 + 2 * (h % 2):6 + 2 * (h % 2), :].rearrange("p b n -> p (b n)"),
                                     ACT.Copy).then_inc(out_read, 1)


def layer_norm_rows(k, name, w_gain, w_bias, x):
    nc = k.nc
    with stage(k, name) as st:
        loaded, order, mean_ready = st.sem("loaded"), st.sem("order"), st.sem("mean_ready")
        squares_summed, variance_ready, root_ready = (st.sem("squares_summed"), st.sem("variance_ready"),
                                                      st.sem("root_ready"))

        @st.block.scalar
        def _(act):
            act.dma_start(k.rows[:, 0, :], w_gain.partition_broadcast(P)).then_inc(loaded, 16)
            act.dma_start(k.rows[:, 1, :], w_bias.partition_broadcast(P)).then_inc(loaded, 16)
            act.wait_ge(mean_ready, 1)
            for t in range(TT):
                squares = k.ps[:, 4 + 2 * t:6 + 2 * t, :].rearrange("p b n -> p (b n)")
                last = nc.scalar.activation(squares, x[:, t, :], ACT.Square, bias=k.stat[:, 2 + t:3 + t],
                                            accum_out=k.stat[:, 4 + t:5 + t])
            last.then_inc(squares_summed, 1)
            act.wait_ge(variance_ready, 1)
            nc.scalar.activation(k.stat[:, 6:8], k.stat[:, 0:2], ACT.Sqrt).then_inc(root_ready, 1)

        @st.block.vector
        def _(dve):
            o = Order(dve, order)
            o(nc.vector.tensor_reduce(k.stat[:, 0:2], x, AX_X, ALU.add))
            nc.vector.tensor_scalar(k.stat[:, 2:4], k.stat[:, 0:2], -1.0 / D, None, ALU.mult).then_inc(mean_ready, 1)
            dve.wait_ge(mean_ready, 1)
            for t in range(TT):
                o(nc.vector.tensor_scalar(k.ps[:, 2 * t:2 * t + 2, :].rearrange("p b n -> p (b n)"), x[:, t, :],
                                          k.stat[:, 2 + t:3 + t], None, ALU.add))
            dve.wait_ge(squares_summed, 1)
            nc.vector.tensor_scalar(k.stat[:, 0:2], k.stat[:, 4:6], 1.0 / D, 1e-5, ALU.mult,
                                    ALU.add).then_inc(variance_ready, 1)
            dve.wait_ge(root_ready, 1)
            o(nc.vector.reciprocal(k.stat[:, 6:8], k.stat[:, 6:8]))
            dve.wait_ge(loaded, 32)
            for t in range(TT):
                o(nc.vector.scalar_tensor_tensor(x[:, t, :], k.ps[:, 2 * t:2 * t + 2, :].rearrange("p b n -> p (b n)"),
                                                 k.stat[:, 6 + t:7 + t], k.rows[:, 0, :], ALU.mult, ALU.mult))
                o(nc.vector.tensor_tensor(x[:, t, :], x[:, t, :], k.rows[:, 1, :], ALU.add))


def block2(k, w, c, v):
    s = k.stream
    causal = k.causal[:, :].rearrange("p (t n) -> p t n", t=TT)
    normed_features(k, "features_even", k.x, k.h)
    load(k, "load_decay", [(v.decay.rearrange("p c n -> p (c n)"), c["decay"])])
    rotation_tables(k, w, v)
    s.stage("in_even")
    rotate(k, "rotate_retention", [v.rq, v.rk], k.pair_rot, v.cos[:, 0:2, :], v.sin[:, 0:2, :], v.turned)
    retention(k, v)
    feature_norm(k, "retention_norm", v.cat[:, 0:16, :], RET_HEADS, 4, v.cat[:, 0:16, :], v.squares, 1e-5,
                 center=True, gate=v.rg)
    feature_norm(k, "q_norm", v.mq, 1, 2, v.mq, v.qm_squares, 1e-6, gain=lambda i: column(k, "q_norm_even_2", i))
    feature_norm(k, "kv_norm", v.mkv, 1, 2, v.mkv, v.qm_squares, 1e-6, gain=lambda i: column(k, "kv_norm_even_2", i))
    s.stage("mla_up")
    rotate(k, "rotate_mla", [v.qpe, v.kpe], k.half_rot, v.cos[:, 2:3, :], v.sin[:, 2:3, :], v.turned_pe)
    groups = []
    for h in range(MLA_HEADS):
        r = 64 * (h % 2)
        u = unit([(v.qn[:, h, :], v.kn[:, h, :]), (v.qpe[r:r + 64, h // 2, :], v.kpe[r:r + 64, 0, :])],
                 lambda b, h=h: v.vm[:, b, h * P:(h + 1) * P], (MLA_NOPE + MLA_ROPE) ** -0.5, mask=causal)
        groups.append(([u], 0, P, v.cat[:, 16 + h, :], v.mg[:, h, :]))
    attention(k, "latent_attention", groups, v.work)
    s.stage("out_even")
    layer_norm_rows(k, "layer_norm_even", w["ln_g_2"][0], w["ln_b_2"][0], k.x)
    normed_features(k, "features_odd", k.x, k.h)
    s.stage("in_odd")
    rotate(k, "rotate_moba", [v.q2, v.k2], k.half_rot, v.cos[:, 2:3, :], v.sin[:, 2:3, :], v.turned)
    groups = []
    for h in range(MOBA_HEADS):
        r = 64 * (h % 2)
        u = unit([(v.q2[r:r + 64, h // 2, :], v.k2[r:r + 64, h // 2, :])],
                 lambda b, h=h: v.v2[:, b, h * MOBA_DH:(h + 1) * MOBA_DH], 0.125, mask=causal)
        groups.append(([u], r, MOBA_DH, v.cat2[r:r + 64, h // 2, :], v.g2[r:r + 64, h // 2, :]))
    attention(k, "block_attention", groups, v.work2)
    s.stage("out_odd")
    layer_norm_rows(k, "layer_norm_odd", w["ln_g_2"][1], w["ln_b_2"][1], k.x)


LSTM_HEADS, QK_CONV, CONF_K = 4, 4, 31
NSA_HEADS, NSA_GROUPS, N_CMP = 8, 2, S // 16 - 1


def plan_block3(k, w):
    a = k.area
    v = Fields()
    v.ya, v.yb, v.yc, v.gate = a(0, 8), a(2048, 8), a(4096, 8), a(6144, 1, 1024)
    v.c, v.ada = k.c_cols[:, 0:8].unsqueeze(2), k.c_cols[:, 8:24].unsqueeze(2)
    v.c_all = a(9792, 8, P)
    row = lambda at, n: a(7168 + at, 1, n)[0:1, 0, :]
    v.row_gate, v.row_av, v.row_if = row(0, 1024), row(1024, 1024), row(2048, 8)
    v.row_vs, v.row_vw, v.row_g = row(2056, 256), row(2312, 256), row(2568, 24)
    v.qk_pad, v.qk, v.av = a(9792, 16, S + QK_CONV - 1), a(13936, 16), a(18032, 2, 1024)
    v.ao, v.az, v.i_f = v.yc, v.yb, k.i_f
    v.decays, v.sqk, v.probs_t = a(9792, 8), a(11840, 8), a(13936, 8)
    v.a_all = k.xn[:, 0, :].rearrange("p (c n) -> p c n", n=P)
    v.squares_a = a(9792, 8)
    v.u_pad, v.ba, v.bb = a(9792, 8, S + CONF_K - 1), a(12080, 8), a(14128, 8)
    v.u, v.bz, v.squares_b = a(16176, 8), a(18224, 8), a(12080, 8)
    v.cq, v.ckv, v.ks, v.kw = a(9792, 8), a(11840, 4), a(12864, 2), a(13376, 2)
    v.vs, v.vw, v.cz = a(13888, 2), a(14400, 2), a(14912, 8)
    v.work, v.blocks = a(16960, 4), a(17984, 64, 2 * N_CMP)
    v.w2, v.hidden = a(19904, 4, P), a(20416, 4, 2 * N_CMP)
    v.kc, v.vc = a(20536, 1, 2 * N_CMP), a(20566, 2, P)
    v.g3 = k.g3
    v.mg, v.merged, v.o_tok = a(9792, 24), a(15936, 8), a(17984, 2, 1024)

    s, wi = k.stream, w["w_in_3"]

    def biased(key):
        return lambda c: k.cols[:, ds(COL[key] + c, 1)]

    def F(c0, dst, key, func=ACT.Identity, count=1, chunks=4, width=512):
        return run("F", wi, c0, k.h, to_features(dst, func=func, chunks=chunks, bias=biased(key)), count=count,
                   width=width)

    def T(c0, dst, row_, count=1, width=512):
        return run("T", wi, c0, k.h, to_tokens(dst, width=width), count=count, width=width,
                   bias=lambda p: row_[:, p * width:(p + 1) * width])

    def gate_out(nc, banks, p):
        return nc.scalar.activation(v.gate[:, :, ds(p * 512, 512)], banks[:, 0:1, :], ACT.Copy)

    s.add([run("F", w["w_ada_3"], 0, v.c, to_features(v.ada), count=4, n=1),
           run("T", w["w_ada_3"], 2048, v.c_all, gate_out, count=2, tiles=1,
               bias=lambda p: v.row_gate[:, p * 512:(p + 1) * 512])])
    s.add([F(0, v.qk_pad[:, :, QK_CONV - 1:], "qk", count=4), T(2048, v.av, v.row_av, count=2),
           F(3072, v.ao, "ao", ACT.Sigmoid, 2), F(4096, v.az, "az", ACT.Silu, 2),
           T(5120, v.i_f, v.row_if, width=8)])
    s.add([F(5128, v.ba, "ba", count=2), F(6152, v.bb, "bb", ACT.Sigmoid, 2), F(7176, v.bz, "bz", ACT.Silu, 2)])
    s.add([F(8200, v.cq, "cq", count=2), F(9224, v.ckv, "ckc"), F(9736, v.ks, "cks", chunks=2, width=256),
           T(9992, v.vs, v.row_vs, width=256), F(10248, v.kw, "ckw", chunks=2, width=256),
           T(10504, v.vw, v.row_vw, width=256), T(10760, v.g3, v.row_g, width=24),
           F(10784, v.cz, "cz", ACT.Silu, 2)])

    w1 = w["nsa_cmp_w1_3"].rearrange("j k c -> (j k) c")

    def w1_rows(p):
        return [(lambda slot, h=h: slot[:, h * 8 * 256:(h + 1) * 8 * 256].rearrange("p (k c) -> p k c", k=8),
                 w1[(p * 16 + h * 8) * P:(p * 16 + h * 8 + 8) * P, :].rearrange("(k p) c -> p k c", p=P))
                for h in range(2)]

    def gelu_out(nc, banks, q):
        return nc.scalar.activation(v.hidden[:, 2 * q:2 * q + 2, :], banks[:, :, 0:2 * N_CMP], ACT.Gelu_apprx_tanh)

    s.add([run("F", None, 0, lambda p: v.blocks[:, p * 16:(p + 1) * 16, :], gelu_out, count=4, acc=2, n=2 * N_CMP,
               width=256, nk=16, loads=w1_rows)])
    s.add([F(11808, v.mg, "mg", ACT.Sigmoid, count=6)])

    def gated(b):
        def evict(nc, banks, p):
            at = v.mg[:, ds(p * 4 + b * 8, 4), :]
            return nc.vector.tensor_tensor(at, at, banks.rearrange("p b (h n) -> p (b h) n", h=2), ALU.mult)
        return evict
    s.add([run("F", w["w_branch_3"][b], 0, y, gated(b), on="dve", count=2)
           for b, y in enumerate((v.ya, v.yb, v.yc))])
    s.add([run("T", w["w_out_3"], 0, v.merged, to_tokens(v.o_tok), count=2)])
    return v


def load_block3(k, w, v):
    nc = k.nc
    b_in = w["b_in_3"].flatten()
    rows = [(v.row_gate, w["b_ada_3"].flatten()[2048:3072])]
    rows += [(r, b_in[at:at + n]) for r, at, n in ((v.row_av, 2048, 1024), (v.row_if, 5120, 8),
                                                  (v.row_vs, 9992, 256), (v.row_vw, 10504, 256),
                                                  (v.row_g, 10760, 24))]
    with stage(k, "load_block3") as st:
        loaded = st.sem("loaded")

        @st.block.scalar
        def _(act):
            with nc.allow_non_contiguous_dma(reason="1024 values of c, one to a partition and chunk"):
                act.dma_start(k.c_cols[:, 0:8], w["c_3"].flatten().rearrange("(k p) -> p k", p=P)).then_inc(loaded, 16)
            for dst, src in rows:
                act.dma_start(dst, src.unsqueeze(0)).then_inc(loaded, 16)
            act.wait_ge(loaded, 16 * (1 + len(rows)))

        @st.block.vector
        def _(dve):
            dve.wait_ge(loaded, 16 * (1 + len(rows)))
            nc.vector.tensor_copy(v.c_all, v.c.broadcast_to([P, DC, P]))


def modulation(k, v):
    nc = k.nc
    ada = k.c_cols[:, 8:24]
    with stage(k, "modulation") as st:
        order = st.sem("order")

        @st.block.vector
        def _(dve):
            o = Order(dve, order)
            o(nc.vector.tensor_tensor(ada, ada, k.cols[:, COL["shift"]:COL["shift"] + 16], ALU.add))
            o(nc.vector.scalar_tensor_tensor(ada[:, 8:16], ada[:, 8:16], 1.0,
                                             k.cols[:, COL["norm_pre_3"]:COL["norm_pre_3"] + 8], ALU.add, ALU.mult))
            nc.vector.memset(v.qk_pad[:, :, 0:QK_CONV - 1], 0.0)


def causal_conv(k, name, x_pad, out, taps, key, bias=None, silu_bias=None):
    nc = k.nc
    n = out.shape[1]
    with stage(k, name) as st:
        tap_done = st.sem("tap_done")

        @st.block.vector
        def _(dve):
            for tap in range(taps):
                for c in range(n):
                    w = column(k, key, tap * n + c)
                    src = x_pad[:, c, tap:tap + S]
                    if tap == 0:
                        if bias is None:
                            ins = nc.vector.tensor_scalar(out[:, c, :], src, w, None, ALU.mult)
                        else:
                            ins = nc.vector.tensor_scalar(out[:, c, :], src, w, bias(c), ALU.mult, ALU.add)
                    else:
                        dve.wait_ge(tap_done, (tap - 1) * n + c + 1)
                        ins = nc.vector.scalar_tensor_tensor(out[:, c, :], src, w, out[:, c, :], ALU.mult, ALU.add)
                    ins.then_inc(tap_done, 1)

        @st.block.scalar
        def _(act):
            if silu_bias is not None:
                for c in range(n):
                    act.wait_ge(tap_done, (taps - 1) * n + c + 1)
                    nc.scalar.activation(out[:, c, :], out[:, c, :], ACT.Silu, bias=silu_bias(c))


def mlstm(k, v):
    nc = k.nc
    small = k.lstm
    lf, f_sum, a = small[:, 0:8], small[:, 8:16], small[:, 16:24]
    neg_m, neg_stab, den, pos = small[:, 24:32], small[:, 32:40], small[:, 40:48], small[:, 48:56]
    i_gate, f_gate = v.i_f[:, :, 0:4], v.i_f[:, :, 4:8]
    th = lambda x: x.rearrange("p (t h) -> p t h", t=TT)
    with stage(k, "mlstm") as st:
        act_order, dve_order, logs_ready = st.sem("act_order"), st.sem("dve_order"), st.sem("logs_ready")
        lf_ready, sums_ready, a_ready = st.sem("lf_ready"), st.sem("sums_ready"), st.sem("a_ready")
        rows_ready, max_ready, exp_done = st.sem("rows_ready"), st.sem("max_ready"), st.sem("exp_done")
        scores_ready, probs_ready = st.sem("scores_ready"), st.sem("probs_ready")
        transposed, pt_ready, out_ready = st.sem("transposed"), st.sem("pt_ready"), st.sem("out_ready")
        heads = lambda x: x.rearrange("p (h t) n -> p h t n", t=TT)
        banks = lambda b: k.ps[:, b:b + 4, :].rearrange("p b (t n) -> p b t n", t=TT)

        @st.block.scalar
        def _(act):
            o = Order(act, act_order)
            t1 = th(pos)
            o(nc.scalar.activation(t1, f_gate, ACT.Abs))
            o(nc.scalar.activation(t1, t1, ACT.Exp, scale=-1.0))
            nc.scalar.activation(t1, t1, ACT.Ln, bias=1.0).then_inc(logs_ready, 1)
            act.wait_ge(max_ready, 1)
            for i in range(8):
                nc.scalar.activation(v.decays[:, i, :], v.decays[:, i, :], ACT.Exp, bias=neg_m[:, i:i + 1])
            nc.scalar.activation(neg_stab, neg_stab, ACT.Exp).then_inc(exp_done, 1)
            act.wait_ge(transposed, 1)
            nc.scalar.activation(v.probs_t.rearrange("p c n -> p (c n)"),
                                 k.ps[:, 0:4, :].rearrange("p b n -> p (b n)"), ACT.Copy).then_inc(pt_ready, 1)
            act.wait_ge(out_ready, 1)
            nc.scalar.activation(v.ya.rearrange("p c n -> p (c n)"),
                                 k.ps[:, 4:8, :].rearrange("p b n -> p (b n)"), ACT.Copy)

        @st.block.tensor
        def _(pe):
            for h in range(LSTM_HEADS):
                for t in range(TT):
                    for c in range(2):
                        last = nc.tensor.matmul(k.ps[:, 4 + h, t * S:(t + 1) * S],
                                                v.qk[:, 2 * h + c, t * P:(t + 1) * P], v.qk[:, 8 + 2 * h + c, :],
                                                start=(c == 0), stop=(c == 1))
            last.then_inc(scores_ready, 1)
            pe.wait_ge(lf_ready, 1)
            nc.tensor.matmul(k.ps[:, 0, 0:4], k.upper[:, :], lf[:, 0:4], start=True, stop=True)
            nc.tensor.matmul(k.ps[:, 0, 4:8], k.ones[:, :], lf[:, 0:4], start=True, stop=False)
            nc.tensor.matmul(k.ps[:, 0, 4:8], k.upper[:, :], lf[:, 4:8], start=False, stop=True).then_inc(sums_ready, 1)
            pe.wait_ge(a_ready, 1)
            for h in range(LSTM_HEADS):
                for b in range(TT):
                    last = nc.tensor.matmul(k.ps[:, 1 + h // 2, (h % 2) * S + b * P:(h % 2) * S + (b + 1) * P],
                                            v.a_all[:, b * 4 + h, :], k.ident[:, :], start=True, stop=True)
            last.then_inc(rows_ready, 1)
            pe.wait_ge(probs_ready, 1)
            for h in range(LSTM_HEADS):
                for b in range(TT):
                    for t in range(TT):
                        last = nc.tensor.transpose(k.ps[:, h, b * S + t * P:b * S + (t + 1) * P],
                                                   v.sqk[:, 2 * h + t, b * P:(b + 1) * P], k.ident[:, :])
            last.then_inc(transposed, 1)
            pe.wait_ge(pt_ready, 1)
            for h in range(LSTM_HEADS):
                for c in range(2):
                    for b in range(TT):
                        last = nc.tensor.matmul(k.ps[:, 4 + h, c * S:(c + 1) * S],
                                                v.av[:, b, h * 256 + c * P:h * 256 + (c + 1) * P],
                                                v.probs_t[:, 2 * h + b, :], start=(b == 0), stop=(b == 1))
            last.then_inc(out_ready, 1)

        @st.block.vector
        def _(dve):
            o = Order(dve, dve_order)
            o(nc.vector.tensor_tensor(v.ao, v.ao, v.az, ALU.mult))
            dve.wait_ge(logs_ready, 1)
            nc.vector.scalar_tensor_tensor(th(lf), f_gate, 0.0, th(pos), ALU.min, ALU.subtract).then_inc(lf_ready, 1)
            dve.wait_ge(sums_ready, 1)
            o(nc.vector.tensor_copy(f_sum, k.ps[:, 0, 0:8]))
            o(nc.vector.tensor_tensor(th(a), i_gate, th(f_sum), ALU.subtract))
            nc.vector.tensor_copy(v.a_all, a.unsqueeze(2).broadcast_to([P, 8, P])).then_inc(a_ready, 1)
            dve.wait_ge(rows_ready, 1)
            mask = k.causal[:, :].rearrange("p (t n) -> p t n", t=TT)
            for h in range(LSTM_HEADS):
                row = k.ps[:, 1 + h // 2, (h % 2) * S:(h % 2 + 1) * S].unsqueeze(1).broadcast_to([P, TT, S])
                o(nc.vector.tensor_tensor(v.decays[:, 2 * h:2 * h + 2, :], row, mask, ALU.add))
            o(nc.vector.tensor_reduce(neg_m, v.decays, AX_X, ALU.max))
            o(nc.vector.tensor_scalar(neg_m, neg_m, 0.0, -1.0, ALU.max, ALU.mult))
            f_ht = f_sum.rearrange("p (t h) -> p h t", t=TT)
            ht = lambda x: x.rearrange("p (h t) -> p h t", t=TT)
            nc.vector.tensor_tensor(ht(neg_stab), ht(neg_m), f_ht, ALU.subtract).then_inc(max_ready, 1)
            dve.wait_ge(scores_ready, 1)
            dve.wait_ge(exp_done, 1)
            o(nc.vector.scalar_tensor_tensor(v.sqk.rearrange("p c n -> p (c n)"),
                                             k.ps[:, 4:8, :].rearrange("p b n -> p (b n)"), 1.0 / 16,
                                             v.decays.rearrange("p c n -> p (c n)"), ALU.mult, ALU.mult))
            o(nc.vector.tensor_reduce(den, v.sqk, AX_X, ALU.add))
            o(nc.vector.tensor_scalar(pos, den, -1.0, None, ALU.mult))
            o(nc.vector.tensor_tensor(den, den, pos, ALU.max))
            o(nc.vector.tensor_tensor(den, den, neg_stab, ALU.max))
            o(nc.vector.reciprocal(den, den))
            nc.vector.tensor_tensor(v.sqk, v.sqk, den.unsqueeze(2).broadcast_to([P, 8, S]),
                                    ALU.mult).then_inc(probs_ready, 1)


def glu_input(k, v):
    nc = k.nc
    with stage(k, "glu_input") as st:
        @st.block.vector
        def _(dve):
            nc.vector.memset(v.u_pad[:, :, 0:CONF_K - 1], 0.0)
            nc.vector.tensor_tensor(v.u_pad[:, :, CONF_K - 1:], v.ba, v.bb, ALU.mult)


def compression_blocks(k, w, v):
    nc = k.nc
    with stage(k, "compression_blocks") as st:
        loaded = st.sem("loaded")

        @st.block.vector
        def _(dve):
            for j in range(2):
                for g in range(NSA_GROUPS):
                    t = v.ckv[:, 2 * j + g, :].rearrange("p (n l) -> p l n", l=16)
                    pe_ = k.cols[:, COL["pe"] + 32 * j:COL["pe"] + 32 * j + 32].unsqueeze(2)
                    for half in range(2):
                        nc.vector.tensor_tensor(
                            v.blocks[:, 32 * j + 16 * half:32 * j + 16 * half + 16, g * N_CMP:(g + 1) * N_CMP],
                            t[:, :, half:half + N_CMP],
                            pe_[:, 16 * half:16 * half + 16, :].broadcast_to([P, 16, N_CMP]), ALU.add)

        @st.block.scalar
        def _(act):
            act.dma_start(v.w2, w["nsa_cmp_w2_3"].rearrange("j (k p) c -> p (j k) c", p=P)).then_inc(loaded, 16)
            nc.scalar.activation(v.g3, v.g3, ACT.Sigmoid)
            act.wait_ge(loaded, 16)


def compressed_keys(k, v):
    nc = k.nc
    with stage(k, "compressed_keys") as st:
        ready = st.sem("ready")

        @st.block.tensor
        def _(pe):
            for c in range(2):
                last = nc.tensor.matmul(k.ps[:, 0, 0:2 * N_CMP], v.w2[:, c, :], v.hidden[:, c, :], start=(c == 0),
                                        stop=(c == 1))
            last.then_inc(ready, 1)
            for g in range(NSA_GROUPS):
                for c in range(2):
                    last = nc.tensor.matmul(k.ps[0:N_CMP, 1, g * P:(g + 1) * P],
                                            v.hidden[:, 2 + c, g * N_CMP:(g + 1) * N_CMP], v.w2[:, 2 + c, :],
                                            start=(c == 0), stop=(c == 1))
            last.then_inc(ready, 1)

        @st.block.vector
        def _(dve):
            dve.wait_ge(ready, 1)
            nc.vector.tensor_copy(v.kc[:, 0, :], k.ps[:, 0, 0:2 * N_CMP])
            dve.wait_ge(ready, 2)
            nc.vector.tensor_copy(v.vc[0:N_CMP, :, :].rearrange("p g n -> p (g n)"), k.ps[0:N_CMP, 1, 0:2 * P])


def merge(k, v):
    nc = k.nc
    with stage(k, "merge") as st:
        order = st.sem("order")

        @st.block.vector
        def _(dve):
            o = Order(dve, order)
            o(nc.vector.tensor_tensor(v.merged, v.mg[:, 0:8, :], v.mg[:, 8:16, :], ALU.add))
            o(nc.vector.tensor_tensor(v.merged, v.merged, v.mg[:, 16:24, :], ALU.add))


def add_gated(k, v):
    nc = k.nc
    with stage(k, "add_gated") as st:
        order = st.sem("order")

        @st.block.vector
        def _(dve):
            o = Order(dve, order)
            o(nc.vector.tensor_tensor(v.o_tok, v.o_tok, v.gate.broadcast_to([P, TT, D]), ALU.mult))
            o(nc.vector.tensor_tensor(k.x, k.x, v.o_tok, ALU.add))


def block3(k, w, c, v):
    s = k.stream
    load_block3(k, w, v)
    s.stage("ada")
    modulation(k, v)
    normed_features(k, "norm_pre", k.x, k.h, lambda i: k.c_cols[:, 16 + i:17 + i],
                    lambda i: k.c_cols[:, 8 + i:9 + i])
    s.stage("in_lstm")
    causal_conv(k, "qk_conv", v.qk_pad, v.qk, QK_CONV, "conv", silu_bias=lambda i: column(k, "mlstm_conv_b_3", i))
    mlstm(k, v)
    feature_norm(k, "mlstm_norm", v.ya, LSTM_HEADS, 2, v.ya, v.squares_a, 1e-5, center=True,
                 gain=lambda i: column(k, "mlstm_norm_3", i), gate=v.ao)
    s.stage("in_conv")
    glu_input(k, v)
    causal_conv(k, "conformer_conv", v.u_pad, v.u, CONF_K, "dw", bias=lambda i: column(k, "conf_dw_b_3", i))
    feature_norm(k, "conformer_norm", v.u, 1, 8, v.yb, v.squares_b, 1e-5, center=True, silu=True,
                 gain=lambda i: column(k, "conf_ln_g_3", i), shift=lambda i: column(k, "conf_ln_b_3", i), gate=v.bz)
    s.stage("in_sparse")
    compression_blocks(k, w, v)
    s.stage("compress")
    compressed_keys(k, v)
    causal = k.causal[:, :].rearrange("p (t n) -> p t n", t=TT)
    cmp_mask = k.cmp_mask[:, :].rearrange("p (t n) -> p t n", t=TT)
    groups = []
    for h in range(NSA_HEADS):
        g, q = h // (NSA_HEADS // NSA_GROUPS), v.cq[:, h, :]
        us = [unit([(q, v.kc[:, 0, g * N_CMP:(g + 1) * N_CMP])], lambda b, g=g: v.vc[0:N_CMP, g, :], P ** -0.5,
                   mask=cmp_mask, n=N_CMP, factor=v.g3[:, :, 3 * h], floor=True)]
        for i, (keys, vals) in enumerate(((v.ks, v.vs), (v.kw, v.vw))):
            us.append(unit([(q, keys[:, g, :])], lambda b, g=g, vals=vals: vals[:, b, g * P:(g + 1) * P], P ** -0.5,
                           mask=causal, factor=v.g3[:, :, 3 * h + 1 + i]))
        groups.append((us, 0, P, v.yc[:, h, :], v.cz[:, h, :]))
    attention(k, "sparse_attention", groups, v.work)
    s.stage("merge_gates")
    s.stage("branches")
    merge(k, v)
    s.stage("out_merged")
    load(k, "load_norm_post", [(k.rows[:, 0, :], w["norm_post_3"].flatten().partition_broadcast(P))])
    final_norm(k, v.o_tok, k.rows[:, 0, :], v.o_tok)
    add_gated(k, v)


AREA = 21250


def build(nc, w, c, out, parts=(1, 2, 3)):
    k = Fields()
    k.nc = nc

    def sb(name, shape, dt=F32):
        return nc.alloc_sbuf_tensor(name, shape, dt)

    k.ring = sb("ring", [P, SLOTS, SLOT])
    k.w_hi, k.w_lo = sb("w_hi", [P, 2, SLOT // 2], F32R), sb("w_lo", [P, 2, SLOT // 2], F32R)
    k.x, k.xn = sb("x_tokens", [P, TT, D])[:, :, :], sb("xn", [P, TT, D])[:, :, :]
    k.h = (sb("h_hi", [P, DC, S], F32R)[:, :, :], sb("h_lo", [P, DC, S], F32R)[:, :, :])
    base = nc.sbuf_base
    arena = sb("arena", [P, AREA])

    def pair_part(name, at, chunks):
        return nc.alloc_sbuf_tensor_at(name, [P, chunks, S], F32R, offset=arena_base + at * 4)[:, :, :]
    arena_base = -(-base // 32) * 32
    k.pair_part = pair_part
    k.area = lambda at, chunks, n=S: arena[:, at:at + chunks * n].rearrange("p (c n) -> p c n", c=chunks)
    k.ident, k.ones, k.upper = sb("ident", [P, P]), sb("ones", [P, P]), sb("upper", [P, P])
    k.pair_rot, k.half_rot = sb("pair_rot", [P, P]), sb("half_rot", [P, P])
    k.ones_n, k.causal, k.freq = sb("ones_n", [P, P]), sb("causal", [P, TT * S]), sb("freq", [P, 3])
    k.cmp_mask, k.experts = sb("cmp_mask", [P, TT * 15]), sb("experts", [P, 8])[:, :]
    k.cols, k.rows = sb("cols", [P, 640]), k.xn
    k.norm_row = k.xn.rearrange("p t n -> p (t n)")
    k.stat, k.soft = sb("stat", [P, 8]), sb("soft", [P, 2, 8])[:, :, :]
    k.small, k.small_u = sb("small", [P, 64]), sb("small_u", [P, 16], U32)
    k.eps_cols, k.ones_row, k.neg_lam = sb("eps_cols", [P, 2]), sb("ones_row", [1, P]), sb("neg_lam", [P, TT])
    k.eps = lambda e: k.eps_cols[:, 0:1] if e == 1e-6 else k.eps_cols[:, 1:2]
    k.lam_in = k.xn[:, 0, 0:256].rearrange("p (i n) -> p i n", i=4)
    k.logits, k.expert_weights = sb("logits", [P, TT, 8])[:, :, :], sb("expert_weights", [P, TT, 8])[:, :, :]
    k.pos = sb("positions", [P, S], I32)
    k.c_cols, k.lstm = sb("c_cols", [P, 24]), sb("lstm", [P, 56])
    k.i_f, k.g3 = sb("i_f", [P, TT, 8])[:, :, :], sb("g3", [P, TT, 24])[:, :, :]
    k.ps = nc.alloc_psum_tensor("ps", [P, 8, 512], F32)
    k.panel_used = nc.alloc_semaphore("panel_used")
    k.panel_loaded = [nc.alloc_semaphore(f"panel_loaded{i}") for i in range(SLOTS)]
    k.hi_ready, k.lo_ready = nc.alloc_semaphore("hi_ready"), nc.alloc_semaphore("lo_ready")
    k.first_half_used = nc.alloc_semaphore("first_half_used")
    k.group_read = [nc.alloc_semaphore(f"group_read{i}") for i in range(SLOTS)]
    k.stream = Stream(k)

    v1 = plan_block1(k, w)
    v2 = plan_block2(k, w) if 2 in parts else None
    v3 = plan_block3(k, w) if 3 in parts else None
    if 1 not in parts:
        k.stream = Stream(k)
        v2 = plan_block2(k, w) if 2 in parts else None
        v3 = plan_block3(k, w) if 3 in parts else None
    assert nc.sbuf_base >= arena_base + 4 * AREA
    setup(k, w, c, v1)
    if 1 in parts:
        block1(k, w, c, v1)
    if 2 in parts:
        block2(k, w, c, v2)
    if 3 in parts:
        block3(k, w, c, v3)

    stored = nc.alloc_semaphore("stored")
    with stage(k, "store") as st:
        @st.block.sync
        def _(sp):
            sp.dma_start(out.rearrange("(t p) d -> p t d", p=P), k.x).then_inc(stored, 16)
            sp.wait_ge(stored, 16)


def laid_out(name, a):
    a = np.ascontiguousarray(a)
    if name in ("x", "mem"):
        return a.reshape(S, D)
    if name in ("moe_w_gate_up", "moe_w_down"):
        return a.reshape(a.shape[1:])
    if name.startswith("dense_w"):
        return a
    if a.ndim >= 3:
        return a.reshape(a.shape[1:])
    return a


def kernel(**inputs):
    import concourse.bacc as bacc
    from concourse.bass_utils import run_bass_kernel_spmd

    nc = bacc.Bacc("TRN2", target_bir_lowering=False, num_devices=1)
    arrays, w, c = {}, {}, {}
    for name, a in inputs.items():
        if name == "b_lb_logits":
            continue
        a = laid_out(name, a)
        arrays[f"in_{name}"] = a
        w[name] = nc.dram_tensor(f"in_{name}", a.shape, mybir.dt.from_np(a.dtype), kind="ExternalInput").ap()
    for name, a in constant_arrays().items():
        arrays[f"const_{name}"] = a
        c[name] = nc.dram_tensor(f"const_{name}", a.shape, F32, kind="ExternalInput").ap()
    out = nc.dram_tensor("out", [S, D], F32, kind="ExternalOutput").ap()
    build(nc, w, c, out)
    r = run_bass_kernel_spmd(nc, [arrays], core_ids=[0])
    return r.results[0]["out"].reshape(1, S, D)
```

```python
from contextlib import ExitStack, contextmanager

import numpy as np

import concourse.bass as bass
from concourse import mybir

F32 = mybir.dt.float32
F32R = mybir.dt.float32r
I32 = mybir.dt.int32
U32 = mybir.dt.uint32
ACT = mybir.ActivationFunctionType
ALU = mybir.AluOpType
AX_X = mybir.AxisListType.X
ds = bass.ds

P = 128
S = 256
TT = S // P
D = 1024
DC = D // P
SLOTS = 3
SLOT = 4096
STAGE_SEMS = range(190, 232)
NEG = -1e30


def alibi_slopes(n):
    return 2.0 ** (-8.0 * np.arange(1, n + 1) / n)


def constant_arrays():
    t = np.arange(S)
    c = {}
    c["ident"] = np.eye(P)
    c["upper"] = np.triu(np.ones((P, P)))
    c["ones"] = np.ones((P, P))

    def token_major(m):
        return m.reshape(TT, P, -1).transpose(1, 0, 2)

    causal = np.where(t[None, :] <= t[:, None], 0.0, NEG)
    c["causal"] = token_major(causal)
    allowed = (t[None, :] // 64) <= (t[:, None] // 64)
    dist = np.abs(t[:, None] - t[None, :]).astype(np.float32)
    biases = [np.where(allowed, -np.float32(s) * dist, NEG) for s in alibi_slopes(6)]
    c["alibi"] = np.stack([np.concatenate([b[P:, :], b[:P, :P]], 1) for b in biases], 1)
    rel = (t[None, :] - t[:, None]).astype(np.float64)
    log_g = np.log(1.0 - 2.0 ** (-5.0 - np.arange(4)))
    c["decay"] = np.stack([token_major(np.where(rel >= 0, np.exp(g * np.maximum(rel, 0)) / 16.0, 0.0))
                           for g in log_g], 1)
    j, tt = np.arange(P)[:, None], np.arange(P)[None, :]
    sums, masks = [np.where(j > tt, 1.0, 0.0)], []
    for half in (64, 32, 16, 8, 4, 2, 1):
        mid = (tt // (2 * half)) * 2 * half + half
        sums.append(np.where(tt >= mid, (j >= mid) & (j <= tt), (j > tt) & (j < mid)))
        s_, t_ = np.arange(P)[:, None], np.arange(P)[None, :]
        masks.append((s_ // (2 * half) == t_ // (2 * half)) & (s_ % (2 * half) < half) & (t_ % (2 * half) >= half))
    sums.append(np.where(j <= tt, 1.0, 0.0))
    masks.append(np.eye(P))
    c["levels"] = np.stack(sums, 1)
    c["level_masks"] = np.stack(masks, 1)
    pair = np.zeros((P, P))
    for i in range(0, P, 2):
        pair[i, i + 1], pair[i + 1, i] = -1.0, 1.0
    half = np.zeros((P, P))
    for b in (0, 64):
        for i in range(32):
            half[b + i, b + 32 + i], half[b + 32 + i, b + i] = -1.0, 1.0
    c["pair_rot"], c["half_rot"] = pair.T, half.T
    lin = np.linspace(0.0, 1.0, P, dtype=np.float32)
    ret = (np.float32(1.0) / (np.float32(10000.0) ** lin)).astype(np.float32)
    ang = (np.float32(1.0) / np.float32(10000.0) ** (np.arange(0, 64, 2, dtype=np.float32) / np.float32(64))
           ).astype(np.float32)
    c["freq"] = np.stack([np.repeat(ret[:64], 2), np.repeat(ret[64:], 2), np.tile(ang, 4)], 1)
    n_cmp = S // 16 - 1
    end = np.arange(n_cmp) * 16 + 31
    c["cmp_mask"] = token_major(np.where(end[None, :] <= t[:, None], 0.0, NEG))
    c["experts"] = np.tile(np.arange(8.0), (P, 1))
    return {k: np.ascontiguousarray(v.reshape(v.shape[0], -1), dtype=np.float32) for k, v in c.items()}


def column_table():
    rows, at = [], {}

    def add(key, name, offset, n):
        at[key] = sum(r[2] for r in rows)
        rows.append((name, offset, n))

    for key, n in (("a_norm_mix", 8), ("a_mem_norm", 8), ("b_norm_mix", 8), ("b_mem_norm", 8), ("dense_norm", 8),
                   ("moe_norm", 8), ("a_subln", 1), ("b_out_norm", 1), ("q_norm_even_2", 2), ("kv_norm_even_2", 2),
                   ("norm_pre_3", 8), ("mlstm_norm_3", 8), ("conf_ln_g_3", 8), ("conf_ln_b_3", 8),
                   ("conf_dw_b_3", 8), ("mlstm_conv_b_3", 16)):
        add(key, key, 0, n)
    add("shift", "b_ada_3", 0, 8)
    add("scale", "b_ada_3", 1024, 8)
    for key, off, n in (("qk", 0, 16), ("ao", 3072, 8), ("az", 4096, 8), ("ba", 5128, 8), ("bb", 6152, 8),
                        ("bz", 7176, 8), ("cq", 8200, 8), ("ckc", 9224, 2), ("cvc", 9480, 2), ("cks", 9736, 2),
                        ("ckw", 10248, 2), ("cz", 10784, 8), ("mg", 11808, 24)):
        add(key, "b_in_3", off, n)
    add("conv", "mlstm_conv_w_3", 0, 64)
    add("pe", "nsa_cmp_pe_3", 0, 64)
    add("dw", "conf_dw_w_3", 0, 248)
    return rows, at


COLUMN_ROWS, COL = column_table()
N_COLS = sum(r[2] for r in COLUMN_ROWS)


class Fields:
    pass


class Order:

    def __init__(self, eng, sem):
        self.eng, self.sem, self.n = eng, sem, 0

    def __call__(self, instruction):
        instruction.then_inc(self.sem, 1)
        self.n += 1
        self.eng.wait_ge(self.sem, self.n)


class Stage:

    def __init__(self, nc, block, stack):
        self.nc, self.block, self.stack, self.n = nc, block, stack, 0

    def sem(self, name):
        s = self.stack.enter_context(self.nc.semaphore(name, num=STAGE_SEMS[self.n]))
        self.n += 1
        return s


@contextmanager
def stage(k, name):
    nc = k.nc
    with ExitStack() as stack:
        with nc.Block(no_gpsimd_drain=True) as block:
            st = Stage(nc, block, stack)
            st.name = name
            yield st
        if st.n:
            nc.all_engine_barrier(sems_to_clear=range(STAGE_SEMS[0], STAGE_SEMS[0] + st.n))


def run(kind, w, c0, src, evict, on="act", count=1, width=512, nk=DC, k0=0, acc=1, n=S, tiles=TT,
        rows=P, loads=None, bias=None, pieces=None, source=None):
    half = nk // 2

    def whole(p):
        def part(a, b):
            rows = w[(k0 + a) * P:(k0 + b) * P, :].rearrange("(k p) c -> p k c", p=P)
            cols = c0 + p * width
            return (lambda slot: slot[:, a * width:b * width].rearrange("p (k c) -> p k c", k=b - a),
                    rows[:, :, ds(cols, width)])
        return [part(0, half), part(half, nk)]

    r = Fields()
    r.source = source or (src if callable(src) else lambda p: src)
    r.kind, r.src, r.evict, r.on, r.count, r.width, r.nk = kind, src, evict, on, count, width, nk
    r.acc, r.n, r.tiles, r.rows, r.loads, r.bias = acc, n, tiles, rows, loads or whole, bias
    r.split = isinstance(src, tuple)
    r.parts = (2 if width >= 2 * P else 1) if r.split else 0
    r.per_turn = SLOTS
    w_ = width // max(r.parts, 1)
    grid = lambda slot: slot[:, 0:nk * width].rearrange("p (k c) -> p k c", k=nk)
    r.by_rows = r.split and kind == "T" and r.parts == 2
    if r.by_rows:
        r.part_view = lambda slot, p, h: grid(slot)[:, h * (nk // 2):(h + 1) * (nk // 2), :]
        r.part_shape = lambda p: (nk // 2, width)
    else:
        r.part_view = lambda slot, p, h: grid(slot)[:, :, h * w_:(h + 1) * w_]
        r.part_shape = lambda p: (nk, w_)
    r.pieces = pieces
    return r


def grouped_loads(w, nk, outer, inner, pick):
    def loads(p):
        out = []
        for kk in range(nk):
            rows = pick(w[kk * P:(kk + 1) * P, :], p)
            out.append((lambda slot, kk=kk: slot[:, kk * outer * inner:(kk + 1) * outer * inner]
                        .rearrange("p (g c) -> p g c", g=outer), rows))
        return out
    return loads


def nonzero(value):
    return not isinstance(value, int) or value > 0


class Stream:

    def __init__(self, k):
        self.k = k
        self.jobs = []
        self.starts = []
        self.flat = []
        self.groups = self.halves = self.pairs = 0
        self.at = 0

    def add(self, runs):
        self.jobs.append(runs)
        self.starts.append(len(self.flat))
        for r in runs:
            r.first, r.group, r.halves, r.pairs = len(self.flat), self.groups, self.halves, self.pairs
            self.flat += [(r, p) for p in range(r.count)]
            self.groups += r.count // r.acc if r.kind != "experts" else 0
            self.halves += r.count * r.parts
            self.pairs += r.count * (r.parts == 2)

    def place(self, r, i, j):
        m, per = Fields(), r.per_turn
        m.r, m.j, m.i = r, j, i
        m.p = i * per + j
        m.number = i * per + (r.first + j)
        m.slot = (r.first + j) % SLOTS
        m.uses = i * (per // SLOTS) + (r.first + j) // SLOTS
        group = r.group + j // r.acc
        m.bank, m.before = group % SLOTS, i + group // SLOTS
        m.halves = i * (per * r.parts) + (r.halves + j * r.parts)
        m.pairs = i * (per * (r.parts == 2)) + (r.pairs + j * (r.parts == 2))
        return m

    def load(self, sp, r, i, j):
        m = self.place(r, i, j)
        if nonzero(m.uses):
            sp.wait_ge(self.k.panel_used, m.number - (SLOTS - 1))
        for dst, src in (r.loads(m.p) if r.kind != "experts" else r.expert_loads(i + j // r.per_turn, j % r.per_turn)):
            sp.dma_start(dst(self.k.ring[:, m.slot, :]), src).then_inc(self.k.panel_loaded[m.slot], 16)

    def load_range(self, sp, a, b):
        while a < b:
            r, p = self.flat[a]
            n = min(r.count - p, b - a)
            trips = n // r.per_turn if n >= 2 * r.per_turn and a >= SLOTS else 0
            if trips:
                with sp.Fori(0, trips) as i:
                    for j in range(r.per_turn):
                        self.load(sp, r, i, p + j)
            for m in range(trips * r.per_turn, n):
                self.load(sp, r, 0, p + m)
            a += n

    def ahead(self, sp):
        i = self.at
        nxt = self.starts[i + 1] if i + 1 < len(self.starts) else len(self.flat)
        self.load_range(sp, self.starts[i] + SLOTS, min(nxt + SLOTS, len(self.flat)))

    def round_weights(self, act, m, halves=(0, 1)):
        k = self.k
        for h in halves[0:m.r.parts]:
            if h == 0:
                act.wait_ge(k.panel_loaded[m.slot], (m.uses + 1) * 32)
            if h == 0 and m.r.parts == 2:
                if nonzero(m.pairs):
                    act.wait_ge(k.first_half_used, m.pairs)
            elif nonzero(m.number):
                act.wait_ge(k.panel_used, m.number)
            b = h + 2 - m.r.parts
            src = m.r.part_view(k.ring[:, m.slot, :], m.j, h)
            k.nc.scalar.activation(self.part(k.w_hi, b, m), src, ACT.Copy).then_inc(k.hi_ready, 1)

    def rest_of_weights(self, dve, m, halves=(0, 1)):
        k = self.k
        for h in halves[0:m.r.parts]:
            dve.wait_ge(k.hi_ready, m.halves + (h + 1))
            b = h + 2 - m.r.parts
            src = m.r.part_view(k.ring[:, m.slot, :], m.j, h)
            k.nc.vector.tensor_tensor(self.part(k.w_lo, b, m), src, self.part(k.w_hi, b, m).bitcast(F32),
                                      ALU.subtract).then_inc(k.lo_ready, 1)

    def part(self, tensor, b, m):
        nk, width = m.r.part_shape(m.j)
        return tensor[:, b, 0:nk * width].rearrange("p (k c) -> p k c", k=nk)

    def each(self, eng, r, body):
        trips = r.count // SLOTS if r.count >= 2 * SLOTS and r.acc == 1 and r.group >= SLOTS else 0
        if trips:
            with eng.Fori(0, trips) as i:
                for j in range(SLOTS):
                    body(self.place(r, i, j))
        for p in range(trips * SLOTS, r.count):
            body(self.place(r, 0, p))

    def begins_early(self, i):
        return 0 < i < len(self.jobs) and self.jobs[i][0].parts == 2

    def open_stage(self, prepare):
        prepare(self.place(self.jobs[self.at][0], 0, 0), (1,) if self.begins_early(self.at) else (0, 1))

    def first_of_next(self, prepare):
        if self.begins_early(self.at + 1):
            prepare(self.place(self.jobs[self.at + 1][0], 0, 0), (0,))

    def each_with_next(self, eng, runs, prepare, body, side):
        for step in side.get(0, ()):
            step()
        self.open_stage(prepare)
        for step in side.get(1, ()):
            step()
        for n, r in enumerate(runs):
            trips = (r.count - 1) // SLOTS if r.count > 2 * SLOTS and r.acc == 1 and r.group >= SLOTS else 0
            if side:
                trips = 0
            if trips:
                with eng.Fori(0, trips) as i:
                    for j in range(SLOTS):
                        prepare(self.place(r, i, j + 1))
                        body(self.place(r, i, j))
            for p in range(trips * SLOTS, r.count):
                if p + 1 < r.count:
                    prepare(self.place(r, 0, p + 1))
                elif n + 1 < len(runs):
                    prepare(self.place(runs[n + 1], 0, 0))
                else:
                    self.first_of_next(prepare)
                body(self.place(r, 0, p))
                for step in side.get(r.first - runs[0].first + p + 2, ()):
                    step()

    def products(self, pe, m):
        k, nc, r = self.k, self.k.nc, m.r
        begins, ends = m.j % r.acc == 0, m.j % r.acc == r.acc - 1
        if not r.split:
            pe.wait_ge(k.panel_loaded[m.slot], (m.uses + 1) * 32)
        if begins and nonzero(m.before):
            pe.wait_ge(k.group_read[m.bank], m.before)
        src = r.source(m.p)
        nk, width = r.part_shape(m.j)
        for h in range(max(r.parts, 1)):
            if r.split:
                pe.wait_ge(k.lo_ready, m.halves + (h + 1))
                b = h + 2 - r.parts
                w_hi, w_lo = self.part(k.w_hi, b, m), self.part(k.w_lo, b, m)
                passes = ((w_hi, src[0]), (w_hi, src[1]), (w_lo, src[0])) if r.kind == "F" else \
                    ((w_hi, src[0]), (w_lo, src[0]), (w_hi, src[1]))
            else:
                passes = ((k.ring[:, m.slot, 0:nk * width].rearrange("p (k c) -> p k c", k=nk), src),)
            for o in range(width // P if r.kind == "F" else r.tiles):
                if r.kind == "F":
                    at = (h * (width // P) + o) * (r.n if r.acc == 1 else 512)
                    out = k.ps[:, 2 * m.bank + at // 512, at % 512:at % 512 + r.n]
                else:
                    at = 0 if r.by_rows else h * width
                    out = k.ps[0:r.rows, 2 * m.bank + o, at:at + width]
                first_row = h * nk if r.by_rows else 0
                opens = begins and not (r.by_rows and h == 1)
                closes = ends and not (r.by_rows and h == 0)
                for c in range(nk):
                    if r.pieces and m.j < 2 * r.acc and h in (0, r.by_rows) and o == 0 and (first_row + c) % 4 == 0:
                        pe.wait_ge(self.source_split, 2 * r.pieces(m.j) + min(first_row + c, 4) // 4 + 1)
                    for i, (w, x) in enumerate(passes):
                        if r.kind == "F":
                            lhs, rhs = w[:, c, o * P:(o + 1) * P], x[:, c, :]
                        else:
                            lhs, rhs = x[:, first_row + c, o * P:o * P + r.rows], w[:, c, :]
                        last = nc.tensor.matmul(out, lhs, rhs, start=(opens and c == 0 and i == 0),
                                                stop=(closes and c == nk - 1 and i == len(passes) - 1
                                                      and r.bias is None))
                if r.bias is not None and closes:
                    row = r.bias(m.p)[:, at:at + width]
                    last = nc.tensor.matmul(out, k.ones_row[0:1, 0:P], row, start=False, stop=True)
            if h == 0 and r.parts == 2:
                last.then_inc(k.first_half_used, 1)
        last.then_inc(k.panel_used, 1)

    def stage(self, name, side=None, extra=(), source=()):
        k, nc, runs = self.k, self.k.nc, self.jobs[self.at]

        def evict(eng, m, which):
            r = m.r
            if r.on == which and m.j % r.acc == r.acc - 1:
                eng.wait_ge(k.panel_used, m.number + 1)
                q = m.p if r.acc == 1 else m.j // r.acc
                r.evict(nc, k.ps[:, 2 * m.bank:2 * m.bank + 2, :], q).then_inc(k.group_read[m.bank], 1)

        with stage(k, name) as st:
            extra_loaded = st.sem("extra_loaded") if extra else None
            steps = side(st) if side else {}
            if source:
                source_high = st.sem("source_high")
                self.source_split = st.sem("source_split")
                steps = {"act": {q: [lambda q=q: high_parts(q)] for q in range(len(source))},
                         "dve": {q: [lambda q=q: low_parts(q)] for q in range(len(source))}}

            def quads(q):
                return [(i, slice(4 * i, min(4 * i + 4, source[q][0].shape[1]))) for i in range(2)]

            def high_parts(q):
                values, high, _ = source[q]
                for i, at in quads(q):
                    if at.start < values.shape[1]:
                        nc.scalar.activation(high[:, at, :], values[:, at, :], ACT.Copy).then_inc(source_high, 1)

            def low_parts(q):
                values, high, low = source[q]
                for i, at in quads(q):
                    if at.start < values.shape[1]:
                        nc.vector.wait_ge(source_high, 2 * q + i + 1)
                        nc.vector.tensor_tensor(low[:, at, :], values[:, at, :], high[:, at, :].bitcast(F32),
                                                ALU.subtract).then_inc(self.source_split, 1)

            @st.block.sync
            def _(sp):
                for dst, src in extra:
                    sp.dma_start(dst, src).then_inc(extra_loaded, 16)
                self.ahead(sp)
                if extra:
                    sp.wait_ge(extra_loaded, 16 * len(extra))

            @st.block.tensor
            def _(pe):
                beside = steps.get("pe")
                for r in runs:
                    if not beside:
                        self.each(pe, r, lambda m: self.products(pe, m))
                        continue
                    for p in range(r.count):
                        self.products(pe, self.place(r, 0, p))
                        for step in beside.get(r.first - runs[0].first + p + 2, ()):
                            step()

            @st.block.scalar
            def _(act):
                self.each_with_next(act, runs, lambda m, halves=(0, 1): self.round_weights(act, m, halves),
                                    lambda m: evict(act, m, "act"), steps.get("act", {}))

            @st.block.vector
            def _(dve):
                self.each_with_next(dve, runs, lambda m, halves=(0, 1): self.rest_of_weights(dve, m, halves),
                                    lambda m: evict(dve, m, "dve"), steps.get("dve", {}))

            if "pool" in steps:
                @st.block.gpsimd
                def _(pool):
                    for step in steps["pool"]:
                        step()

        self.at += 1


def to_features(dst, c0=0, func=ACT.Copy, chunks=4, bias=None, scale=1.0):
    def evict(nc, banks, p):
        flat = banks.rearrange("p b n -> p (b n)")
        if bias is None:
            return nc.scalar.activation(dst[:, ds(p * 4 + c0, chunks), :].rearrange("p c n -> p (c n)"),
                                        flat[:, 0:chunks * dst.shape[2]], func, scale=scale)
        n = dst.shape[2]
        for c in range(chunks):
            last = nc.scalar.activation(dst[:, ds(p * 4 + (c0 + c), 1), :].rearrange("p c n -> p (c n)"),
                                        flat[:, c * n:(c + 1) * n], func, bias=bias(p * 4 + c))
        return last
    return evict


def to_tokens(dst, f0=0, width=512):
    def evict(nc, banks, p):
        return nc.scalar.activation(dst[:, :, ds(p * 512 + f0, width)], banks[:, :, 0:width], ACT.Copy)
    return evict


def add_to_residual(x, alpha=None):
    def evict(nc, banks, p):
        at = x[:, :, ds(p * 512, 512)]
        if alpha is None:
            return nc.vector.tensor_tensor(at, at, banks[:, :, :], ALU.add)
        return nc.vector.scalar_tensor_tensor(at, at, alpha, banks[:, :, :], ALU.mult, ALU.add)
    return evict


def column(k, key, c=0):
    return k.cols[:, COL[key] + c:COL[key] + c + 1]


def normed_features(k, name, x, out, gain=None, shift=None, eps=1e-6):
    nc = k.nc
    with stage(k, name) as st:
        squares_summed, mean_ready = st.sem("squares_summed"), st.sem("mean_ready")
        root_ready, scaled = st.sem("root_ready"), st.sem("scaled")
        transposed, dve_order = st.sem("transposed"), st.sem("dve_order")
        high_ready = st.sem("high_ready")
        y = k.xn if gain is not None else x
        split = isinstance(out, tuple)
        high = out[0] if split else out

        def chunk(c):
            return k.ps[:, c // 2, (c % 2) * S:(c % 2 + 1) * S]

        @st.block.scalar
        def _(act):
            if gain is not None:
                for t in range(TT):
                    squares = k.ps[:, 4 + 2 * t:6 + 2 * t, :].rearrange("p b n -> p (b n)")
                    last = nc.scalar.activation(squares, x[:, t, :], ACT.Square, accum_out=k.stat[:, t:t + 1])
                last.then_inc(squares_summed, 1)
                act.wait_ge(mean_ready, 1)
                nc.scalar.activation(k.stat[:, 4:6], k.stat[:, 2:4], ACT.Sqrt).then_inc(root_ready, 1)
            for c in range(DC):
                act.wait_ge(transposed, c // 2 + 1)
                if gain is None:
                    last = nc.scalar.activation(high[:, c, :], chunk(c), ACT.Copy)
                else:
                    last = nc.scalar.activation(high[:, c, :], chunk(c), ACT.Identity, scale=gain(c),
                                                bias=shift(c) if shift else 0.0)
                if c % 2:
                    last.then_inc(high_ready, 1)

        @st.block.vector
        def _(dve):
            o = Order(dve, dve_order)
            if gain is not None:
                dve.wait_ge(squares_summed, 1)
                nc.vector.tensor_scalar(k.stat[:, 2:4], k.stat[:, 0:2], 1.0 / D, eps, ALU.mult,
                                        ALU.add).then_inc(mean_ready, 1)
                dve.wait_ge(root_ready, 1)
                o(nc.vector.reciprocal(k.stat[:, 6:8], k.stat[:, 4:6]))
                for t in range(TT):
                    nc.vector.tensor_scalar(k.xn[:, t, :], x[:, t, :], k.stat[:, 6 + t:7 + t], None,
                                            ALU.mult).then_inc(scaled, 1)
            if not split:
                return
            for c in range(DC):
                dve.wait_ge(high_ready, c // 2 + 1)
                low, hi = out[1][:, c, :], out[0][:, c, :].bitcast(F32)
                if gain is None:
                    nc.vector.tensor_tensor(low, chunk(c), hi, ALU.subtract)
                elif shift is None:
                    nc.vector.scalar_tensor_tensor(low, chunk(c), gain(c), hi, ALU.mult, ALU.subtract)
                else:
                    o(nc.vector.tensor_scalar(chunk(c), chunk(c), gain(c), shift(c), ALU.mult, ALU.add))
                    nc.vector.tensor_tensor(low, chunk(c), hi, ALU.subtract)

        @st.block.tensor
        def _(pe):
            if gain is not None:
                pe.wait_ge(scaled, TT)
            for c in range(DC):
                for t in range(TT):
                    last = nc.tensor.transpose(k.ps[:, c // 2, (c % 2) * S + t * P:(c % 2) * S + (t + 1) * P],
                                               y[:, t, c * P:(c + 1) * P], k.ident[:, :])
                if c % 2:
                    last.then_inc(transposed, 1)


def feature_norm(k, name, x, heads, per, out, tmp, eps, pieces, center=False, gain=None, one_gain=None, shift=None,
                 gate=None):
    nc = k.nc
    with stage(k, name) as st:
        ones_ready, sums_ready = st.sem("ones_ready"), st.sem("sums_ready")
        centred, squared, squares_ready = st.sem("centred"), st.sem("squared"), st.sem("squares_ready")
        root_ready, dve_order, scaled = st.sem("root_ready"), st.sem("dve_order"), st.sem("scaled")
        silu_ready = st.sem("silu_ready")
        by_head = lambda y: y.rearrange("p (h g) n -> p h g n", h=heads)
        n = len(pieces)
        tokens = S if pieces[0][1] == (0, S) else P

        def of(y, p):
            (h0, h1), (t0, t1) = pieces[p]
            return by_head(y)[:, h0:h1, :, t0:t1]

        def sums(first_bank, p):
            (h0, h1), _ = pieces[p]
            return k.ps[:, first_bank + p % 2, 0:(h1 - h0) * tokens]

        def spread(row, p):
            (h0, h1), _ = pieces[p]
            return row.rearrange("p (h n) -> p h n", h=h1 - h0).unsqueeze(2).broadcast_to([P, h1 - h0, per, tokens])

        def root(p):
            (h0, h1), _ = pieces[p]
            return k.norm_row[:, (p % 2) * 512:(p % 2) * 512 + (h1 - h0) * tokens]

        @st.block.tensor
        def _(pe):
            pe.wait_ge(ones_ready, 1)

            def total(y, bank, p):
                (h0, h1), (t0, t1) = pieces[p]
                for h in range(h1 - h0):
                    for g in range(per):
                        last = nc.tensor.matmul(sums(bank, p)[:, h * tokens:(h + 1) * tokens], k.ones_n[:, :],
                                                y[:, (h0 + h) * per + g, t0:t1], start=(g == 0), stop=(g == per - 1))
                return last
            for s in range(n + 1):
                if s < n and center:
                    if s >= 2:
                        pe.wait_ge(centred, s - 1)
                    total(x, 0, s).then_inc(sums_ready, 1)
                if s >= 1:
                    pe.wait_ge(squared, s)
                    if s >= 3:
                        pe.wait_ge(root_ready, s - 2)
                    total(tmp, 4, s - 1).then_inc(squares_ready, 1)

        @st.block.scalar
        def _(act):
            for s in range(n + 1):
                if s < n:
                    if center:
                        act.wait_ge(centred, s + 1)
                    nc.scalar.activation(of(tmp, s), of(x, s), ACT.Square).then_inc(squared, 1)
                if s >= 1:
                    act.wait_ge(squares_ready, s)
                    if s >= 3:
                        act.wait_ge(scaled, s - 2)
                    nc.scalar.activation(root(s - 1), sums(4, s - 1), ACT.Sqrt,
                                         bias=k.eps(eps)).then_inc(root_ready, 1)
            if shift is not None:
                for p in range(n):
                    act.wait_ge(scaled, p + 1)
                    for c in range(heads * per):
                        t0, t1 = pieces[p][1]
                        last = nc.scalar.activation(tmp[:, c, t0:t1], x[:, c, t0:t1], ACT.Silu, scale=gain(c),
                                                    bias=shift(c))
                    last.then_inc(silu_ready, 1)

        @st.block.vector
        def _(dve):
            o = Order(dve, dve_order)

            def finish(p):
                (h0, h1), (t0, t1) = pieces[p]
                dve.wait_ge(root_ready, p + 1)
                o(nc.vector.reciprocal(root(p), root(p)))
                plain = gate is None and gain is None
                dst = of(out, p) if plain else of(x, p)
                if one_gain is None:
                    last = nc.vector.tensor_tensor(dst, of(x, p), spread(root(p), p), ALU.mult)
                else:
                    assert per == 1
                    h = h1 - h0
                    last = nc.vector.scalar_tensor_tensor(dst.rearrange("p h g n -> p (h g) n"),
                                                          of(x, p).rearrange("p h g n -> p (h g) n"), one_gain,
                                                          root(p).rearrange("p (h n) -> p h n", h=h), ALU.mult,
                                                          ALU.mult)
                last.then_inc(scaled, 1)
                if plain or shift is not None:
                    return
                dve.wait_ge(scaled, p + 1)
                if gain is None:
                    nc.vector.tensor_tensor(of(out, p), of(x, p), of(gate, p), ALU.mult)
                    return
                for c in range(h0 * per, h1 * per):
                    if gate is not None:
                        nc.vector.scalar_tensor_tensor(out[:, c, t0:t1], x[:, c, t0:t1], gain(c), gate[:, c, t0:t1],
                                                       ALU.mult, ALU.mult)
                    else:
                        nc.vector.tensor_scalar(out[:, c, t0:t1], x[:, c, t0:t1], gain(c), None, ALU.mult)

            nc.vector.tensor_scalar(k.ones_n[:, :], k.ones[:, :], 1.0 / (per * P), None,
                                    ALU.mult).then_inc(ones_ready, 1)
            for s in range(n + 1):
                if s < n and center:
                    dve.wait_ge(sums_ready, s + 1)
                    nc.vector.tensor_tensor(of(x, s), of(x, s), spread(sums(0, s), s), ALU.subtract).then_inc(centred, 1)
                if s >= 1:
                    if center:
                        dve.wait_ge(centred, s)
                    finish(s - 1)
            if shift is not None:
                for p in range(n):
                    dve.wait_ge(silu_ready, p + 1)
                    nc.vector.tensor_tensor(of(out, p), of(tmp, p), of(gate, p), ALU.mult)


WHOLE = (0, S)


def unit(scores, values, scale=1.0, mask=None, causal=False, n=S, factor=None, floor=False):
    u = Fields()
    u.scores, u.values, u.scale, u.mask, u.n, u.factor, u.floor = scores, values, scale, mask, n, factor, floor
    u.causal = causal
    u.tiles = [(1, 0, S), (0, S, P)] if causal else [(0, 0, n), (1, S, n)]
    u.blocks = [(0, P, 0, 0), (1, P, P, S)] if causal else \
        [(b, min(P, n - b * P), 0, b * S) for b in range(-(-n // P))]
    u.width = S + P if causal else len(u.blocks) * S
    return u


def attention(k, name, groups, work):
    nc = k.nc
    units = []
    for g, (us, r0, dv, dst, gate) in enumerate(groups):
        for i, u in enumerate(us):
            units.append((u, g, i == 0, i == len(us) - 1))
    n_units = len(units)
    exps = k.xn.rearrange("p t (c n) -> p (t c) n", n=2 * S)
    exps_t = work[:, 0:4, :].rearrange("p (b s) n -> p b (s n)", b=2)
    diagonals = work[:, 4:6, :].rearrange("p b (t n) -> p b t n", t=TT)
    score_banks = (0, 1, 6)

    with stage(k, name) as st:
        scores_ready, neg_max_ready, exp_done = st.sem("scores_ready"), st.sem("neg_max_ready"), st.sem("exp_done")
        norms_ready, transposed, pt_ready = st.sem("norms_ready"), st.sem("transposed"), st.sem("pt_ready")
        values_done, out_read, dve_order = st.sem("values_done"), st.sem("out_read"), st.sem("dve_order")

        def scores_of(s):
            return k.ps[:, score_banks[s % 3], :]

        @st.block.tensor
        def _(pe):
            for s in range(n_units + 3):
                if s < n_units:
                    u = units[s][0]
                    if s >= 3:
                        pe.wait_ge(exp_done, s - 2)
                    for t, at, n in u.tiles:
                        for i, (q, key) in enumerate(u.scores):
                            last = nc.tensor.matmul(scores_of(s)[:, at:at + n], q[:, t * P:(t + 1) * P], key[:, 0:n],
                                                    start=(i == 0), stop=(i == len(u.scores) - 1))
                    last.then_inc(scores_ready, 1)
                if 2 <= s <= n_units + 1:
                    m = s - 2
                    u = units[m][0]
                    pe.wait_ge(norms_ready, m + 1)
                    if m >= 2:
                        pe.wait_ge(pt_ready, m - 1)
                    for b, rows, first_token, to in u.blocks:
                        for t, at, n in sorted(u.tiles):
                            if t * P >= first_token:
                                last = nc.tensor.matmul(
                                    k.ps[0:rows, 2 + m % 2, to + t * P - first_token:to + (t + 1) * P - first_token],
                                    exps[:, m % 4, at + b * P:at + b * P + rows], diagonals[:, m % 2, t, :],
                                    start=True, stop=True)
                    last.then_inc(transposed, 1)
                if s >= 3:
                    m = s - 3
                    u, g, first, is_last = units[m]
                    _, r0, dv, _, _ = groups[g]
                    pe.wait_ge(pt_ready, m + 1)
                    if first and g >= 2:
                        pe.wait_ge(out_read, g - 1)
                    for b, rows, first_token, to in u.blocks:
                        last = nc.tensor.matmul(k.ps[r0:r0 + dv, 4 + g % 2, first_token:S], u.values(b),
                                                exps_t[0:rows, m % 2, to:to + S - first_token],
                                                start=(first and b == 0),
                                                stop=(is_last and b == u.blocks[-1][0]))
                    last.then_inc(values_done, 1)

        @st.block.vector
        def _(dve):
            o = Order(dve, dve_order)

            def masked_max(s):
                u = units[s][0]
                dve.wait_ge(scores_ready, s + 1)
                if s >= 2:
                    dve.wait_ge(exp_done, s - 1)
                bank, top = scores_of(s), k.soft[:, s % 2, 0:2]
                grid = bank.rearrange("p (t n) -> p t n", t=TT)[:, :, 0:u.n]
                if u.causal and u.mask.shape[1] == P:
                    diagonal = bank[:, P:3 * P].rearrange("p (t n) -> p t n", t=TT)
                    o(nc.vector.tensor_tensor(diagonal, diagonal, u.mask.unsqueeze(1).broadcast_to([P, TT, P]),
                                              ALU.add))
                elif u.causal:
                    o(nc.vector.tensor_tensor(bank[:, 0:u.width], bank[:, 0:u.width], u.mask, ALU.add))
                elif u.mask is not None:
                    o(nc.vector.tensor_tensor(grid, grid, u.mask, ALU.add))
                plain = u.scale == 1.0 and not u.floor
                if u.causal:
                    for t, at, n in u.tiles:
                        last = nc.vector.tensor_reduce(top[:, t:t + 1], bank[:, at:at + n], AX_X, ALU.max,
                                                       negate=plain)
                        if t == 1 and not plain:
                            o(last)
                else:
                    last = nc.vector.tensor_reduce(top, grid, AX_X, ALU.max, negate=plain)
                if not plain:
                    o(last)
                    if u.floor:
                        last = nc.vector.tensor_scalar(top, top, -1e20, -u.scale, ALU.max, ALU.mult)
                    else:
                        last = nc.vector.tensor_scalar(top, top, -u.scale, None, ALU.mult)
                last.then_inc(neg_max_ready, 1)

            def norms(m):
                u = units[m][0]
                soft = k.soft[:, m % 2, :]
                dve.wait_ge(exp_done, m + 1)
                if u.floor:
                    o(nc.vector.tensor_scalar(soft[:, 4:6], soft[:, 4:6], 1e-30, None, ALU.max))
                o(nc.vector.reciprocal(soft[:, 6:8], soft[:, 4:6]))
                if u.factor is not None:
                    o(nc.vector.tensor_tensor(soft[:, 6:8], soft[:, 6:8], u.factor, ALU.mult))
                if m >= 2:
                    dve.wait_ge(transposed, m - 1)
                for t in range(TT):
                    last = nc.vector.tensor_scalar(diagonals[:, m % 2, t, :], k.ident[:, :], soft[:, 6 + t:7 + t],
                                                   None, ALU.mult)
                last.then_inc(norms_ready, 1)

            def outputs(m):
                u, g, _, is_last = units[m]
                if is_last and groups[g][4] is not None:
                    _, r0, dv, dst, gate = groups[g]
                    dve.wait_ge(values_done, m + 1)
                    nc.vector.tensor_tensor(dst, k.ps[r0:r0 + dv, 4 + g % 2, 0:S], gate,
                                            ALU.mult).then_inc(out_read, 1)

            for s in range(n_units + 4):
                if s < n_units:
                    masked_max(s)
                if 1 <= s <= n_units:
                    norms(s - 1)
                if s >= 4:
                    outputs(s - 4)

        @st.block.scalar
        def _(act):
            for s in range(n_units + 4):
                if s < n_units:
                    u = units[s][0]
                    act.wait_ge(neg_max_ready, s + 1)
                    if s >= 4:
                        act.wait_ge(transposed, s - 3)
                    if s >= 2:
                        act.wait_ge(norms_ready, s - 1)
                    for t, at, n in u.tiles:
                        last = nc.scalar.activation(exps[:, s % 4, at:at + n], scores_of(s)[:, at:at + n], ACT.Exp,
                                                    bias=k.soft[:, s % 2, t:1 + t], scale=u.scale,
                                                    accum_out=k.soft[:, s % 2, 4 + t:5 + t])
                    last.then_inc(exp_done, 1)
                if 2 <= s <= n_units + 1:
                    m = s - 2
                    u = units[m][0]
                    act.wait_ge(transposed, m + 1)
                    if m >= 2:
                        act.wait_ge(values_done, m - 1)
                    rows = min(P, u.n)
                    nc.scalar.activation(exps_t[0:rows, m % 2, 0:u.width], k.ps[0:rows, 2 + m % 2, 0:u.width],
                                         ACT.Copy).then_inc(pt_ready, 1)
                if s >= 4:
                    m = s - 4
                    u, g, _, is_last = units[m]
                    if is_last and groups[g][4] is None:
                        _, r0, dv, dst, _ = groups[g]
                        act.wait_ge(values_done, m + 1)
                        nc.scalar.activation(dst, k.ps[r0:r0 + dv, 4 + g % 2, 0:S], ACT.Copy).then_inc(out_read, 1)


def swiglu_run(w_gate_up, w_down, experts, ff):
    gu = ff // 256
    tiles = ff // P
    down = -(-tiles // 4)
    per = gu + down
    g_rows = w_gate_up.rearrange("e (k p) n -> p (e k) n", p=P)
    d_rows = w_down.rearrange("e (f p) n -> p (e f) n", p=P)

    def rows(c):
        return min(4, tiles - (c - gu) * 4)

    def expert_loads(e, c):
        if c < gu:
            return [(lambda slot, h=h: slot.rearrange("p (k h c) -> p k h c", k=DC, h=2)[:, :, h, :],
                     g_rows[:, ds(e * DC, DC), h * ff + c * 256:h * ff + (c + 1) * 256]) for h in range(2)]
        f0, half = (c - gu) * 4, rows(c) // 2
        return [(lambda slot, h=h: slot[:, h * half * D:(h + 1) * half * D].rearrange("p (f c) -> p f c", f=half),
                 d_rows[:, ds(e * tiles + (f0 + h * half), half), :]) for h in range(2)]

    def part_view(slot, j, h):
        c = j % per
        if c < gu:
            return slot.rearrange("p (k h c) -> p k h c", k=DC, h=2)[:, :, h, :]
        return slot[:, 0:rows(c) * D].rearrange("p (f c) -> p f c", f=rows(c))[:, :, h * 512:(h + 1) * 512]

    r = Fields()
    r.kind, r.count, r.per_turn, r.acc, r.parts = "experts", experts * per, per, 1, 2
    r.expert_loads, r.part_view = expert_loads, part_view
    r.part_shape = lambda j: (DC, 256) if j % per < gu else (rows(j % per), 512)
    r.gu, r.tiles, r.experts, r.rows = gu, tiles, experts, rows
    return r


def swiglu(k, name, x, h_in, hidden, gated, raw, weight=None, extra=()):
    nc, stream = k.nc, k.stream
    r = stream.jobs[stream.at][0]
    gu, per = r.gu, r.per_turn
    assert r.experts == 1 or (per % SLOTS == 0 and gu % 2 == 0)

    def over_experts(eng, body):
        body(0)
        if r.experts > 1:
            with eng.Fori(1, r.experts - 1) as e:
                body(e)
            body(r.experts - 1)

    def later(e, c=0):
        return not isinstance(e, int) or e > 0 or c > 0

    def with_next(e, prepare, panel):
        last = isinstance(e, int) and e == r.experts - 1
        for c in range(per):
            if c + 1 < per or not last:
                prepare(stream.place(r, e, c + 1))
            else:
                stream.first_of_next(prepare)
            panel(c)

    with stage(k, name) as st:
        silu_ready, product_ready, hidden_ready = st.sem("silu_ready"), st.sem("product_ready"), st.sem("hidden_ready")
        hidden_high_ready, y_added = st.sem("hidden_high_ready"), st.sem("y_added")
        extra_loaded = st.sem("extra_loaded") if extra else None

        @st.block.sync
        def _(sp):
            for dst, src in extra:
                sp.dma_start(dst, src).then_inc(extra_loaded, 16)
            stream.ahead(sp)
            if extra:
                sp.wait_ge(extra_loaded, 16 * len(extra))

        @st.block.tensor
        def _(pe):
            def expert(e):
                for c in range(per):
                    m = stream.place(r, e, c)
                    for h in range(2):
                        pe.wait_ge(k.lo_ready, m.halves + (h + 1))
                        w_hi, w_lo = stream.part(k.w_hi, h, m), stream.part(k.w_lo, h, m)
                        if c < gu:
                            if h == 0 and later(e, c // 2):
                                pe.wait_ge(product_ready, e * gu + (c - 1))
                            passes = ((w_hi, h_in[0]), (w_hi, h_in[1]), (w_lo, h_in[0]))
                            for f in range(2):
                                for kk in range(DC):
                                    for i, (w, src) in enumerate(passes):
                                        last = nc.tensor.matmul(k.ps[:, 2 * (c % 2) + h, f * S:(f + 1) * S],
                                                                w[:, kk, f * P:(f + 1) * P], src[:, kk, :],
                                                                start=(kk == 0 and i == 0),
                                                                stop=(kk == DC - 1 and i == 2))
                        else:
                            f0, rows = (c - gu) * 4, r.rows(c)
                            if h == 0:
                                if c == gu and later(e):
                                    pe.wait_ge(y_added, e)
                                pe.wait_ge(hidden_ready, e * gu + (f0 + rows) // 2)
                            passes = ((hidden[0], w_hi), (hidden[0], w_lo), (hidden[1], w_hi))
                            for f in range(rows):
                                for t in range(TT):
                                    for i, (src, w) in enumerate(passes):
                                        last = nc.tensor.matmul(k.ps[:, 4 + 2 * t + h, :],
                                                                src[:, f0 + f, t * P:(t + 1) * P], w[:, f, :],
                                                                start=(f0 + f == 0 and i == 0),
                                                                stop=(f0 + f == r.tiles - 1 and i == 2))
                        last.then_inc(k.first_half_used if h == 0 else k.panel_used, 1)
            over_experts(pe, expert)

        @st.block.scalar
        def _(act):
            def expert(e):
                def panel(c):
                    if c < gu:
                        act.wait_ge(k.panel_used, e * per + (r.first + c + 1))
                        if later(e, c // 2):
                            act.wait_ge(product_ready, e * gu + (c - 1))
                        nc.scalar.activation(gated[:, c % 2, :], k.ps[:, 2 * (c % 2), :],
                                             ACT.Silu).then_inc(silu_ready, 1)
                with_next(e, lambda m, halves=(0, 1): stream.round_weights(act, m, halves), panel)
            stream.open_stage(lambda m, halves: stream.round_weights(act, m, halves))
            over_experts(act, expert)

        @st.block.vector
        def _(dve):
            def expert(e):
                def panel(c):
                    if c < gu:
                        tile = lambda t: t[:, 2 * c:2 * c + 2, :].rearrange("p f n -> p (f n)")
                        dve.wait_ge(silu_ready, e * gu + (c + 1))
                        if later(e, c // 2):
                            dve.wait_ge(hidden_ready, e * gu + (c - 1))
                        nc.vector.tensor_tensor(raw[:, c % 2, :], gated[:, c % 2, :], k.ps[:, 2 * (c % 2) + 1, :],
                                                ALU.mult).then_inc(product_ready, 1)
                        dve.wait_ge(product_ready, e * gu + (c + 1))
                        nc.vector.tensor_copy(tile(hidden[0]), raw[:, c % 2, :]).then_inc(hidden_high_ready, 1)
                        dve.wait_ge(hidden_high_ready, e * gu + (c + 1))
                        nc.vector.tensor_tensor(tile(hidden[1]), raw[:, c % 2, :], tile(hidden[0]).bitcast(F32),
                                                ALU.subtract).then_inc(hidden_ready, 1)
                with_next(e, lambda m, halves=(0, 1): stream.rest_of_weights(dve, m, halves), panel)
                dve.wait_ge(k.panel_used, e * per + (r.first + per))
                if later(e):
                    dve.wait_ge(y_added, e)
                for t in range(TT):
                    xt = x[:, t, :].rearrange("p (h n) -> p h n", h=2)
                    y = k.ps[:, 4 + 2 * t:6 + 2 * t, :]
                    if weight is None:
                        last = nc.vector.tensor_tensor(xt, xt, y, ALU.add)
                    else:
                        last = nc.vector.scalar_tensor_tensor(xt, y, weight[:, t, ds(e, 1)], xt, ALU.mult, ALU.add)
                last.then_inc(y_added, 1)
            stream.open_stage(lambda m, halves: stream.rest_of_weights(dve, m, halves))
            over_experts(dve, expert)

    stream.at += 1


def top_two_weights(k, logits, weights):
    nc = k.nc
    with stage(k, "top_two") as st:
        dve_order, exp_ready, exps_done = st.sem("dve_order"), st.sem("exp_ready"), st.sem("exps_done")
        top = k.small[:, 0:16].rearrange("p (t e) -> p t e", t=TT)
        index = k.small_u[:, 0:16].rearrange("p (t e) -> p t e", t=TT)
        index_f = k.small[:, 16:32].rearrange("p (t e) -> p t e", t=TT)
        w = k.small[:, 32:40].rearrange("p (t e) -> p t e", t=TT)
        picked = k.small[:, 48:56]

        @st.block.vector
        def _(dve):
            o = Order(dve, dve_order)
            for t in range(TT):
                o(nc.vector.max(top[:, t, :], logits[:, t, :]))
                o(nc.vector.max_index(index[:, t, :], top[:, t, :], logits[:, t, :]))
            o(nc.vector.tensor_copy(index_f, index))
            o(nc.vector.tensor_tensor(w[:, :, 0], top[:, :, 1], top[:, :, 0], ALU.subtract))
            o(nc.vector.memset(k.small[:, 40:41], 0.0))
            nc.vector.tensor_copy(w[:, :, 3], w[:, :, 0]).then_inc(exp_ready, 1)
            dve.wait_ge(exps_done, 1)
            o(nc.vector.tensor_scalar(w[:, :, 2], w[:, :, 1], 1.0, None, ALU.add))
            o(nc.vector.reciprocal(w[:, :, 0], w[:, :, 2]))
            o(nc.vector.tensor_tensor(w[:, :, 1], w[:, :, 1], w[:, :, 0], ALU.mult))
            for t in range(TT):
                o(nc.vector.tensor_scalar(weights[:, t, :], k.experts, index_f[:, t, 0:1], w[:, t, 0:1],
                                          ALU.is_equal, ALU.mult))
                o(nc.vector.tensor_scalar(picked, k.experts, index_f[:, t, 1:2], w[:, t, 1:2],
                                          ALU.is_equal, ALU.mult))
                o(nc.vector.tensor_tensor(weights[:, t, :], weights[:, t, :], picked, ALU.add))

        @st.block.scalar
        def _(act):
            act.wait_ge(exp_ready, 1)
            nc.scalar.activation(w[:, :, 1], w[:, :, 3], ACT.Exp).then_inc(exps_done, 1)


def load(k, name, pairs):
    with stage(k, name) as st:
        loaded = st.sem("loaded")

        @st.block.sync
        def _(sp):
            for dst, src in pairs:
                sp.dma_start(dst, src).then_inc(loaded, 16)
            sp.wait_ge(loaded, 16 * len(pairs))


def final_norm(k, x, gain_row, out):
    nc = k.nc
    with stage(k, "final_norm") as st:
        squares_summed, mean_ready = st.sem("squares_summed"), st.sem("mean_ready")
        root_ready, dve_order = st.sem("root_ready"), st.sem("dve_order")

        @st.block.scalar
        def _(act):
            for t in range(TT):
                squares = k.ps[:, 2 * t:2 * t + 2, :].rearrange("p b n -> p (b n)")
                last = nc.scalar.activation(squares, x[:, t, :], ACT.Square, accum_out=k.stat[:, t:t + 1])
            last.then_inc(squares_summed, 1)
            act.wait_ge(mean_ready, 1)
            nc.scalar.activation(k.stat[:, 4:6], k.stat[:, 2:4], ACT.Sqrt).then_inc(root_ready, 1)

        @st.block.vector
        def _(dve):
            o = Order(dve, dve_order)
            dve.wait_ge(squares_summed, 1)
            nc.vector.tensor_scalar(k.stat[:, 2:4], k.stat[:, 0:2], 1.0 / D, 1e-6, ALU.mult,
                                    ALU.add).then_inc(mean_ready, 1)
            dve.wait_ge(root_ready, 1)
            o(nc.vector.reciprocal(k.stat[:, 6:8], k.stat[:, 4:6]))
            for t in range(TT):
                nc.vector.scalar_tensor_tensor(out[:, t, :], x[:, t, :], k.stat[:, 6 + t:7 + t], gain_row,
                                               ALU.mult, ALU.mult)


LAM_INIT = 0.8 - 0.6 * float(np.exp(-0.3 * 0))
HEADS1 = 6
MEM_HEADS = 4


def plan_block1(k, w):
    a = k.area
    v = Fields()
    v.km, v.vm, v.cat = [a(0, 2), a(1024, 2)], [a(512, 2), a(1536, 2)], a(2048, 8)
    v.mem_tok = a(6144, 2, 1024)
    v.qk, v.v_tok, v.qm = a(4096, 12), a(7168, 2, 768), a(8704, 2)
    v.alibi, v.work, v.tmp, v.rows = a(9216, 6, S + P), a(12288, 6), a(13312, 6), a(14848, 5, P)
    v.dense_hidden = (k.pair_part("dense_hidden_hi", 4096, 22), k.pair_part("dense_hidden_lo", 9728, 22))
    v.dense_gated, v.dense_raw = a(15360, 2, 512), a(16384, 2, 512)
    v.q, v.fz, v.i_tok, v.g = a(4096, 6), a(5632, 2, 768), a(7168, 2, 768), a(8704, 6)
    v.log_f, v.kT, v.qm_b = v.fz, a(10240, 6), a(11776, 2)
    v.levels, v.level_masks, v.decays = a(12288, 9, P), a(13440, 8, P), a(14464, 16, P)
    v.qe, v.ke, v.attn, v.cross = a(16512, 14, P), a(18304, 14, P), a(20096, 6, P), a(0, 4, P)
    v.k_tok, v.tmp_b, v.work_b = a(14464, 2, 768), a(16000, 6), a(17536, 6)
    v.hidden = (k.pair_part("hidden_hi", 0, 28), k.pair_part("hidden_lo", 7168, 28))
    v.gated, v.raw = a(14336, 2, 512), a(15360, 2, 512)

    v.mem_pair = (k.pair_part("mem_hi", 4096, 8), k.pair_part("mem_lo", 12288, 8))
    v.cat_parts = (v.cat, k.pair_part("cat_hi", 4096, 8), k.pair_part("cat_lo", 2048, 8))

    s = k.stream
    for i, m in enumerate("ab"):
        kv = w[f"{m}_w_mem_kv"]
        s.add([run("F", kv, 0, v.mem_pair, to_features(v.km[i], chunks=2), width=256),
               run("T", kv, 256, v.mem_pair, to_tokens(v.vm[i], width=256), width=256)])
    s.add([run("F", w["a_w_in"], 0, k.h, to_features(v.qk, scale=0.125)),
           run("F", w["a_w_in"], 512, k.h, to_features(v.qk, 4, chunks=2, scale=0.125), width=256),
           run("F", w["a_w_in"], 768, k.h, to_features(v.qk, 6, chunks=2), width=256),
           run("F", w["a_w_in"], 1024, k.h, to_features(v.qk, 8)),
           run("T", w["a_w_in"], 1536, k.h, to_tokens(v.v_tok)),
           run("T", w["a_w_in"], 2048, k.h, to_tokens(v.v_tok, 512, 256), width=256),
           run("F", w["a_w_in"], 2304, k.h, to_features(v.qm, chunks=2, scale=0.125), width=256)])
    s.add([run("T", w["a_w_out"], 0, v.cat_parts[1:], add_to_residual(k.x), on="dve", count=2, pieces=lambda p: 0)])
    s.add([swiglu_run(w["dense_w_gate_up"], w["dense_w_down"], 1, 2816)])
    wb = w["b_w_in"]
    s.add([run("F", wb, 0, k.h, to_features(v.q)),
           run("F", wb, 512, k.h, to_features(v.q, 4, chunks=2), width=256),
           run("T", wb, 768, k.h, to_tokens(v.fz)), run("T", wb, 1280, k.h, to_tokens(v.fz, 512, 256), width=256),
           run("T", wb, 1536, k.h, to_tokens(v.i_tok)),
           run("T", wb, 2048, k.h, to_tokens(v.i_tok, 512, 256), width=256),
           run("F", wb, 2304, k.h, to_features(v.g, func=ACT.Silu)),
           run("F", wb, 2816, k.h, to_features(v.g, 4, ACT.Silu, chunks=2), width=256),
           run("F", wb, 3072, k.h, to_features(v.qm_b, chunks=2, scale=0.125), width=256)])
    s.add([run("T", w["b_w_out"], 0, v.cat_parts[1:], add_to_residual(k.x), on="dve", count=2, pieces=lambda p: 0)])
    s.add([run("T", w["moe_router"], 0, k.h, to_tokens(k.logits, width=8), width=8)])
    s.add([swiglu_run(w["moe_w_gate_up"], w["moe_w_down"], 8, 3584)])
    return v


def setup(k, w, c, v):
    nc = k.nc
    small = [(k.ident, "ident"), (k.ones, "ones"), (k.upper, "upper"), (k.causal, "causal"),
             (k.pair_rot, "pair_rot"), (k.half_rot, "half_rot"), (k.freq, "freq"), (k.cmp_mask, "cmp_mask"),
             (k.experts, "experts")]
    pieces, r = [], 0
    for name, offset, n in COLUMN_ROWS:
        done = 0
        while done < n:
            m = min(n - done, P - r % P)
            src = w[name].flatten()[offset + done * P:offset + (done + m) * P].rearrange("(n d) -> n d", d=P)
            pieces.append((v.rows[r % P:r % P + m, r // P, :], src))
            r += m
            done += m
    last_rows = N_COLS % P
    lam = k.lam_in
    with stage(k, "setup") as st:
        loaded, rows_loaded, lam_loaded = st.sem("loaded"), st.sem("rows_loaded"), st.sem("lam_loaded")
        zeroed, transposed, order = st.sem("zeroed"), st.sem("transposed"), st.sem("order")
        lam_sums, lam_exps = st.sem("lam_sums"), st.sem("lam_exps")

        @st.block.sync
        def _(sp):
            sp.dma_start(k.x[:, :, :], w["x"].rearrange("(t p) d -> p t d", p=P)).then_inc(loaded, 16)
            sp.dma_start(v.mem_tok, w["mem"].rearrange("(t p) d -> p t d", p=P)).then_inc(loaded, 16)
            for dst, name in small:
                sp.dma_start(dst[:, :], c[name]).then_inc(loaded, 16)
            k.stream.load_range(sp, 0, SLOTS)
            sp.wait_ge(loaded, 16 * (2 + len(small)))

        @st.block.scalar
        def _(act):
            act.wait_ge(zeroed, 1)
            for dst, src in pieces:
                act.dma_start(dst, src).then_inc(rows_loaded, 16)
            for i, name in enumerate(("a_lam_q1", "a_lam_k1", "a_lam_q2", "a_lam_k2")):
                act.dma_start(lam[:, i, :], w[name].flatten().partition_broadcast(P)).then_inc(lam_loaded, 16)
            act.wait_ge(lam_sums, 1)
            nc.scalar.activation(k.small[:, 2:4], k.small[:, 0:2], ACT.Exp).then_inc(lam_exps, 1)

        @st.block.tensor
        def _(pe):
            pe.wait_ge(rows_loaded, 16 * len(pieces))
            pe.wait_ge(loaded, 16 * (2 + len(small)))
            for i in range(5):
                last = nc.tensor.transpose(k.ps[:, i // 4, (i % 4) * P:(i % 4 + 1) * P], v.rows[:, i, :], k.ident[:, :])
            last.then_inc(transposed, 1)

        @st.block.vector
        def _(dve):
            o = Order(dve, order)
            nc.vector.memset(v.rows[:, 4, :], 0.0).then_inc(zeroed, 1)
            o(nc.vector.memset(k.eps_cols[:, 0:1], 1e-6))
            o(nc.vector.memset(k.eps_cols[:, 1:2], 1e-5))
            o(nc.vector.memset(k.ones_row[:, :], 1.0))
            o(nc.vector.memset(k.small[:, :], 0.0))
            dve.wait_ge(lam_loaded, 64)
            for i in range(2):
                o(nc.vector.tensor_tensor(lam[:, 2 * i, :], lam[:, 2 * i, :], lam[:, 2 * i + 1, :], ALU.mult))
                o(nc.vector.tensor_reduce(k.small[:, i:i + 1], lam[:, 2 * i, :], AX_X, ALU.add))
            nc.vector.memset(k.small[:, 4:5], 0.0).then_inc(lam_sums, 1)
            dve.wait_ge(lam_exps, 1)
            o(nc.vector.tensor_tensor(k.neg_lam[:, 0:1], k.small[:, 3:4], k.small[:, 2:3], ALU.subtract))
            o(nc.vector.tensor_scalar(k.neg_lam[:, 0:1], k.neg_lam[:, 0:1], LAM_INIT, None, ALU.subtract))
            o(nc.vector.tensor_copy(k.neg_lam[:, 1:2], k.neg_lam[:, 0:1]))
            dve.wait_ge(transposed, 1)
            o(nc.vector.tensor_copy(k.cols[:, 0:512], k.ps[:, 0, :]))
            o(nc.vector.tensor_copy(k.cols[:, 512:640], k.ps[:, 1, 0:P]))
            at = COL["a_subln"]
            o(nc.vector.tensor_scalar(k.cols[:, at:at + 1], k.cols[:, at:at + 1], 1.0 - LAM_INIT, None, ALU.mult))


def memory_groups(k, qm, km, vm, cat):
    groups = []
    for h in range(MEM_HEADS):
        r = 64 * (h % 2)
        u = unit([(qm[r:r + 64, h // 2, :], km[r:r + 64, h // 2, :])],
                 lambda b, h=h: vm[:, b, h * 64:(h + 1) * 64])
        groups.append(([u], r, 64, cat[r:r + 64, 6 + h // 2, :], None))
    return groups


def hgrn_gates(k, v):
    nc = k.nc
    with stage(k, "hgrn_gates") as st:
        act_order, log_ready, keys_ready = st.sem("act_order"), st.sem("log_ready"), st.sem("keys_ready")
        transposed, dve_order = st.sem("transposed"), st.sem("dve_order")
        t1 = v.tmp_b.rearrange("p c n -> p (c n)")
        fz = v.fz.rearrange("p t n -> p (t n)")

        @st.block.scalar
        def _(act):
            o = Order(act, act_order)
            nc.scalar.activation(v.k_tok.rearrange("p t n -> p (t n)"), fz, ACT.Sigmoid,
                                 scale=-1.0).then_inc(keys_ready, 1)
            o(nc.scalar.activation(t1, fz, ACT.Abs))
            o(nc.scalar.activation(t1, t1, ACT.Exp, scale=-1.0))
            nc.scalar.activation(t1, t1, ACT.Ln, bias=1.0).then_inc(log_ready, 1)

        @st.block.tensor
        def _(pe):
            pe.wait_ge(keys_ready, 1)
            for h in range(HEADS1):
                for t in range(TT):
                    last = nc.tensor.transpose(k.ps[:, h // 2, (h % 2) * S + t * P:(h % 2) * S + (t + 1) * P],
                                               v.k_tok[:, t, h * P:(h + 1) * P], k.ident[:, :])
            last.then_inc(transposed, 1)

        @st.block.vector
        def _(dve):
            dve.wait_ge(transposed, 1)
            nc.vector.tensor_copy(v.kT.rearrange("p c n -> p (c n)"),
                                  k.ps[:, 0:3, :].rearrange("p b n -> p (b n)"))
            dve.wait_ge(log_ready, 1)
            nc.vector.scalar_tensor_tensor(v.log_f.rearrange("p t n -> p (t n)"), fz, 0.0, t1, ALU.min,
                                           ALU.subtract)


def hgrn_attention(k, v):
    nc = k.nc
    n = HEADS1 * TT
    with stage(k, "hgrn_attention") as st:
        sums_ready, exp_done, decayed = st.sem("sums_ready"), st.sem("exp_done"), st.sem("decayed")
        scores_done, attn_ready = st.sem("scores_done"), st.sem("attn_ready")
        out_ready, out_read, dve_order = st.sem("out_ready"), st.sem("out_read"), st.sem("dve_order")
        levels = v.levels.rearrange("p l t -> p (l t)")

        def halves(m, x):
            return x[:, (m % 2) * 7:(m % 2) * 7 + 7, :]

        @st.block.tensor
        def _(pe):
            def exponents(m):
                h, t = divmod(m, TT)
                if m >= 2:
                    pe.wait_ge(exp_done, m - 1)
                for b in range(2):
                    last = nc.tensor.matmul(k.ps[:, 2 * (m % 2) + b, :], v.log_f[:, t, h * P:(h + 1) * P],
                                            levels[:, t * P + b * 512:t * P + (b + 1) * 512], start=True, stop=True)
                last.then_inc(sums_ready, 1)

            def outputs(h):
                pe.wait_ge(attn_ready, TT * (h + 1))
                if h >= 1:
                    pe.wait_ge(out_read, h)
                at = (h % 2) * S
                vals = [v.i_tok[:, t, h * P:(h + 1) * P] for t in range(TT)]
                a = v.attn[:, (h % 2) * 3:(h % 2) * 3 + 3, :]
                nc.tensor.matmul(k.ps[:, 7, at:at + P], vals[0], a[:, 0, :], start=True, stop=True)
                nc.tensor.matmul(k.ps[:, 7, at + P:at + S], vals[0], a[:, 2, :], start=True, stop=False)
                nc.tensor.matmul(k.ps[:, 7, at + P:at + S], vals[1], a[:, 1, :], start=False,
                                 stop=True).then_inc(out_ready, 1)

            exponents(0)
            for m in range(n):
                h, t = divmod(m, TT)
                if m + 1 < n:
                    exponents(m + 1)
                pe.wait_ge(decayed, m + 1)
                if m >= 1:
                    pe.wait_ge(attn_ready, m)
                for lv in range(7):
                    nc.tensor.matmul(k.ps[:, 4 + lv // 4, (lv % 4) * P:(lv % 4 + 1) * P], halves(m, v.ke)[:, lv, :],
                                     halves(m, v.qe)[:, lv, :], start=True, stop=True)
                last = nc.tensor.matmul(k.ps[:, 5, 3 * P:4 * P], v.kT[:, h, t * P:(t + 1) * P],
                                        v.q[:, h, t * P:(t + 1) * P], start=True, stop=True)
                if t:
                    cross = v.cross[:, (h % 2) * 2:(h % 2) * 2 + 2, :]
                    last = nc.tensor.matmul(k.ps[:, 6, 0:P], cross[:, 0, :], cross[:, 1, :], start=True, stop=True)
                last.then_inc(scores_done, 1)
                if t == 0 and h:
                    outputs(h - 1)
            outputs(HEADS1 - 1)

        @st.block.scalar
        def _(act):
            def copy_out(h):
                act.wait_ge(out_ready, h + 1)
                nc.scalar.activation(v.cat[:, h, :], k.ps[:, 7, (h % 2) * S:(h % 2 + 1) * S], ACT.Copy).then_inc(out_read, 1)

            for m in range(n):
                act.wait_ge(sums_ready, m + 1)
                if m >= 2:
                    act.wait_ge(decayed, m - 1)
                nc.scalar.activation(v.decays[:, (m % 2) * 8:(m % 2) * 8 + 8, :].rearrange("p l t -> p (l t)"),
                                     k.ps[:, 2 * (m % 2):2 * (m % 2) + 2, :].rearrange("p b n -> p (b n)"),
                                     ACT.Exp).then_inc(exp_done, 1)
                if m % 2 and m > 2:
                    copy_out((m - 3) // 2)
            copy_out(HEADS1 - 1)

        @st.block.vector
        def _(dve):
            o = Order(dve, dve_order)

            def decay(m):
                h, t = divmod(m, TT)
                dve.wait_ge(exp_done, m + 1)
                if m >= 2:
                    dve.wait_ge(scores_done, m - 1)
                e = v.decays[:, (m % 2) * 8:(m % 2) * 8 + 8, :]
                lv = e[:, 1 - t:8 - t, :]
                q1, k1 = (x[:, h:h + 1, t * P:(t + 1) * P] for x in (v.q, v.kT))
                nc.vector.tensor_tensor(halves(m, v.qe), lv, q1.broadcast_to([P, 7, P]), ALU.mult)
                nc.vector.tensor_tensor(halves(m, v.ke), lv, k1.broadcast_to([P, 7, P]), ALU.mult)
                cross = v.cross[:, (h % 2) * 2:(h % 2) * 2 + 2, :]
                if t == 0:
                    nc.vector.tensor_tensor(cross[:, 0:1, :], e[:, 0:1, :], k1, ALU.mult).then_inc(decayed, 1)
                else:
                    nc.vector.tensor_tensor(cross[:, 1:2, :], e[:, 7:8, :], q1, ALU.mult).then_inc(decayed, 1)

            def mask(m):
                h, t = divmod(m, TT)
                dve.wait_ge(scores_done, m + 1)
                if h >= 2 and t == 0:
                    dve.wait_ge(out_ready, h - 1)
                scores = k.ps[:, 4:6, :].rearrange("p b n -> p (b n)")
                o(nc.vector.tensor_tensor(scores, scores, v.level_masks.rearrange("p l t -> p (l t)"), ALU.mult))
                a = v.attn[:, (h % 2) * 3:(h % 2) * 3 + 3, :]
                if t:
                    o(nc.vector.tensor_copy(a[:, 2, :], k.ps[:, 6, 0:P]))
                nc.vector.tensor_reduce(a[:, t, :], scores.rearrange("p (l t) -> p t l", l=8), AX_X,
                                        ALU.add).then_inc(attn_ready, 1)

            decay(0)
            for m in range(n):
                if m + 1 < n:
                    decay(m + 1)
                mask(m)


def block1(k, w, c, v):
    nc, s = k.nc, k.stream
    normed_features(k, "mem_norm_a", v.mem_tok, v.mem_pair, lambda i: column(k, "a_mem_norm", i))
    s.stage("mem_kv_a", extra=[(v.alibi.rearrange("p c n -> p (c n)"), c["alibi"])])
    normed_features(k, "mem_norm_b", v.mem_tok, v.mem_pair, lambda i: column(k, "b_mem_norm", i))
    s.stage("mem_kv_b")
    normed_features(k, "norm_mix_a", k.x, k.h, lambda i: column(k, "a_norm_mix", i))
    s.stage("in_a")
    groups = []
    for h in range(HEADS1):
        us = []
        for m in range(2):
            r = 64 * m
            us.append(unit([(v.qk[r:r + 64, h, :], v.qk[r:r + 64, 6 + h, :])],
                           lambda b, h=h: v.v_tok[:, b, h * P:(h + 1) * P],
                           mask=v.alibi[:, h, :], causal=True, factor=k.neg_lam[:, :] if m else None))
        groups.append((us, 0, P, v.cat[:, h, :], None))
    attention(k, "diff_attention", groups + memory_groups(k, v.qm, v.km[0], v.vm[0], v.cat), v.work)
    head_pairs = [((h, h + 2), WHOLE) for h in range(0, HEADS1, 2)]
    feature_norm(k, "subln", v.cat[:, 0:6, :], 6, 1, v.cat[:, 0:6, :], v.tmp, 1e-6, head_pairs,
                 one_gain=column(k, "a_subln"))
    s.stage("out_a", source=[v.cat_parts])
    normed_features(k, "dense_norm", k.x, k.h, lambda i: column(k, "dense_norm", i))
    swiglu(k, "dense", k.x, k.h, v.dense_hidden, v.dense_gated, v.dense_raw)
    normed_features(k, "norm_mix_b", k.x, k.h, lambda i: column(k, "b_norm_mix", i))
    s.stage("in_b", extra=[(v.levels.rearrange("p c n -> p (c n)"), c["levels"]),
                           (v.level_masks.rearrange("p c n -> p (c n)"), c["level_masks"])])
    hgrn_gates(k, v)
    hgrn_attention(k, v)
    attention(k, "memory_attention_b", memory_groups(k, v.qm_b, v.km[1], v.vm[1], v.cat), v.work_b)
    feature_norm(k, "out_norm_b", v.cat[:, 0:6, :], 6, 1, v.cat[:, 0:6, :], v.tmp_b, 1e-6, head_pairs,
                 one_gain=column(k, "b_out_norm"), gate=v.g)
    s.stage("out_b", source=[v.cat_parts])
    normed_features(k, "moe_norm", k.x, k.h, lambda i: column(k, "moe_norm", i))
    s.stage("router")
    top_two_weights(k, k.logits, k.expert_weights)
    swiglu(k, "experts", k.x, k.h, v.hidden, v.gated, v.raw, weight=k.expert_weights,
           extra=[(k.rows[:, 0, :], w["final_norm"].flatten().partition_broadcast(P))])
    final_norm(k, k.x, k.rows[:, 0, :], k.x)


RET_HEADS, RET_DV = 4, 512
MLA_HEADS, MLA_NOPE, MLA_ROPE, MLA_V = 8, 128, 64, 128
MOBA_HEADS, MOBA_DH = 16, 64
DN_ALPHA = 4.0 ** 0.25


def rows_of_eight(w, width=512):
    def loads(p):
        c0, k0 = (p // 3) * width, (p % 3) * 8
        return [(lambda slot, h=h: slot[:, h * 4 * width:(h + 1) * 4 * width].rearrange("p (k c) -> p k c", k=4),
                 w[(k0 + 4 * h) * P:(k0 + 4 * h + 4) * P, c0:c0 + width].rearrange("(k p) c -> p k c", p=P))
                for h in range(2)]
    return loads


def plan_block2(k, w):
    a = k.area
    v = Fields()
    v.rq, v.rk, v.rv, v.rg = a(0, 8), a(2048, 8), a(4096, 2, 2048), a(8192, 16)
    v.squares, v.cat, v.decay = a(0, 16), a(12288, 24), a(16384, 8)
    v.angle, v.turned, v.cos, v.sin = a(12288, 3), k.xn.rearrange("p t (c n) -> p (t c) n", n=S)[:, 0:4, :], a(18432, 3), a(19200, 3)
    v.mq, v.mkv, v.kpe = a(19968, 2), a(20480, 2), a(20992, 1)
    v.mq_mkv = a(19968, 4)
    v.weights = k.xn[:, 0, :].rearrange("p (c n) -> p c n", c=4)
    v.qn, v.kn, v.qpe, v.vm, v.mg = a(0, 8), a(2048, 8), a(4096, 4), a(5120, 2, 1024), a(7168, 8)
    v.work, v.turned_pe, v.qm_squares = a(9216, 6), a(10240, 8), a(10240, 4)
    v.q2, v.k2, v.v2, v.g2, v.cat2 = a(0, 8), a(2048, 8), a(4096, 2, 1024), a(6144, 8), a(8192, 8)
    v.work2 = a(10240, 6)
    s = k.stream
    wi = w["w_in_even_2"]

    def twice(p):
        src = wi[:, 6656:6720].rearrange("(k p) c -> p k c", p=P)
        return [(lambda slot, h=h: slot[:, 0:DC * P].rearrange("p (k c) -> p k c", k=DC)[:, :, h * 64:(h + 1) * 64],
                 src) for h in range(2)]

    s.add([run("F", wi, 0, k.h, to_features(v.rq), count=2), run("F", wi, 1024, k.h, to_features(v.rk), count=2),
           run("T", wi, 2048, k.h, to_tokens(v.rv), count=4),
           run("F", wi, 4096, k.h, to_features(v.rg, func=ACT.Silu), count=4),
           run("F", wi, 6144, k.h, to_features(v.mq, chunks=2), width=256),
           run("F", wi, 6400, k.h, to_features(v.mkv, chunks=2), width=256),
           run("F", wi, 6656, k.h, to_features(v.kpe, chunks=1), width=P, loads=twice)])

    def split(w_, head, lo, hi, heads):
        return grouped_loads(w_, 2, heads, hi - lo, lambda rows, p: rows.rearrange("p (h c) -> p h c", c=head)[
            :, heads * p:heads * (p + 1), lo:hi])

    scale = (MLA_NOPE + MLA_ROPE) ** -0.5
    uq, ukv = w["w_uq_even_2"], w["w_ukv_even_2"]
    s.add([run("F", wi, 6720, k.h, to_features(v.mg, func=ACT.Silu), count=2),
           run("F", uq, 0, v.mq, to_features(v.qn, scale=scale), count=2, nk=2, loads=split(uq, 192, 0, 128, 4)),
           run("F", uq, 0, v.mq, to_features(v.qpe, scale=scale), nk=2, loads=split(uq, 192, 128, 192, 8)),
           run("F", ukv, 0, v.mkv, to_features(v.kn), count=2, nk=2, loads=split(ukv, 256, 0, 128, 4)),
           run("T", ukv, 0, v.mkv, to_tokens(v.vm), count=2, nk=2, loads=split(ukv, 256, 128, 256, 4))])
    hi, lo = k.pair_part("cat_even_hi", 0, 24), k.pair_part("cat_even_lo", 12288, 24)
    eight = lambda x, q: x[:, 8 * q:8 * q + 8, :]
    v.cat_parts = [(eight(v.cat, q), eight(hi, q), eight(lo, q)) for q in range(3)]
    s.add([run("T", None, 0, v.cat_parts[0][1:], add_to_residual(k.x, DN_ALPHA), on="dve", count=6, acc=3,
               loads=rows_of_eight(w["w_out_even_2"]), source=lambda p: v.cat_parts[p % 3][1:],
               pieces=lambda p: p % 3)])
    wo = w["w_in_odd_2"]
    s.add([run("F", wo, 0, k.h, to_features(v.q2, scale=MOBA_DH ** -0.5), count=2), run("F", wo, 1024, k.h, to_features(v.k2), count=2),
           run("T", wo, 2048, k.h, to_tokens(v.v2), count=2),
           run("F", wo, 3072, k.h, to_features(v.g2, func=ACT.Silu), count=2)])
    v.cat2_parts = (v.cat2, k.pair_part("cat_odd_hi", 0, 8), k.pair_part("cat_odd_lo", 8192, 8))
    s.add([run("T", w["w_out_odd_2"], 0, v.cat2_parts[1:], add_to_residual(k.x, DN_ALPHA), on="dve", count=2,
               pieces=lambda p: 0)])
    return v


def rotation_tables(k, st, w, v):
    nc = k.nc
    two_pi = 2.0 * np.pi
    c1 = 6.28125
    c2 = float(np.float32(two_pi - c1))
    c2 = float(np.float32(np.round(c2 * 2 ** 20) / 2 ** 20))
    c3 = float(np.float32(two_pi - c1 - c2))
    magic = 1.5 * 2.0 ** 23
    limit = 3.1415925
    positions_loaded, tables_order = st.sem("positions_loaded"), st.sem("tables_order")
    reduced, tables_ready = st.sem("reduced"), st.sem("tables_ready")
    flat = lambda x: x.rearrange("p c n -> p (c n)")
    angle, cos, sin = flat(v.angle), flat(v.cos), flat(v.sin)

    def request():
        nc.scalar.dma_start(k.pos[:, :], w["positions_2"].flatten().partition_broadcast(P)).then_inc(positions_loaded, 16)

    def angles():
        o = Order(nc.vector, tables_order)
        nc.vector.wait_ge(positions_loaded, 16)
        o(nc.vector.tensor_copy(v.cos[:, 0, :], k.pos[:, :]))
        for j in range(3):
            o(nc.vector.tensor_scalar(v.angle[:, j, :], v.cos[:, 0, :], k.freq[:, j:j + 1], None, ALU.mult))
        o(nc.vector.tensor_scalar(cos, angle, 1.0 / two_pi, None, ALU.mult))
        o(nc.vector.tensor_scalar(cos, cos, magic, None, ALU.add))
        o(nc.vector.tensor_scalar(cos, cos, magic, None, ALU.subtract))
        for part in (c1, c2, c3):
            o(nc.vector.scalar_tensor_tensor(angle, cos, -part, angle, ALU.mult, ALU.add))
        o(nc.vector.tensor_scalar(sin, angle, limit, -limit, ALU.min, ALU.max))
        o(nc.vector.tensor_scalar(cos, angle, np.pi / 2, -two_pi, ALU.is_gt, ALU.mult))
        o(nc.vector.scalar_tensor_tensor(cos, angle, np.pi / 2, cos, ALU.add, ALU.add))
        nc.vector.tensor_scalar(cos, cos, limit, -limit, ALU.min, ALU.max).then_inc(reduced, 1)

    def sines():
        nc.scalar.wait_ge(reduced, 1)
        nc.scalar.activation(sin, sin, ACT.Sin).then_inc(tables_ready, 1)
        nc.scalar.activation(cos, cos, ACT.Sin).then_inc(tables_ready, 1)

    return {"act": {0: [request], 3: [sines]}, "dve": {2: [angles]}}, tables_ready


def rotation(k, st, pieces, partner, cos, sin, turned, first, tables_ready=None):
    nc = k.nc
    j = cos.shape[1]
    runs = k.stream.jobs[k.stream.at]
    flat = [(r, p) for r in runs for p in range(r.count)]
    turned_ready, turned_used, rotated = st.sem("turned_ready"), st.sem("turned_used"), st.sem("rotated")

    def turn(i):
        m = k.stream.place(flat[i][0], 0, flat[i][1])
        nc.tensor.wait_ge(k.group_read[m.bank], m.before + 1)
        if i:
            nc.tensor.wait_ge(turned_used, i)
        for c in range(4):
            last = nc.tensor.matmul(k.ps[:, 6 + c // 2, (c % 2) * S:(c % 2 + 1) * S], partner[:, :],
                                    pieces[i][:, c, :], start=True, stop=True)
        last.then_inc(turned_ready, 1)

    def rotate_(i):
        x = pieces[i]

        def tabled(t):
            return t.broadcast_to([P, 4, S]) if j == 1 else t.unsqueeze(1).broadcast_to([P, 4 // j, j, S])

        def grouped(y):
            return y if j == 1 else y.rearrange("p (a j) n -> p a j n", j=j)
        if i == 0 and tables_ready is not None:
            nc.vector.wait_ge(tables_ready, 2)
        nc.vector.wait_ge(turned_ready, i + 1)
        if i:
            nc.vector.wait_ge(rotated, 2 * i)
        banks = k.ps[:, 6:8, :].rearrange("p b (h n) -> p (b h) n", h=2)
        nc.vector.tensor_tensor(grouped(turned), grouped(banks), tabled(sin), ALU.mult).then_inc(turned_used, 1)
        nc.vector.wait_ge(turned_used, i + 1)
        nc.vector.tensor_tensor(grouped(x), grouped(x), tabled(cos), ALU.mult).then_inc(rotated, 1)
        nc.vector.wait_ge(rotated, 2 * i + 1)
        nc.vector.tensor_tensor(x, x, turned, ALU.add).then_inc(rotated, 1)

    return {"pe": {first + i + 2: [lambda i=i: turn(i)] for i in range(len(pieces))},
            "dve": {first + i + 2: [lambda i=i: rotate_(i)] for i in range(len(pieces))}}


def even_steps(k, st, w, v):
    tables, tables_ready = rotation_tables(k, st, w, v)
    pieces = [x[:, 4 * i:4 * i + 4, :] for x in (v.rq, v.rk) for i in range(2)]
    steps = rotation(k, st, pieces, k.pair_rot, v.cos[:, 0:2, :], v.sin[:, 0:2, :], v.turned, 6, tables_ready)
    return {"act": tables["act"], "pe": steps["pe"], "dve": {**tables["dve"], **steps["dve"]}}


def odd_steps(k, st, v):
    pieces = [x[:, 4 * i:4 * i + 4, :] for x in (v.q2, v.k2) for i in range(2)]
    return rotation(k, st, pieces, k.half_rot, v.cos[:, 2:3, :], v.sin[:, 2:3, :], v.turned, 1)


def rotate(k, name, pieces, partner, cos, sin, turned):
    nc = k.nc
    j = cos.shape[1]
    with stage(k, name) as st:
        turned_ready, order, piece_done = st.sem("turned_ready"), st.sem("order"), st.sem("piece_done")

        @st.block.tensor
        def _(pe):
            for i, x in enumerate(pieces):
                if i >= 2:
                    pe.wait_ge(piece_done, i - 1)
                for c in range(x.shape[1]):
                    last = nc.tensor.matmul(k.ps[:, 4 * (i % 2) + c // 2, (c % 2) * S:(c % 2 + 1) * S], partner[:, :],
                                            x[:, c, :], start=True, stop=True)
                last.then_inc(turned_ready, 1)

        @st.block.vector
        def _(dve):
            o = Order(dve, order)
            for i, x in enumerate(pieces):
                n = x.shape[1]
                reps = n // j

                def tabled(t):
                    if j == 1:
                        return t.broadcast_to([P, n, S])
                    return t.unsqueeze(1).broadcast_to([P, reps, j, S])

                def grouped(y):
                    return y if j == 1 else y.rearrange("p (a j) n -> p a j n", j=j)
                banks = k.ps[:, 4 * (i % 2):4 * (i % 2) + 4, :].rearrange("p b (h n) -> p (b h) n", h=2)[:, 0:n, :]
                dve.wait_ge(turned_ready, i + 1)
                nc.vector.tensor_tensor(grouped(turned[:, 0:n, :]), grouped(banks), tabled(sin), ALU.mult)
                o(nc.vector.tensor_tensor(grouped(x), grouped(x), tabled(cos), ALU.mult))
                o(nc.vector.tensor_tensor(x, x, turned[:, 0:n, :], ALU.add))
                nc.vector.memset(k.small[:, 63:64], 0.0).then_inc(piece_done, 1)


def retention(k, v):
    nc = k.nc
    with stage(k, "retention") as st:
        scores_ready, decayed = st.sem("scores_ready"), st.sem("decayed")
        out_ready, out_read = st.sem("out_ready"), st.sem("out_read")

        @st.block.tensor
        def _(pe):
            def scores(h):
                if h >= 2:
                    pe.wait_ge(decayed, h - 1)
                for b in range(TT):
                    for c in range(2):
                        last = nc.tensor.matmul(k.ps[:, h % 2, b * S:(b + 1) * S],
                                                v.rk[:, 2 * h + c, b * P:(b + 1) * P], v.rq[:, 2 * h + c, :],
                                                start=(c == 0), stop=(c == 1))
                last.then_inc(scores_ready, 1)

            scores(0)
            for h in range(RET_HEADS):
                if h + 1 < RET_HEADS:
                    scores(h + 1)
                pe.wait_ge(decayed, h + 1)
                if h >= 2:
                    pe.wait_ge(out_read, h - 1)
                for c in range(RET_DV // P):
                    for b in range(TT):
                        last = nc.tensor.matmul(k.ps[:, 4 + 2 * (h % 2) + c // 2, (c % 2) * S:(c % 2 + 1) * S],
                                                v.rv[:, b, h * RET_DV + c * P:h * RET_DV + (c + 1) * P],
                                                v.weights[:, 2 * (h % 2) + b, :], start=(b == 0), stop=(b == 1))
                last.then_inc(out_ready, 1)

        @st.block.vector
        def _(dve):
            for h in range(RET_HEADS):
                dve.wait_ge(scores_ready, h + 1)
                if h >= 2:
                    dve.wait_ge(out_ready, h - 1)
                nc.vector.tensor_tensor(v.weights[:, 2 * (h % 2):2 * (h % 2) + 2, :],
                                        k.ps[:, h % 2, :].rearrange("p (b n) -> p b n", b=2),
                                        v.decay[:, 2 * h:2 * h + 2, :], ALU.mult).then_inc(decayed, 1)

        @st.block.scalar
        def _(act):
            for h in range(RET_HEADS):
                act.wait_ge(out_ready, h + 1)
                nc.scalar.activation(v.cat[:, 4 * h:4 * h + 4, :].rearrange("p c n -> p (c n)"),
                                     k.ps[:, 4 + 2 * (h % 2):6 + 2 * (h % 2), :].rearrange("p b n -> p (b n)"),
                                     ACT.Copy).then_inc(out_read, 1)


def layer_norm_rows(k, name, w_gain, w_bias, x):
    nc = k.nc
    with stage(k, name) as st:
        loaded, order, mean_ready = st.sem("loaded"), st.sem("order"), st.sem("mean_ready")
        squares_summed, variance_ready, root_ready = (st.sem("squares_summed"), st.sem("variance_ready"),
                                                      st.sem("root_ready"))

        @st.block.scalar
        def _(act):
            act.dma_start(k.rows[:, 0, :], w_gain.partition_broadcast(P)).then_inc(loaded, 16)
            act.dma_start(k.rows[:, 1, :], w_bias.partition_broadcast(P)).then_inc(loaded, 16)
            act.wait_ge(mean_ready, 1)
            for t in range(TT):
                squares = k.ps[:, 4 + 2 * t:6 + 2 * t, :].rearrange("p b n -> p (b n)")
                last = nc.scalar.activation(squares, x[:, t, :], ACT.Square, bias=k.stat[:, 2 + t:3 + t],
                                            accum_out=k.stat[:, 4 + t:5 + t])
            last.then_inc(squares_summed, 1)
            act.wait_ge(variance_ready, 1)
            nc.scalar.activation(k.stat[:, 6:8], k.stat[:, 0:2], ACT.Sqrt).then_inc(root_ready, 1)

        @st.block.vector
        def _(dve):
            o = Order(dve, order)
            o(nc.vector.tensor_reduce(k.stat[:, 0:2], x, AX_X, ALU.add))
            nc.vector.tensor_scalar(k.stat[:, 2:4], k.stat[:, 0:2], -1.0 / D, None, ALU.mult).then_inc(mean_ready, 1)
            dve.wait_ge(mean_ready, 1)
            for t in range(TT):
                o(nc.vector.tensor_scalar(k.ps[:, 2 * t:2 * t + 2, :].rearrange("p b n -> p (b n)"), x[:, t, :],
                                          k.stat[:, 2 + t:3 + t], None, ALU.add))
            dve.wait_ge(squares_summed, 1)
            nc.vector.tensor_scalar(k.stat[:, 0:2], k.stat[:, 4:6], 1.0 / D, 1e-5, ALU.mult,
                                    ALU.add).then_inc(variance_ready, 1)
            dve.wait_ge(root_ready, 1)
            o(nc.vector.reciprocal(k.stat[:, 6:8], k.stat[:, 6:8]))
            dve.wait_ge(loaded, 32)
            for t in range(TT):
                o(nc.vector.scalar_tensor_tensor(x[:, t, :], k.ps[:, 2 * t:2 * t + 2, :].rearrange("p b n -> p (b n)"),
                                                 k.stat[:, 6 + t:7 + t], k.rows[:, 0, :], ALU.mult, ALU.mult))
                o(nc.vector.tensor_tensor(x[:, t, :], x[:, t, :], k.rows[:, 1, :], ALU.add))


def block2(k, w, c, v):
    s = k.stream
    triangle = k.causal[:, 0:P]
    normed_features(k, "features_even", k.x, k.h)
    s.stage("in_even", side=lambda st: even_steps(k, st, w, v), extra=[(v.decay.rearrange("p c n -> p (c n)"), c["decay"])])
    retention(k, v)
    feature_norm(k, "retention_norm", v.cat[:, 0:16, :], RET_HEADS, 4, v.cat[:, 0:16, :], v.squares, 1e-5,
                 [((h, h + 1), WHOLE) for h in range(RET_HEADS)], center=True, gate=v.rg)
    feature_norm(k, "latent_norm", v.mq_mkv, 2, 2, v.mq_mkv, v.qm_squares, 1e-6, [((h, h + 1), WHOLE) for h in range(2)],
                 gain=lambda i: column(k, "q_norm_even_2" if i < 2 else "kv_norm_even_2", i % 2))
    s.stage("mla_up")
    rotate(k, "rotate_mla", [v.qpe, v.kpe], k.half_rot, v.cos[:, 2:3, :], v.sin[:, 2:3, :], v.turned_pe)
    groups = []
    for h in range(MLA_HEADS):
        r = 64 * (h % 2)
        u = unit([(v.qn[:, h, :], v.kn[:, h, :]), (v.qpe[r:r + 64, h // 2, :], v.kpe[r:r + 64, 0, :])],
                 lambda b, h=h: v.vm[:, b, h * P:(h + 1) * P], mask=triangle, causal=True)
        groups.append(([u], 0, P, v.cat[:, 16 + h, :], v.mg[:, h, :]))
    attention(k, "latent_attention", groups, v.work)
    s.stage("out_even", source=v.cat_parts)
    layer_norm_rows(k, "layer_norm_even", w["ln_g_2"][0], w["ln_b_2"][0], k.x)
    normed_features(k, "features_odd", k.x, k.h)
    s.stage("in_odd", side=lambda st: odd_steps(k, st, v))
    groups = []
    for h in range(MOBA_HEADS):
        r = 64 * (h % 2)
        u = unit([(v.q2[r:r + 64, h // 2, :], v.k2[r:r + 64, h // 2, :])],
                 lambda b, h=h: v.v2[:, b, h * MOBA_DH:(h + 1) * MOBA_DH], mask=triangle, causal=True)
        groups.append(([u], r, MOBA_DH, v.cat2[r:r + 64, h // 2, :], v.g2[r:r + 64, h // 2, :]))
    attention(k, "block_attention", groups, v.work2)
    s.stage("out_odd", source=[v.cat2_parts])
    layer_norm_rows(k, "layer_norm_odd", w["ln_g_2"][1], w["ln_b_2"][1], k.x)


LSTM_HEADS, QK_CONV, CONF_K = 4, 4, 31
WIDE_TWICE = [1, 2, 2, 3, 3, 4, 4, 5, 6, 7, 8, 10, 10, 11]
NSA_HEADS, NSA_GROUPS, N_CMP = 8, 2, S // 16 - 1


def plan_block3(k, w):
    a = k.area
    v = Fields()
    v.ya, v.yb, v.yc, v.gate = a(0, 8), a(2048, 8), a(4096, 8), a(6144, 1, 1024)
    v.c, v.c_all, v.ada_rows = k.c_cols[:, 0:8].unsqueeze(2), a(9792, 8, P), a(16000, 1, 2048)
    row = lambda at, n: a(7168 + at, 1, n)[0:1, 0, :]
    v.row_gate, v.row_av, v.row_if = row(0, 1024), row(1024, 1024), row(2048, 8)
    v.row_vs, v.row_vw, v.row_g = row(2056, 256), row(2312, 256), row(2568, 24)
    v.qk_pad, v.qk, v.av = a(9792, 16, S + QK_CONV - 1), a(13936, 16), a(18032, 2, 1024)
    v.ao, v.az, v.i_f = v.yc, v.yb, k.i_f
    v.decays, v.sqk, v.probs_t = a(9792, 8), a(11840, 8), a(13936, 8)
    v.a_all = k.xn[:, 0, :].rearrange("p (c n) -> p c n", n=P)
    v.squares_a = a(9792, 8)
    v.u_pad, v.ba, v.bb = a(16960, 8, S + CONF_K - 1), a(12080, 8), a(14128, 8)
    v.products = a(19300, 2)
    v.u, v.bz, v.squares_b = v.yc, v.yb, a(16960, 8)
    v.cq, v.ckv, v.ks, v.kw = a(9792, 8), a(11840, 4), a(12864, 2), a(13376, 2)
    v.vs, v.vw, v.cz = a(13888, 2), a(14400, 2), a(14912, 8)
    v.work, v.blocks = a(16960, 6), a(17984, 64, 2 * N_CMP)
    v.w2, v.hidden, v.hidden_tok = a(19904, 4, P), a(20416, 4, 2 * N_CMP), k.xn[:, 0:1, 0:512]
    v.kc, v.vc = a(20536, 1, 2 * N_CMP), a(20566, 2, P)
    v.g3 = k.g3
    v.mg, v.merged, v.o_tok = a(9792, 24), a(15936, 8), a(17984, 2, 1024)

    s, wi = k.stream, w["w_in_3"]

    def biased(key):
        return lambda c: k.cols[:, ds(COL[key] + c, 1)]

    def F(c0, dst, key, func=ACT.Identity, count=1, chunks=4, width=512):
        return run("F", wi, c0, k.h, to_features(dst, func=func, chunks=chunks, bias=biased(key)), count=count,
                   width=width)

    def T(c0, dst, row_, count=1, width=512):
        return run("T", wi, c0, k.h, to_tokens(dst, width=width), count=count, width=width,
                   bias=lambda p: row_[:, p * width:(p + 1) * width])

    def gate_out(nc, banks, p):
        return nc.scalar.activation(v.gate[:, :, ds(p * 512, 512)], banks[:, 0:1, :], ACT.Copy)

    def row_out(nc, banks, p):
        return nc.scalar.activation(v.ada_rows[:, :, ds(p * 512, 512)], banks[:, 0:1, :], ACT.Copy)

    s.add([run("T", w["w_ada_3"], 0, v.c_all, row_out, count=4, tiles=1),
           run("T", w["w_ada_3"], 2048, v.c_all, gate_out, count=2, tiles=1,
               bias=lambda p: v.row_gate[:, p * 512:(p + 1) * 512])])
    s.add([F(0, v.qk_pad[:, :, QK_CONV - 1:], "qk", count=4), T(2048, v.av, v.row_av, count=2),
           F(3072, v.ao, "ao", ACT.Sigmoid, 2), F(4096, v.az, "az", ACT.Silu, 2),
           T(5120, v.i_f, v.row_if, width=8)])
    s.add([F(5128, v.ba, "ba", count=2), F(6152, v.bb, "bb", ACT.Sigmoid, 2), F(7176, v.bz, "bz", ACT.Silu, 2)])
    s.add([F(8200, v.cq, "cq", count=2), F(9224, v.ckv, "ckc"), F(9736, v.ks, "cks", chunks=2, width=256),
           T(9992, v.vs, v.row_vs, width=256), F(10248, v.kw, "ckw", chunks=2, width=256),
           T(10504, v.vw, v.row_vw, width=256), T(10760, v.g3, v.row_g, width=24),
           F(10784, v.cz, "cz", ACT.Silu, 2)])

    w1 = w["nsa_cmp_w1_3"].rearrange("j k c -> (j k) c")

    def w1_rows(p):
        return [(lambda slot, h=h: slot[:, h * 8 * 256:(h + 1) * 8 * 256].rearrange("p (k c) -> p k c", k=8),
                 w1[(p * 16 + h * 8) * P:(p * 16 + h * 8 + 8) * P, :].rearrange("(k p) c -> p k c", p=P))
                for h in range(2)]

    def gelu_out(nc, banks, q):
        return nc.scalar.activation(v.hidden_tok[0:2 * N_CMP, :, 256 * q:256 * q + 256],
                                    banks[0:2 * N_CMP, 0:1, 0:256], ACT.Gelu_apprx_tanh)

    s.add([run("T", None, 0, lambda p: v.blocks[:, p * 16:(p + 1) * 16, :], gelu_out, count=4, acc=2, tiles=1,
               rows=2 * N_CMP, width=256, nk=16, loads=w1_rows)])
    s.add([F(11808, v.mg, "mg", ACT.Sigmoid, count=6)])

    def gated(b):
        def evict(nc, banks, p):
            at = v.mg[:, ds(p * 4 + b * 8, 4), :]
            return nc.vector.tensor_tensor(at, at, banks.rearrange("p b (h n) -> p (b h) n", h=2), ALU.mult)
        return evict
    v.branches = [(y, k.pair_part(f"{n}_hi", at, 8), k.pair_part(f"{n}_lo", low_at, 8))
                  for y, n, at, low_at in ((v.ya, "ya", 15936, 0), (v.yb, "yb", 17984, 2048), (v.yc, "yc", 7168, 4096))]
    s.add([run("F", w["w_branch_3"][b], 0, pair[1:], gated(b), on="dve", count=2, pieces=lambda p, b=b: b)
           for b, pair in enumerate(v.branches)])
    v.merged_parts = (v.merged, k.pair_part("merged_hi", 9792, 8), k.pair_part("merged_lo", 15936, 8))
    s.add([run("T", w["w_out_3"], 0, v.merged_parts[1:], to_tokens(v.o_tok), count=2, pieces=lambda p: 0)])
    return v


def load_block3(k, w, v):
    nc = k.nc
    b_in = w["b_in_3"].flatten()
    rows = [(v.row_gate, w["b_ada_3"].flatten()[2048:3072])]
    rows += [(r, b_in[at:at + n]) for r, at, n in ((v.row_av, 2048, 1024), (v.row_if, 5120, 8),
                                                  (v.row_vs, 9992, 256), (v.row_vw, 10504, 256),
                                                  (v.row_g, 10760, 24))]
    with stage(k, "load_block3") as st:
        loaded = st.sem("loaded")

        @st.block.scalar
        def _(act):
            with nc.allow_non_contiguous_dma(reason="1024 values of c, one to a partition and chunk"):
                act.dma_start(k.c_cols[:, 0:8], w["c_3"].flatten().rearrange("(k p) -> p k", p=P)).then_inc(loaded, 16)
            for dst, src in rows:
                act.dma_start(dst, src.unsqueeze(0)).then_inc(loaded, 16)
            act.wait_ge(loaded, 16 * (1 + len(rows)))

        @st.block.vector
        def _(dve):
            dve.wait_ge(loaded, 16 * (1 + len(rows)))
            nc.vector.tensor_copy(v.c_all, v.c.broadcast_to([P, DC, P]))


def modulation(k, v):
    nc = k.nc
    ada = k.c_cols[:, 8:24]
    with stage(k, "modulation") as st:
        order, turned = st.sem("order"), st.sem("turned")

        @st.block.tensor
        def _(pe):
            for i in range(16):
                last = nc.tensor.matmul(k.ps[:, 0, i:i + 1], v.ada_rows[0:1, 0, i * P:(i + 1) * P],
                                        k.ones_row[0:1, 0:1], start=True, stop=True)
            last.then_inc(turned, 1)

        @st.block.vector
        def _(dve):
            o = Order(dve, order)
            dve.wait_ge(turned, 1)
            o(nc.vector.tensor_tensor(ada, k.ps[:, 0, 0:16], k.cols[:, COL["shift"]:COL["shift"] + 16], ALU.add))
            o(nc.vector.scalar_tensor_tensor(ada[:, 8:16], ada[:, 8:16], 1.0,
                                             k.cols[:, COL["norm_pre_3"]:COL["norm_pre_3"] + 8], ALU.add, ALU.mult))
            nc.vector.memset(v.qk_pad[:, :, 0:QK_CONV - 1], 0.0)


def two_step_taps(engine, order, x_pad, out, products, tap_done, multiplied, weight, bias):
    chunks = [c for tap, c in order if tap == 0]

    def product(i):
        tap, c = order[i]
        src, n = x_pad[:, c, tap:tap + S], len(chunks)
        if tap == 0:
            engine.tensor_scalar(out[:, c, :], src, weight(tap, c), bias(c), ALU.mult, ALU.add).then_inc(multiplied, 1)
        else:
            if i > 2 * n:
                engine.wait_ge(tap_done, i - 2 * n)
            engine.tensor_scalar(products[:, i % (n + 1), :], src, weight(tap, c), None,
                                 ALU.mult).then_inc(multiplied, 1)

    def add(i):
        tap, c = order[i]
        if tap > 0:
            engine.wait_ge(multiplied, i + 1)
            if tap > 1:
                engine.wait_ge(tap_done, i + 1 - 2 * len(chunks))
            engine.tensor_tensor(out[:, c, :], out[:, c, :], products[:, i % (len(chunks) + 1), :],
                                 ALU.add).then_inc(tap_done, 1)

    def step(i):
        if i + 1 < len(order):
            product(i + 1)
        add(i)
    return [lambda: product(0)] + [lambda i=i: step(i) for i in range(len(order))]


def causal_conv(k, st, x_pad, out, taps, key, engines, share, bias=None, ready=None, products=None):
    n = out.shape[1]
    steps, sems = {}, {}
    for name, engine, chunks, rounds in engines:
        tap_done = st.sem(f"{name}_tap_done")
        order = [(tap, c) for at in range(0, len(chunks), rounds) for tap in range(taps)
                 for c in chunks[at:at + rounds]]
        position = {tc: i for i, tc in enumerate(order)}
        for c in chunks:
            sems[c] = (tap_done, position[(taps - 1, c)] + 1)

        multiplied = st.sem(f"{name}_multiplied") if name == "pool" else None

        def step(tap, c, engine=engine, tap_done=tap_done, position=position):
            w = column(k, key, tap * n + c)
            src = x_pad[:, c, tap:tap + S]
            if tap == 0:
                if ready:
                    ready(engine, c)
                if bias is None:
                    ins = engine.tensor_scalar(out[:, c, :], src, w, None, ALU.mult)
                else:
                    ins = engine.tensor_scalar(out[:, c, :], src, w, bias(c), ALU.mult, ALU.add)
            else:
                engine.wait_ge(tap_done, position[(tap - 1, c)] + 1)
                ins = engine.scalar_tensor_tensor(out[:, c, :], src, w, out[:, c, :], ALU.mult, ALU.add)
            ins.then_inc(tap_done, 1)

        todo = [lambda tc=tc, step=step: step(*tc) for tc in order]
        if multiplied is not None:
            todo = two_step_taps(engine, order, x_pad, out, products, tap_done, multiplied,
                                 lambda tap, c: column(k, key, tap * n + c), bias)
        panels = share.get(name)
        if panels is None:
            steps[name] = todo
        else:
            per = -(-len(todo) // len(panels))
            steps[name] = {q: [] for q in panels}
            for i, q in enumerate(panels):
                steps[name][q] += todo[i * per:(i + 1) * per]
    return steps, sems


def mlstm(k, v):
    nc = k.nc
    small = k.lstm
    lf, f_sum, a = small[:, 0:8], small[:, 8:16], small[:, 16:24]
    neg_m, neg_stab, den, pos = small[:, 24:32], small[:, 32:40], small[:, 40:48], small[:, 48:56]
    i_gate, f_gate = v.i_f[:, :, 0:4], v.i_f[:, :, 4:8]
    th = lambda x: x.rearrange("p (t h) -> p t h", t=TT)
    with stage(k, "mlstm") as st:
        act_order, dve_order, logs_ready = st.sem("act_order"), st.sem("dve_order"), st.sem("logs_ready")
        lf_ready, sums_ready, a_ready = st.sem("lf_ready"), st.sem("sums_ready"), st.sem("a_ready")
        rows_ready, max_ready, exp_done = st.sem("rows_ready"), st.sem("max_ready"), st.sem("exp_done")
        scores_ready, probs_ready = st.sem("scores_ready"), st.sem("probs_ready")
        transposed, pt_ready, out_ready = st.sem("transposed"), st.sem("pt_ready"), st.sem("out_ready")
        heads = lambda x: x.rearrange("p (h t) n -> p h t n", t=TT)
        banks = lambda b: k.ps[:, b:b + 4, :].rearrange("p b (t n) -> p b t n", t=TT)

        @st.block.scalar
        def _(act):
            o = Order(act, act_order)
            t1 = th(pos)
            o(nc.scalar.activation(t1, f_gate, ACT.Abs))
            o(nc.scalar.activation(t1, t1, ACT.Exp, scale=-1.0))
            nc.scalar.activation(t1, t1, ACT.Ln, bias=1.0).then_inc(logs_ready, 1)
            act.wait_ge(max_ready, 1)
            for i in range(8):
                nc.scalar.activation(v.decays[:, i, :], v.decays[:, i, :], ACT.Exp, bias=neg_m[:, i:i + 1])
            nc.scalar.activation(neg_stab, neg_stab, ACT.Exp).then_inc(exp_done, 1)
            act.wait_ge(transposed, 1)
            nc.scalar.activation(v.probs_t.rearrange("p c n -> p (c n)"),
                                 k.ps[:, 0:4, :].rearrange("p b n -> p (b n)"), ACT.Copy).then_inc(pt_ready, 1)
            act.wait_ge(out_ready, 1)
            nc.scalar.activation(v.ya.rearrange("p c n -> p (c n)"),
                                 k.ps[:, 4:8, :].rearrange("p b n -> p (b n)"), ACT.Copy)

        @st.block.tensor
        def _(pe):
            for h in range(LSTM_HEADS):
                for t in range(TT):
                    for c in range(2):
                        last = nc.tensor.matmul(k.ps[:, 4 + h, t * S:(t + 1) * S],
                                                v.qk[:, 2 * h + c, t * P:(t + 1) * P], v.qk[:, 8 + 2 * h + c, :],
                                                start=(c == 0), stop=(c == 1))
            last.then_inc(scores_ready, 1)
            pe.wait_ge(lf_ready, 1)
            nc.tensor.matmul(k.ps[:, 0, 0:4], k.upper[:, :], lf[:, 0:4], start=True, stop=True)
            nc.tensor.matmul(k.ps[:, 0, 4:8], k.ones[:, :], lf[:, 0:4], start=True, stop=False)
            nc.tensor.matmul(k.ps[:, 0, 4:8], k.upper[:, :], lf[:, 4:8], start=False, stop=True).then_inc(sums_ready, 1)
            pe.wait_ge(a_ready, 1)
            for h in range(LSTM_HEADS):
                for b in range(TT):
                    last = nc.tensor.matmul(k.ps[:, 1 + h // 2, (h % 2) * S + b * P:(h % 2) * S + (b + 1) * P],
                                            v.a_all[:, b * 4 + h, :], k.ident[:, :], start=True, stop=True)
            last.then_inc(rows_ready, 1)
            pe.wait_ge(probs_ready, 1)
            for h in range(LSTM_HEADS):
                for b in range(TT):
                    for t in range(TT):
                        last = nc.tensor.transpose(k.ps[:, h, b * S + t * P:b * S + (t + 1) * P],
                                                   v.sqk[:, 2 * h + t, b * P:(b + 1) * P], k.ident[:, :])
            last.then_inc(transposed, 1)
            pe.wait_ge(pt_ready, 1)
            for h in range(LSTM_HEADS):
                for c in range(2):
                    for b in range(TT):
                        last = nc.tensor.matmul(k.ps[:, 4 + h, c * S:(c + 1) * S],
                                                v.av[:, b, h * 256 + c * P:h * 256 + (c + 1) * P],
                                                v.probs_t[:, 2 * h + b, :], start=(b == 0), stop=(b == 1))
            last.then_inc(out_ready, 1)

        @st.block.vector
        def _(dve):
            o = Order(dve, dve_order)
            o(nc.vector.tensor_tensor(v.ao, v.ao, v.az, ALU.mult))
            dve.wait_ge(logs_ready, 1)
            nc.vector.scalar_tensor_tensor(th(lf), f_gate, 0.0, th(pos), ALU.min, ALU.subtract).then_inc(lf_ready, 1)
            dve.wait_ge(sums_ready, 1)
            o(nc.vector.tensor_copy(f_sum, k.ps[:, 0, 0:8]))
            o(nc.vector.tensor_tensor(th(a), i_gate, th(f_sum), ALU.subtract))
            nc.vector.tensor_copy(v.a_all, a.unsqueeze(2).broadcast_to([P, 8, P])).then_inc(a_ready, 1)
            dve.wait_ge(rows_ready, 1)
            mask = k.causal[:, :].rearrange("p (t n) -> p t n", t=TT)
            for h in range(LSTM_HEADS):
                row = k.ps[:, 1 + h // 2, (h % 2) * S:(h % 2 + 1) * S].unsqueeze(1).broadcast_to([P, TT, S])
                o(nc.vector.tensor_tensor(v.decays[:, 2 * h:2 * h + 2, :], row, mask, ALU.add))
            o(nc.vector.tensor_reduce(neg_m, v.decays, AX_X, ALU.max))
            o(nc.vector.tensor_scalar(neg_m, neg_m, 0.0, -1.0, ALU.max, ALU.mult))
            f_ht = f_sum.rearrange("p (t h) -> p h t", t=TT)
            ht = lambda x: x.rearrange("p (h t) -> p h t", t=TT)
            nc.vector.tensor_tensor(ht(neg_stab), ht(neg_m), f_ht, ALU.subtract).then_inc(max_ready, 1)
            dve.wait_ge(scores_ready, 1)
            dve.wait_ge(exp_done, 1)
            o(nc.vector.scalar_tensor_tensor(v.sqk.rearrange("p c n -> p (c n)"),
                                             k.ps[:, 4:8, :].rearrange("p b n -> p (b n)"), 1.0 / 16,
                                             v.decays.rearrange("p c n -> p (c n)"), ALU.mult, ALU.mult))
            o(nc.vector.tensor_reduce(den, v.sqk, AX_X, ALU.add))
            o(nc.vector.tensor_scalar(pos, den, -1.0, None, ALU.mult))
            o(nc.vector.tensor_tensor(den, den, pos, ALU.max))
            o(nc.vector.tensor_tensor(den, den, neg_stab, ALU.max))
            o(nc.vector.reciprocal(den, den))
            nc.vector.tensor_tensor(v.sqk, v.sqk, den.unsqueeze(2).broadcast_to([P, 8, S]),
                                    ALU.mult).then_inc(probs_ready, 1)


def qk_conv(k, st, v):
    nc, stream = k.nc, k.stream
    run_ = stream.jobs[stream.at][0]

    def ready(engine, c):
        m = stream.place(run_, 0, c // 4)
        engine.wait_ge(k.group_read[m.bank], m.before + 1)

    steps, done = causal_conv(k, st, v.qk_pad, v.qk, QK_CONV, "conv", [("dve", nc.vector, list(range(16)), 4)],
                              {"dve": list(range(6, 12))}, ready=ready)

    def silu(c):
        nc.scalar.wait_ge(*done[c])
        nc.scalar.activation(v.qk[:, c, :], v.qk[:, c, :], ACT.Silu, bias=column(k, "mlstm_conv_b_3", c))

    steps["act"] = {7 + i: [lambda c=c: silu(c) for c in range(2 * i, 2 * i + 2)] for i in range(5)}
    steps["act"][12] = [lambda c=c: silu(c) for c in range(10, 16)]
    return steps


def conformer_conv(k, st, v, vector_chunks, vector_steps, pool_chunks=()):
    nc = k.nc
    engines = [("dve", nc.vector, vector_chunks, len(vector_chunks))]
    if pool_chunks:
        engines.append(("pool", nc.gpsimd, pool_chunks, len(pool_chunks)))
    return causal_conv(k, st, v.u_pad, v.u, CONF_K, "dw", engines, {"dve": vector_steps},
                       bias=lambda i: column(k, "conf_dw_b_3", i), products=v.products)[0]


def glu_input(k, v):
    nc = k.nc
    with stage(k, "glu_input") as st:
        @st.block.vector
        def _(dve):
            nc.vector.memset(v.u_pad[:, :, 0:CONF_K - 1], 0.0)
            nc.vector.tensor_tensor(v.u_pad[:, :, CONF_K - 1:], v.ba, v.bb, ALU.mult)


def compression_blocks(k, w, v):
    nc = k.nc
    with stage(k, "compression_blocks") as st:
        loaded = st.sem("loaded")

        @st.block.vector
        def _(dve):
            for j in range(2):
                for g in range(NSA_GROUPS):
                    t = v.ckv[:, 2 * j + g, :].rearrange("p (n l) -> p l n", l=16)
                    pe_ = k.cols[:, COL["pe"] + 32 * j:COL["pe"] + 32 * j + 32].unsqueeze(2)
                    for half in range(2):
                        nc.vector.tensor_tensor(
                            v.blocks[:, 32 * j + 16 * half:32 * j + 16 * half + 16, g * N_CMP:(g + 1) * N_CMP],
                            t[:, :, half:half + N_CMP],
                            pe_[:, 16 * half:16 * half + 16, :].broadcast_to([P, 16, N_CMP]), ALU.add)

        @st.block.scalar
        def _(act):
            act.dma_start(v.w2, w["nsa_cmp_w2_3"].rearrange("j (k p) c -> p (j k) c", p=P)).then_inc(loaded, 16)
            nc.scalar.activation(v.g3, v.g3, ACT.Sigmoid)
            act.wait_ge(loaded, 16)


def compressed_keys(k, v):
    nc = k.nc
    with stage(k, "compressed_keys") as st:
        ready, turned, hidden_ready = st.sem("ready"), st.sem("turned"), st.sem("hidden_ready")

        @st.block.tensor
        def _(pe):
            n = 2 * N_CMP
            for c in range(4):
                last = nc.tensor.transpose(k.ps[:, 2, c * n:(c + 1) * n], v.hidden_tok[0:n, 0, c * P:(c + 1) * P],
                                           k.ident[0:n, 0:n])
            last.then_inc(turned, 1)
            pe.wait_ge(hidden_ready, 1)
            for c in range(2):
                last = nc.tensor.matmul(k.ps[:, 0, 0:2 * N_CMP], v.w2[:, c, :], v.hidden[:, c, :], start=(c == 0),
                                        stop=(c == 1))
            last.then_inc(ready, 1)
            for g in range(NSA_GROUPS):
                for c in range(2):
                    last = nc.tensor.matmul(k.ps[0:N_CMP, 1, g * P:(g + 1) * P],
                                            v.hidden[:, 2 + c, g * N_CMP:(g + 1) * N_CMP], v.w2[:, 2 + c, :],
                                            start=(c == 0), stop=(c == 1))
            last.then_inc(ready, 1)

        @st.block.vector
        def _(dve):
            dve.wait_ge(turned, 1)
            nc.vector.tensor_copy(v.hidden.rearrange("p c n -> p (c n)"),
                                  k.ps[:, 2, 0:8 * N_CMP]).then_inc(hidden_ready, 1)
            dve.wait_ge(ready, 1)
            nc.vector.tensor_copy(v.kc[:, 0, :], k.ps[:, 0, 0:2 * N_CMP])
            dve.wait_ge(ready, 2)
            nc.vector.tensor_copy(v.vc[0:N_CMP, :, :].rearrange("p g n -> p (g n)"), k.ps[0:N_CMP, 1, 0:2 * P])


def merge(k, v):
    nc = k.nc
    with stage(k, "merge") as st:
        order = st.sem("order")

        @st.block.vector
        def _(dve):
            o = Order(dve, order)
            o(nc.vector.tensor_tensor(v.merged, v.mg[:, 0:8, :], v.mg[:, 8:16, :], ALU.add))
            o(nc.vector.tensor_tensor(v.merged, v.merged, v.mg[:, 16:24, :], ALU.add))


def add_gated(k, v):
    nc = k.nc
    with stage(k, "add_gated") as st:
        order = st.sem("order")

        @st.block.vector
        def _(dve):
            o = Order(dve, order)
            o(nc.vector.tensor_tensor(v.o_tok, v.o_tok, v.gate.broadcast_to([P, TT, D]), ALU.mult))
            o(nc.vector.tensor_tensor(k.x, k.x, v.o_tok, ALU.add))


def block3(k, w, c, v):
    s = k.stream
    load_block3(k, w, v)
    s.stage("ada")
    modulation(k, v)
    normed_features(k, "norm_pre", k.x, k.h, lambda i: k.c_cols[:, 16 + i:17 + i],
                    lambda i: k.c_cols[:, 8 + i:9 + i])
    s.stage("in_lstm", side=lambda st: qk_conv(k, st, v))
    mlstm(k, v)
    feature_norm(k, "mlstm_norm", v.ya, LSTM_HEADS, 2, v.ya, v.squares_a, 1e-5,
                 [((h, h + 1), WHOLE) for h in range(LSTM_HEADS)], center=True,
                 gain=lambda i: column(k, "mlstm_norm_3", i), gate=v.ao)
    s.stage("in_conv")
    glu_input(k, v)
    s.stage("in_sparse", side=lambda st: conformer_conv(k, st, v, [2, 3, 4, 5, 6], WIDE_TWICE, [7]))
    compression_blocks(k, w, v)
    s.stage("compress", side=lambda st: conformer_conv(k, st, v, [0, 1], [0]))
    compressed_keys(k, v)
    feature_norm(k, "conformer_norm", v.u, 1, 8, v.yb, v.squares_b, 1e-5,
                 [((0, 1), (t * P, (t + 1) * P)) for t in range(TT)], center=True,
                 gain=lambda i: column(k, "conf_ln_g_3", i), shift=lambda i: column(k, "conf_ln_b_3", i), gate=v.bz)
    triangle = k.causal[:, 0:P]
    cmp_mask = k.cmp_mask[:, :].rearrange("p (t n) -> p t n", t=TT)
    groups = []
    for h in range(NSA_HEADS):
        g, q = h // (NSA_HEADS // NSA_GROUPS), v.cq[:, h, :]
        us = [unit([(q, v.kc[:, 0, g * N_CMP:(g + 1) * N_CMP])], lambda b, g=g: v.vc[0:N_CMP, g, :], P ** -0.5,
                   mask=cmp_mask, n=N_CMP, factor=v.g3[:, :, 3 * h], floor=True)]
        for i, (keys, vals) in enumerate(((v.ks, v.vs), (v.kw, v.vw))):
            us.append(unit([(q, keys[:, g, :])], lambda b, g=g, vals=vals: vals[:, b, g * P:(g + 1) * P], P ** -0.5,
                           mask=triangle, causal=True, factor=v.g3[:, :, 3 * h + 1 + i]))
        groups.append((us, 0, P, v.yc[:, h, :], v.cz[:, h, :]))
    attention(k, "sparse_attention", groups, v.work)
    s.stage("merge_gates")
    s.stage("branches", source=v.branches)
    merge(k, v)
    s.stage("out_merged", source=[v.merged_parts], extra=[(k.rows[:, 0, :], w["norm_post_3"].flatten().partition_broadcast(P))])
    final_norm(k, v.o_tok, k.rows[:, 0, :], v.o_tok)
    add_gated(k, v)


AREA = 21250


def build(nc, w, c, out, parts=(1, 2, 3)):
    k = Fields()
    k.nc = nc

    def sb(name, shape, dt=F32):
        return nc.alloc_sbuf_tensor(name, shape, dt)

    k.ring = sb("ring", [P, SLOTS, SLOT])
    k.w_hi, k.w_lo = sb("w_hi", [P, 2, SLOT // 2], F32R), sb("w_lo", [P, 2, SLOT // 2], F32R)
    k.x, k.xn = sb("x_tokens", [P, TT, D])[:, :, :], sb("xn", [P, TT, D])[:, :, :]
    k.h = (sb("h_hi", [P, DC, S], F32R)[:, :, :], sb("h_lo", [P, DC, S], F32R)[:, :, :])
    base = nc.sbuf_base
    arena = sb("arena", [P, AREA])

    def pair_part(name, at, chunks):
        return nc.alloc_sbuf_tensor_at(name, [P, chunks, S], F32R, offset=arena_base + at * 4)[:, :, :]
    arena_base = -(-base // 32) * 32
    k.pair_part = pair_part
    k.area = lambda at, chunks, n=S: arena[:, at:at + chunks * n].rearrange("p (c n) -> p c n", c=chunks)
    k.ident, k.ones, k.upper = sb("ident", [P, P]), sb("ones", [P, P]), sb("upper", [P, P])
    k.pair_rot, k.half_rot = sb("pair_rot", [P, P]), sb("half_rot", [P, P])
    k.ones_n, k.causal, k.freq = sb("ones_n", [P, P]), sb("causal", [P, TT * S]), sb("freq", [P, 3])
    k.cmp_mask, k.experts = sb("cmp_mask", [P, TT * 15]), sb("experts", [P, 8])[:, :]
    k.cols, k.rows = sb("cols", [P, 640]), k.xn
    k.norm_row = k.xn.rearrange("p t n -> p (t n)")
    k.stat, k.soft = sb("stat", [P, 8]), sb("soft", [P, 2, 8])[:, :, :]
    k.small, k.small_u = sb("small", [P, 64]), sb("small_u", [P, 16], U32)
    k.eps_cols, k.ones_row, k.neg_lam = sb("eps_cols", [P, 2]), sb("ones_row", [1, P]), sb("neg_lam", [P, TT])
    k.eps = lambda e: k.eps_cols[:, 0:1] if e == 1e-6 else k.eps_cols[:, 1:2]
    k.lam_in = k.xn[:, 0, 0:256].rearrange("p (i n) -> p i n", i=4)
    k.logits, k.expert_weights = sb("logits", [P, TT, 8])[:, :, :], sb("expert_weights", [P, TT, 8])[:, :, :]
    k.pos = sb("positions", [P, S], I32)
    k.c_cols, k.lstm = sb("c_cols", [P, 24]), sb("lstm", [P, 56])
    k.i_f, k.g3 = sb("i_f", [P, TT, 8])[:, :, :], sb("g3", [P, TT, 24])[:, :, :]
    k.ps = nc.alloc_psum_tensor("ps", [P, 8, 512], F32)
    k.panel_used = nc.alloc_semaphore("panel_used")
    k.panel_loaded = [nc.alloc_semaphore(f"panel_loaded{i}") for i in range(SLOTS)]
    k.hi_ready, k.lo_ready = nc.alloc_semaphore("hi_ready"), nc.alloc_semaphore("lo_ready")
    k.first_half_used = nc.alloc_semaphore("first_half_used")
    k.group_read = [nc.alloc_semaphore(f"group_read{i}") for i in range(SLOTS)]
    k.stream = Stream(k)

    v1 = plan_block1(k, w)
    v2 = plan_block2(k, w) if 2 in parts else None
    v3 = plan_block3(k, w) if 3 in parts else None
    if 1 not in parts:
        k.stream = Stream(k)
        v2 = plan_block2(k, w) if 2 in parts else None
        v3 = plan_block3(k, w) if 3 in parts else None
    assert nc.sbuf_base >= arena_base + 4 * AREA
    setup(k, w, c, v1)
    if 1 in parts:
        block1(k, w, c, v1)
    if 2 in parts:
        block2(k, w, c, v2)
    if 3 in parts:
        block3(k, w, c, v3)

    stored = nc.alloc_semaphore("stored")
    with stage(k, "store") as st:
        @st.block.sync
        def _(sp):
            sp.dma_start(out.rearrange("(t p) d -> p t d", p=P), k.x).then_inc(stored, 16)
            sp.wait_ge(stored, 16)


def laid_out(name, a):
    a = np.ascontiguousarray(a)
    if name in ("x", "mem"):
        return a.reshape(S, D)
    if name in ("moe_w_gate_up", "moe_w_down"):
        return a.reshape(a.shape[1:])
    if name.startswith("dense_w"):
        return a
    if a.ndim >= 3:
        return a.reshape(a.shape[1:])
    return a


def kernel(**inputs):
    import concourse.bacc as bacc
    from concourse.bass_utils import run_bass_kernel_spmd

    nc = bacc.Bacc("TRN2", target_bir_lowering=False, num_devices=1)
    arrays, w, c = {}, {}, {}
    for name, a in inputs.items():
        if name == "b_lb_logits":
            continue
        a = laid_out(name, a)
        arrays[f"in_{name}"] = a
        w[name] = nc.dram_tensor(f"in_{name}", a.shape, mybir.dt.from_np(a.dtype), kind="ExternalInput").ap()
    for name, a in constant_arrays().items():
        arrays[f"const_{name}"] = a
        c[name] = nc.dram_tensor(f"const_{name}", a.shape, F32, kind="ExternalInput").ap()
    out = nc.dram_tensor("out", [S, D], F32, kind="ExternalOutput").ap()
    build(nc, w, c, out)
    r = run_bass_kernel_spmd(nc, [arrays], core_ids=[0])
    return r.results[0]["out"].reshape(1, S, D)
```
